# Optimizing a Trainium2 kernel written in Bass

```python
import math
import jax
import jax.numpy as jnp
from jax import lax
import numpy as np

D_MODEL = 1024
BATCH = 1
SEQ = 1024
DEPTH = 2
DEC_BATCH = 8
DEC_SEQ = 1
PAST_LEN = 256
PAGE_SIZE = 128

N_A_LAYERS = DEPTH // 2
N_B_LAYERS = DEPTH - N_A_LAYERS

EXPAND = 2
D_INNER = EXPAND * D_MODEL
HEADDIM_A = 64
N_HEADS_A = D_INNER // HEADDIM_A
D_STATE = 128
N_GROUPS_A = 8
HEADS_PER_GROUP = N_HEADS_A // N_GROUPS_A
CONV_W = 4
CONV_DIM = D_INNER + 2 * N_GROUPS_A * D_STATE
IN_PROJ_A = D_INNER + CONV_DIM + N_HEADS_A
SSD_CHUNK = 128
DT_MIN = 0.001
DT_MAX = 0.1

HEAD_DIM_B = 64
N_HEADS_B = D_MODEL // (2 * HEAD_DIM_B)
QK_WIDTH_B = N_HEADS_B * 2 * HEAD_DIM_B
V_WIDTH_B = N_HEADS_B * 2 * HEAD_DIM_B
Q_BLOCK = 128
ROPE_THETA = 10000.0

D_FF = 4 * D_MODEL
DN_ALPHA = (2 * DEPTH) ** 0.25
DN_BETA = (8 * DEPTH) ** -0.25
LN_EPS = 1e-5
RMS_EPS = 1e-5

kernel_name = 'yoco_mamba2_diffattn_step'

def layer_norm(x, g, b):
    xf = x.astype(jnp.float32)
    mu = jnp.mean(xf, -1, keepdims=True)
    var = jnp.mean(jnp.square(xf - mu), -1, keepdims=True)
    return ((xf - mu) * lax.rsqrt(var + LN_EPS) * g + b).astype(x.dtype)

def rms_norm(x, g):
    xf = x.astype(jnp.float32)
    return (xf * lax.rsqrt(jnp.mean(xf * xf, -1, keepdims=True) + RMS_EPS) * g).astype(x.dtype)

def lambda_init_fn(layer):
    return 0.8 - 0.6 * math.exp(-0.3 * layer)

def rope(x, pos):
    half = HEAD_DIM_B // 2
    inv = ROPE_THETA ** (-jnp.arange(half, dtype=jnp.float32) / half)
    ang = pos.astype(jnp.float32)[:, None] * inv[None, :]
    cos = jnp.cos(ang)[None, :, None, None, :]
    sin = jnp.sin(ang)[None, :, None, None, :]
    xf = x.astype(jnp.float32)
    x1, x2 = xf[..., :half], xf[..., half:]
    return jnp.concatenate([x1 * cos - x2 * sin, x2 * cos + x1 * sin], -1).astype(x.dtype)

def causal_conv(xbc, prefix, w, b):
    xpad = jnp.concatenate([prefix.astype(xbc.dtype), xbc], axis=1)
    y = lax.conv_general_dilated(xpad, w[:, None, :].astype(xbc.dtype), window_strides=(1,),
                                 padding='VALID', dimension_numbers=('NWC', 'WIO', 'NWC'),
                                 feature_group_count=CONV_DIM)
    return y + b, xpad[:, -(CONV_W - 1):]

def ssd_scan(x, dt, a, bmat, cmat, h0):
    f32 = jnp.float32
    bt, l = x.shape[:2]
    q = math.gcd(l, SSD_CHUNK)
    nc = l // q
    G, R, P, N = N_GROUPS_A, HEADS_PER_GROUP, HEADDIM_A, D_STATE
    xs = (x.astype(f32) * dt[..., None]).reshape(bt, nc, q, G, R, P)
    da = jnp.moveaxis((dt * a).reshape(bt, nc, q, G, R), 2, -1)
    cs = jnp.cumsum(da, axis=-1)
    bm = bmat.astype(f32).reshape(bt, nc, q, G, N)
    cm = cmat.astype(f32).reshape(bt, nc, q, G, N)
    idx = jnp.arange(q)
    causal = idx[:, None] >= idx[None, :]
    decay = jnp.exp(jnp.where(causal, cs[..., :, None] - cs[..., None, :], -jnp.inf))
    cb = jnp.einsum('bclgn,bcsgn->bcgls', cm, bm)
    y_diag = jnp.einsum('bcgls,bcgrls,bcsgrp->bclgrp', cb, decay, xs)
    decay_to_end = jnp.exp(cs[..., -1:] - cs)
    chunk_states = jnp.einsum('bcsgn,bcgrs,bcsgrp->bcgrpn', bm, decay_to_end, xs)
    chunk_decay = jnp.exp(cs[..., -1])

    def step(h, inp):
        st, dec = inp
        return h * dec[..., None, None] + st, h

    h_final, h_prev = lax.scan(step, h0.astype(f32).reshape(bt, G, R, P, N),
                               (jnp.moveaxis(chunk_states, 1, 0), jnp.moveaxis(chunk_decay, 1, 0)))
    h_prev = jnp.moveaxis(h_prev, 0, 1)
    y_off = jnp.einsum('bclgn,bcgrpn,bcgrl->bclgrp', cm, h_prev, jnp.exp(cs))
    y = (y_diag + y_off).reshape(bt, l, N_HEADS_A, P)
    return y, h_final.reshape(bt, N_HEADS_A, P, N)

def mamba2_mixer(x, conv_prefix, h0, w_in, conv_w, conv_b, dt_bias, a_log, d_skip, norm_g, w_out):
    f32 = jnp.float32
    bt, l, _ = x.shape
    gn = N_GROUPS_A * D_STATE
    zxbcdt = x @ w_in
    z = zxbcdt[..., :D_INNER]
    xbc = zxbcdt[..., D_INNER:D_INNER + CONV_DIM]
    dt_raw = zxbcdt[..., D_INNER + CONV_DIM:]
    xbc, conv_state = causal_conv(xbc, conv_prefix, conv_w, conv_b)
    xbc = jax.nn.silu(xbc)
    xh = xbc[..., :D_INNER].reshape(bt, l, N_HEADS_A, HEADDIM_A)
    bmat = xbc[..., D_INNER:D_INNER + gn].reshape(bt, l, N_GROUPS_A, D_STATE)
    cmat = xbc[..., D_INNER + gn:].reshape(bt, l, N_GROUPS_A, D_STATE)
    dt = jax.nn.softplus(dt_raw.astype(f32) + dt_bias.astype(f32))
    a = -jnp.exp(a_log.astype(f32))
    y, h_final = ssd_scan(xh, dt, a, bmat, cmat, h0)
    y = y + d_skip.astype(f32)[:, None] * xh.astype(f32)
    y = y.reshape(bt, l, D_INNER) * jax.nn.silu(z.astype(f32))
    yg = y.reshape(bt, l, N_GROUPS_A, D_INNER // N_GROUPS_A)
    yg = yg * lax.rsqrt(jnp.mean(yg * yg, -1, keepdims=True) + RMS_EPS)
    y = (yg.reshape(bt, l, D_INNER) * norm_g).astype(x.dtype)
    return y @ w_out, conv_state, h_final.astype(x.dtype)

def shared_kv(h, w_kv, pos):
    bt, l, _ = h.shape
    kv = h @ w_kv
    k = rope(kv[..., :QK_WIDTH_B].reshape(bt, l, N_HEADS_B, 2, HEAD_DIM_B), pos)
    v = kv[..., QK_WIDTH_B:].reshape(bt, l, N_HEADS_B, 2 * HEAD_DIM_B)
    return k, v

def diff_attn_prompt(q, k, v, lam):
    b, s = q.shape[:2]
    nblk = s // Q_BLOCK
    scale = HEAD_DIM_B ** -0.5
    qb = jnp.moveaxis(q.reshape(b, nblk, Q_BLOCK, N_HEADS_B, 2, HEAD_DIM_B), 1, 0)
    kpos = jnp.arange(s)

    def block(args):
        qi, i = args
        sc = jnp.einsum('bqhmd,bkhmd->bhmqk', qi, k).astype(jnp.float32) * scale
        qpos = i * Q_BLOCK + jnp.arange(Q_BLOCK)
        sc = jnp.where(kpos[None, :] <= qpos[:, None], sc, -jnp.inf)
        p = jax.nn.softmax(sc, axis=-1)
        w = (p[:, :, 0] - lam * p[:, :, 1]).astype(v.dtype)
        return jnp.einsum('bhqk,bkhe->bqhe', w, v)

    out = lax.map(block, (qb, jnp.arange(nblk)))
    return jnp.moveaxis(out, 0, 1).reshape(b, s, N_HEADS_B, 2 * HEAD_DIM_B)

def diff_attn_sample(q, k_new, v_new, k_past, v_past, lam):
    t = q.shape[1]
    lp = k_past.shape[1]
    scale = HEAD_DIM_B ** -0.5
    sc_past = jnp.einsum('bqhmd,bkhmd->bhmqk', q, k_past).astype(jnp.float32)
    sc_new = jnp.einsum('bqhmd,bkhmd->bhmqk', q, k_new).astype(jnp.float32)
    tri = jnp.arange(t)[:, None] >= jnp.arange(t)[None, :]
    sc_new = jnp.where(tri, sc_new, -jnp.inf)
    p = jax.nn.softmax(jnp.concatenate([sc_past, sc_new], -1) * scale, axis=-1)
    w = (p[:, :, 0] - lam * p[:, :, 1]).astype(v_new.dtype)
    return (jnp.einsum('bhqk,bkhe->bqhe', w[..., :lp], v_past)
            + jnp.einsum('bhqk,bkhe->bqhe', w[..., lp:], v_new))

def diff_attention(x, k, v, k_past, v_past, pos, lam_init, w_q, lq1, lk1, lq2, lk2, subln_g, w_o):
    f32 = jnp.float32
    bt, l, _ = x.shape
    q = rope((x @ w_q).reshape(bt, l, N_HEADS_B, 2, HEAD_DIM_B), pos)
    lam = (jnp.exp(jnp.sum(lq1.astype(f32) * lk1.astype(f32)))
           - jnp.exp(jnp.sum(lq2.astype(f32) * lk2.astype(f32))) + lam_init)
    if k_past is None:
        o = diff_attn_prompt(q, k, v, lam)
    else:
        o = diff_attn_sample(q, k, v, k_past, v_past, lam)
    o = rms_norm(o, subln_g) * (1.0 - lam_init)
    return o.reshape(bt, l, V_WIDTH_B) @ w_o

def sq_relu_mlp(x, w_up, w_down):
    return jnp.square(jax.nn.relu(x @ w_up)) @ w_down

def trunk(x, pos, conv_init, ssm_init, k_past, v_past, p):
    conv_out, ssm_out = [], []
    k_sh, v_sh = None, None
    for layer in range(DEPTH):
        if layer < N_A_LAYERS:
            i = layer
            y, cst, hst = mamba2_mixer(x, conv_init[i], ssm_init[i], p['w_in_a'][i], p['conv_w_a'][i],
                                       p['conv_b_a'][i], p['dt_bias_a'][i], p['a_log_a'][i],
                                       p['d_skip_a'][i], p['norm_a'][i], p['w_out_a'][i])
            conv_out.append(cst)
            ssm_out.append(hst)
        else:
            if layer == N_A_LAYERS:
                k_sh, v_sh = shared_kv(x, p['w_kv'], pos)
            j = layer - N_A_LAYERS
            y = diff_attention(x, k_sh, v_sh, k_past, v_past, pos, lambda_init_fn(layer),
                               p['w_q_b'][j], p['lambda_q1_b'][j], p['lambda_k1_b'][j],
                               p['lambda_q2_b'][j], p['lambda_k2_b'][j], p['subln_b'][j], p['w_o_b'][j])
        x = layer_norm(DN_ALPHA * x + y, p['ln_g'][layer, 0], p['ln_b'][layer, 0])
        x = layer_norm(DN_ALPHA * x + sq_relu_mlp(x, p['w_up'][layer], p['w_down'][layer]),
                       p['ln_g'][layer, 1], p['ln_b'][layer, 1])
    return x, jnp.stack(conv_out), jnp.stack(ssm_out), k_sh, v_sh

def setup_inputs(seed: int = 0) -> dict:
    key = jax.random.key(seed)
    ks = jax.random.split(key, 32)
    f32 = jnp.float32
    n_pages = PAST_LEN // PAGE_SIZE
    n_phys = (DEC_BATCH * n_pages * 5) // 4

    def nrm(k, shape, scale):
        return jax.random.normal(k, shape, f32) * scale

    x_prompt = nrm(ks[0], (BATCH, SEQ, D_MODEL), 1.0)
    x_sample = nrm(ks[1], (DEC_BATCH, DEC_SEQ, D_MODEL), 1.0)
    state_conv = nrm(ks[2], (N_A_LAYERS, DEC_BATCH, CONV_W - 1, CONV_DIM), 1.0)
    state_ssm = nrm(ks[3], (N_A_LAYERS, DEC_BATCH, N_HEADS_A, HEADDIM_A, D_STATE), 0.1)
    cache_k = nrm(ks[4], (n_phys, PAGE_SIZE, N_HEADS_B, 2, HEAD_DIM_B), 1.0)
    cache_v = nrm(ks[5], (n_phys, PAGE_SIZE, N_HEADS_B, 2 * HEAD_DIM_B), 1.0)
    page_table = jax.random.permutation(ks[6], n_phys)[:DEC_BATCH * n_pages].reshape(
        DEC_BATCH, n_pages).astype(jnp.int32)

    w_in_a = nrm(ks[7], (N_A_LAYERS, D_MODEL, IN_PROJ_A), D_MODEL ** -0.5)
    conv_w_a = nrm(ks[8], (N_A_LAYERS, CONV_W, CONV_DIM), CONV_W ** -0.5)
    conv_b_a = nrm(ks[9], (N_A_LAYERS, CONV_DIM), 0.01)
    u = jax.random.uniform(ks[10], (N_A_LAYERS, N_HEADS_A), f32)
    dt0 = jnp.exp(u * (math.log(DT_MAX) - math.log(DT_MIN)) + math.log(DT_MIN))
    dt_bias_a = dt0 + jnp.log(-jnp.expm1(-dt0))
    a_log_a = jnp.log(jax.random.uniform(ks[11], (N_A_LAYERS, N_HEADS_A), f32, 1.0, 16.0))
    d_skip_a = 1.0 + nrm(ks[12], (N_A_LAYERS, N_HEADS_A), 0.1)
    norm_a = 1.0 + nrm(ks[13], (N_A_LAYERS, D_INNER), 0.02)
    w_out_a = nrm(ks[14], (N_A_LAYERS, D_INNER, D_MODEL), DN_BETA * D_INNER ** -0.5)

    w_kv = nrm(ks[15], (D_MODEL, QK_WIDTH_B + V_WIDTH_B), D_MODEL ** -0.5)
    w_q_b = nrm(ks[16], (N_B_LAYERS, D_MODEL, QK_WIDTH_B), D_MODEL ** -0.5)
    lambda_q1_b = nrm(ks[17], (N_B_LAYERS, HEAD_DIM_B), 0.1)
    lambda_k1_b = nrm(ks[18], (N_B_LAYERS, HEAD_DIM_B), 0.1)
    lambda_q2_b = nrm(ks[19], (N_B_LAYERS, HEAD_DIM_B), 0.1)
    lambda_k2_b = nrm(ks[20], (N_B_LAYERS, HEAD_DIM_B), 0.1)
    subln_b = 1.0 + nrm(ks[21], (N_B_LAYERS, 2 * HEAD_DIM_B), 0.02)
    w_o_b = nrm(ks[22], (N_B_LAYERS, V_WIDTH_B, D_MODEL), DN_BETA * V_WIDTH_B ** -0.5)

    w_up = nrm(ks[23], (DEPTH, D_MODEL, D_FF), D_MODEL ** -0.5)
    w_down = nrm(ks[24], (DEPTH, D_FF, D_MODEL), DN_BETA * D_FF ** -0.5)
    ln_g = 1.0 + nrm(ks[25], (DEPTH, 2, D_MODEL), 0.02)
    ln_b = nrm(ks[26], (DEPTH, 2, D_MODEL), 0.01)
    return {'x_prompt': x_prompt, 'x_sample': x_sample, 'state_conv': state_conv,
            'state_ssm': state_ssm, 'cache_k': cache_k, 'cache_v': cache_v,
            'page_table': page_table, 'w_in_a': w_in_a, 'conv_w_a': conv_w_a,
            'conv_b_a': conv_b_a, 'dt_bias_a': dt_bias_a, 'a_log_a': a_log_a,
            'd_skip_a': d_skip_a, 'norm_a': norm_a, 'w_out_a': w_out_a, 'w_kv': w_kv,
            'w_q_b': w_q_b, 'lambda_q1_b': lambda_q1_b, 'lambda_k1_b': lambda_k1_b,
            'lambda_q2_b': lambda_q2_b, 'lambda_k2_b': lambda_k2_b, 'subln_b': subln_b,
            'w_o_b': w_o_b, 'w_up': w_up, 'w_down': w_down, 'ln_g': ln_g, 'ln_b': ln_b}

def reference(x_prompt, x_sample, state_conv, state_ssm, cache_k, cache_v, page_table,
              w_in_a, conv_w_a, conv_b_a, dt_bias_a, a_log_a, d_skip_a, norm_a, w_out_a,
              w_kv, w_q_b, lambda_q1_b, lambda_k1_b, lambda_q2_b, lambda_k2_b, subln_b, w_o_b,
              w_up, w_down, ln_g, ln_b):
    params = dict(w_in_a=w_in_a, conv_w_a=conv_w_a, conv_b_a=conv_b_a, dt_bias_a=dt_bias_a,
                  a_log_a=a_log_a, d_skip_a=d_skip_a, norm_a=norm_a, w_out_a=w_out_a,
                  w_kv=w_kv, w_q_b=w_q_b, lambda_q1_b=lambda_q1_b, lambda_k1_b=lambda_k1_b,
                  lambda_q2_b=lambda_q2_b, lambda_k2_b=lambda_k2_b, subln_b=subln_b, w_o_b=w_o_b,
                  w_up=w_up, w_down=w_down, ln_g=ln_g, ln_b=ln_b)
    bp, sp = x_prompt.shape[:2]
    pos_p = jnp.arange(sp)
    conv0 = jnp.zeros((N_A_LAYERS, bp, CONV_W - 1, CONV_DIM), x_prompt.dtype)
    ssm0 = jnp.zeros((N_A_LAYERS, bp, N_HEADS_A, HEADDIM_A, D_STATE), x_prompt.dtype)
    y_prompt, conv_p, ssm_p, k_p, v_p = trunk(x_prompt, pos_p, conv0, ssm0, None, None, params)
    bd, ts = x_sample.shape[:2]
    n_pages = page_table.shape[1]
    pos_s = PAST_LEN + jnp.arange(ts)
    k_past = cache_k[page_table].reshape(bd, n_pages * PAGE_SIZE, N_HEADS_B, 2, HEAD_DIM_B)
    v_past = cache_v[page_table].reshape(bd, n_pages * PAGE_SIZE, N_HEADS_B, 2 * HEAD_DIM_B)
    y_sample, conv_s, ssm_s, k_s, v_s = trunk(x_sample, pos_s, state_conv, state_ssm,
                                              k_past, v_past, params)
    return (y_prompt, y_sample, conv_p, ssm_p, k_p, v_p, conv_s, ssm_s, k_s, v_s)


_drawn_inputs = setup_inputs


def setup_inputs(seed=0):
    import zlib

    import numpy as np

    out = dict(_drawn_inputs(seed))
    spreads = {}
    factors = {'conv_b_a': 3.533,
     'd_skip_a': 2.964,
     'norm_a': 21.035,
     'lambda_q1_b': 4.343,
     'lambda_k1_b': 8.0,
     'lambda_q2_b': 8.0,
     'lambda_k2_b': 8.0,
     'subln_b': 24.693}
    for name, (base, spread) in spreads.items():
        noise = np.random.default_rng([zlib.crc32(name.encode()), seed]).standard_normal(out[name].shape)
        drawn = base * np.exp(spread * noise) if base else spread * noise
        out[name] = jnp.asarray(drawn.astype(out[name].dtype))
    for name, factor in factors.items():
        out[name] = (out[name] * factor).astype(out[name].dtype)
    return out
```

```python
import math
from contextlib import ExitStack

import numpy as np

import concourse.bass as bass
from concourse import mybir

F32 = mybir.dt.float32
F32R = mybir.dt.float32r
BF16 = mybir.dt.bfloat16
I32 = mybir.dt.int32
ALU = mybir.AluOpType
ACT = mybir.ActivationFunctionType
AX = mybir.AxisListType

P = 128
D = 1024
SEQ = 1024
NB = 8
T = SEQ + NB
NCH = 3
CW = T // NCH
KD = D // P
D_INNER = 2048
GN = 1024
HEADS_A = 32
GROUPS = 8
R = HEADS_A // GROUPS
CHUNK = 128
CHUNKS = SEQ // CHUNK
CONV_DIM = D_INNER + 2 * GN
CONV_W = 4
HEADS_B = 8
HD = 64
D_FF = 4096
PAST = 256
PAGES = PAST // P
PHYS = NB * PAGES * 5 // 4
ALPHA = 4.0 ** 0.25
EPS = 1e-5
LAM_INIT = 0.8 - 0.6 * math.exp(-0.3)
SCALE = HD ** -0.5
FFB = D_FF // 512

DT_CHUNKS = 3
MAMBA_JOBS = 2 * (6 + 8)
MAMBA_UNITS = 2 * (6 + 2)
MAMBA_ITERS = GROUPS // 2
MLP_CHUNKS = 3 * FFB * 12
MLP_UNITS = FFB * 8
ATT_JOBS = 4 * 3 + 2 * 8
ATT_UNITS = 4 * 3 + 2 * 2
ATT_ITERS = HEADS_B // 4
C_MAMBA = DT_CHUNKS
C_MLP0 = C_MAMBA + MAMBA_ITERS * MAMBA_JOBS * 3
C_ATT = C_MLP0 + MLP_CHUNKS
C_MLP1 = C_ATT + ATT_ITERS * ATT_JOBS * 3
U_MAMBA = 1
U_MLP0 = U_MAMBA + MAMBA_ITERS * MAMBA_UNITS
U_ATT = U_MLP0 + MLP_UNITS
U_MLP1 = U_ATT + ATT_ITERS * ATT_UNITS
UNITS = U_MLP1 + MLP_UNITS
N_CONST = 9
N_ATTC = 8
N_OUTS = 1 + KD


class Place:

    def __init__(self, chunk0, unit0, i=0, chunks=0, units=0):
        assert chunks % 4 == 0 and units % 2 == 0
        self.q, self.u = chunk0, unit0
        self.i, self.dq, self.du = i, chunks, units

    def chunk(self):
        q = self.q
        self.q += 1
        bank = q % 4
        return bank, self.i * (self.dq // 4) + q // 4 + 1, self.i * self.dq + q + 1

    def unit(self):
        u = self.u
        self.u += 1
        return u % 2, self.i * self.du + u + 1


def program(nc, a, o):
    with ExitStack() as ctx:
        def sb(name, shape, dt=F32, into=None):
            return (into or ctx).enter_context(nc.sbuf_tensor(name, shape, dt))

        def sem(name):
            return ctx.enter_context(nc.semaphore(name))

        xh = sb("xh", [P, KD, T], F32R)
        xl = sb("xl", [P, KD, T], F32R)
        acc = sb("acc", [P, KD, T])
        wraw = sb("wraw", [P, 2, 8, P])
        wh0 = sb("wh0", [P, 8, P], F32R)
        wh1 = sb("wh1", [P, 8, P], F32R)
        wl0 = sb("wl0", [P, 8, P], F32R)
        wl1 = sb("wl1", [P, 8, P], F32R)
        wh, wl = [wh0, wh1], [wl0, wl1]
        ident = sb("ident", [P, P])
        ones = sb("ones", [P, 3, P])
        lnp = sb("lnp", [P, 4, 2, KD])
        eps = sb("eps", [P, 1])
        one = sb("one", [P, 1])
        mix = ctx.enter_context(ExitStack())
        yh = sb("yh", [P, 2, T], F32R, mix)
        yl = sb("yl", [P, 2, T], F32R, mix)
        m = mix.enter_context(ExitStack())
        xbc = sb("xbc", [P, 4, T], F32, m)
        zs = sb("zs", [P, 2, T], F32, m)
        y = sb("y", [P, 2, T], F32, m)
        pre = sb("pre", [P, 2, 4 + T], F32, m)
        csg = sb("csg", [8, T + NB], F32R, m)
        dm = sb("dm", [P, 2, 512], F32, m)
        bt = sb("bt", [P, P], F32, m)
        xs = sb("xs", [P, 256], F32, m)
        xe = sb("xe", [P, 256], F32, m)
        e2 = sb("e2", [P, 256], F32, m)
        tok = sb("tok", [P, 4, CHUNKS, HEADS_A], F32, m)
        tg = sb("tg", [P, 4, CHUNKS, R], F32, m)
        hst = sb("hst", [P, 256], F32, m)
        selh = sb("selh", [8, R, P], F32R, m)
        selt = sb("selt", [8, 2, P], F32R, m)
        row127 = sb("row127", [P, P], F32, m)
        capm = sb("capm", [P, P], F32, m)
        scv = sb("scv", [P, 4, 3, NB], F32, m)
        pall = sb("pall", [P, GROUPS, 24], F32, m)
        pg = sb("pg", [P, 24], F32, m)
        cnew = sb("cnew", [P, 4, 11], F32, m)
        dec = sb("dec", [P, 2, 8], F32, m)
        dts = sb("dts", [P, 2, 8], F32, m)
        xdt = sb("xdt", [P, 2, 8], F32, m)
        a32 = sb("a32", [HEADS_A, 4], F32, m)
        m.close()
        m = mix.enter_context(ExitStack())
        dtx = sb("dtx", [HEADS_A, T + NB], F32, m)
        dtt = sb("dtt", [HEADS_A, T], F32, m)
        scanm = sb("scanm", [HEADS_A, T], F32, m)
        cs = sb("cs", [HEADS_A, T + NB], F32, m)
        csh = sb("csh", [HEADS_A, T + NB], F32R, m)
        csl = sb("csl", [HEADS_A, T + NB], F32R, m)
        m.close()
        m = mix.enter_context(ExitStack())
        qh = sb("qh", [P, T], F32R, m)
        ql = sb("ql", [P, T], F32R, m)
        kh = sb("kh", [P, T], F32R, m)
        kl = sb("kl", [P, T], F32R, m)
        raw = sb("raw", [P, T], F32, m)
        rot = sb("rot", [P, T], F32, m)
        cos = sb("cos", [P, T], F32, m)
        sin = sb("sin", [P, T], F32, m)
        pp = sb("pp", [P, 2048], F32, m)
        wth = sb("wth", [P, KD, P], F32R, m)
        wtl = sb("wtl", [P, KD, P], F32R, m)
        vth = sb("vth", [P, KD, P], F32R, m)
        vtl = sb("vtl", [P, KD, P], F32R, m)
        past = sb("past", [P, NB * PAGES, P], F32, m)
        perm = sb("perm", [P, P], F32, m)
        mbf = sb("mbf", [P, 2, P], BF16, m)
        lamv = sb("lamv", [P, 4, HD], F32, m)
        lam = sb("lam", [P, 4], F32, m)
        subg = sb("subg", [P, 1], F32, m)
        half = sb("half", [P, 2, NB], F32, m)
        pair = sb("pair", [16, 12], F32, m)
        smp = sb("smp", [P, 3, NB], F32, m)
        qkn = sb("qkn", [P, 2, NB], F32, m)
        st = sb("st", [P, 8], F32, m)
        srow = sb("srow", [16, 264], F32, m)
        ssc = sb("ssc", [P, PAGES, 2, NB], F32, m)
        wsm = sb("wsm", [P, 3, NB], F32, m)
        m.close()
        mix.close()
        m = ctx.enter_context(ExitStack())
        hh = [sb(f"hh{b}", [P, 4, T], F32R, m) for b in range(2)]
        hl = [sb(f"hl{b}", [P, 4, T], F32R, m) for b in range(2)]
        rl = sb("rl", [P, 4, CW], F32, m)
        m.close()
        m = ctx.enter_context(ExitStack())
        ln0 = sb("ln0", [P, T], F32, m)
        lnq = sb("lnq", [P, 2, T], F32, m)
        m.close()

        jb = ctx.enter_context(nc.psum_tensor("jb", [P, 4, 512], F32))
        aux = ctx.enter_context(nc.psum_tensor("aux", [P, 4, 512], F32))

        csd = nc.dram_tensor("csd", [2, HEADS_A, T + NB], F32, kind="Internal").ap()
        kgat = nc.dram_tensor("kgat", [NB * PAGES, P, D], F32, kind="Internal").ap()
        vgat = nc.dram_tensor("vgat", [NB * PAGES, P, D], F32, kind="Internal").ap()

        raw_in = [sem("raw_in0"), sem("raw_in1")]
        w_split = sem("w_split")
        unit_begun = sem("unit_begun")
        chunk_full = sem("chunk_full")
        bank_free = [sem(f"bank_free{b}") for b in range(4)]
        names = """const_in attc_in x_in x_hi x_ready outs ptab_in gathered
            dt_raw dt_abs dt_exp dt_soft a_neg cs_hi cs_lo cs_stored tok_ps tok_cp end_ps cd_done dte_arg dte_exp tok_done
            sel_done par_half csg_in scv_in cnew_full cnew_out pre_full conv_done tanh_done xbc_done z_full z_done
            h_zero ssd_in ssd_off ssd_b bt_ready e2_ready d_ready e_ready m_ready h_done h_out
            s_in bcs_full dec_ready bb_full cb_full s_new s_out
            yg_ready sq_done sq_sum rms_full rms_sqrt yn_ready y_hi y_lo
            relu_done h_sq h_ready
            ln_sum ln_mu ln_cent ln_sq ln_add ln_var ln_std ln_norm ln_aff ln_hi ln_lo
            lam_sum lam_exp lam_done raw_full perm_full rope_done qk_hi qk_lo k_out raw_v vt_ps vt_hi vt_ready v_out
            s_full nmax_ready p_ready w_ready wt_ps wt_hi wt_ready pv_full o_ready
            qb_full pk_in ssc_ready qkn_ready srow_full snm_ready sexp_ready sp_ready wsm_full wsm_ready pv_in so_full o_smp
            osq_done orms_full orms_sqrt on_ready""".split()
        s = {n: sem(n) for n in names}

        block = ctx.enter_context(nc.Block())

        @block.sync
        def _(sp):
            for u in range(2):
                sp.dma_start(wraw[:, u], a["wstream"][u]).then_inc(raw_in[u], 16)
            sp.dma_start(acc[:], a["xT"]).then_inc(s["x_in"], 16)
            for dst, name in ((ident, "ident"), (ones, "ones"), (lnp, "lnp"), (row127, "row127"),
                              (capm, "capm"), (pall, "par"), (a32, "a32"), (scanm, "scanm")):
                sp.dma_start(dst[:], a[name]).then_inc(s["const_in"], 16)
            sp.dma_start(pre[0:8, 0, 4:772], a["sel"]).then_inc(s["const_in"], 16)
            with sp.Fori(0, (UNITS - 3) // 2) as i:
                for k in range(2):
                    sp.wait_ge(w_split, 2 * i + k + 1)
                    sp.dma_start(wraw[:, k], a["wstream"][2 * i + (k + 2)]).then_inc(raw_in[k], 16)
            sp.wait_ge(w_split, UNITS - 2)
            sp.dma_start(wraw[:, 0], a["wstream"][UNITS - 1]).then_inc(raw_in[0], 16)
            sp.wait_ge(s["outs"], 16 * N_OUTS)

        @block.gpsimd
        def _(pool):
            def split(slot, loaded, begun):
                pool.wait_ge(raw_in[slot], loaded)
                if begun is not None:
                    pool.wait_ge(unit_begun, begun)
                nc.gpsimd.tensor_tensor(wh[slot][:].rearrange("p k m -> p (k m)"), wraw[:, slot].rearrange("p k m -> p (k m)"),
                                        one[:].to_broadcast([P, 8 * P]), ALU.mult)
                pool.drain()
                nc.gpsimd.tensor_tensor(wl[slot][:], wraw[:, slot], wh[slot][:].bitcast(F32),
                                        ALU.subtract).then_inc(w_split, 1)

            nc.gpsimd.memset(one[:], 1.0)
            pool.drain()
            split(0, 16, None)
            split(1, 16, None)
            with pool.Fori(1, (UNITS - 1) // 2) as i:
                split(0, 16 * i + 16, 2 * i)
                split(1, 16 * i + 16, 2 * i + 1)
            split(0, 16 * ((UNITS - 1) // 2) + 16, UNITS - 1)

        @block.tensor
        def _(pe):
            mm = nc.tensor.matmul

            def jobs(at, n, kt, rh, rlo, ready=None):
                for j in range(n):
                    first = (j * kt) % 8 == 0
                    if first:
                        slot, nth = at.unit()
                        pe.wait_ge(w_split, nth)
                    w0 = (j * kt) % 8
                    for c in range(NCH):
                        bank, uses, _ = at.chunk()
                        pe.wait_ge(bank_free[bank], uses)
                        out = jb[:, bank, 0:CW]
                        cols = slice(c * CW, (c + 1) * CW)
                        for k in range(kt):
                            for w, x, p in ((wh, rh, 0), (wh, rlo, 1), (wl, rh, 2)):
                                last = mm(out, w[slot][:, w0 + k], x[:, k, cols],
                                          start=(k == 0 and p == 0), stop=(k == kt - 1 and p == 2))
                                if first and c == 0 and k == 0 and p == 0:
                                    last.then_inc(unit_begun, 1)
                        last.then_inc(chunk_full, 1)

            pe.wait_ge(s["x_ready"], KD)
            pe.wait_ge(s["const_in"], 16 * N_CONST)
            pe.wait_ge(s["sel_done"], 1)
            at = Place(0, 0)
            jobs(at, 1, KD, xh, xl)
            pe.wait_ge(s["cs_hi"], 1)
            for k, src in enumerate((cs, dtx)):
                for c in range(CHUNKS):
                    last = nc.tensor.transpose(aux[:, 0, (k * CHUNKS + c) * HEADS_A:(k * CHUNKS + c + 1) * HEADS_A],
                                               src[:, c * CHUNK:(c + 1) * CHUNK], ident[0:HEADS_A, 0:HEADS_A])
            last.then_inc(s["tok_ps"], 1)
            pe.wait_ge(s["tok_cp"], 1)
            mm(aux[:, 1, 0:256], row127[:], tok[:, 0].rearrange("p c h -> p (c h)"), start=True,
               stop=True).then_inc(s["end_ps"], 1)

            def scan_group(n):
                pe.wait_ge(s["xbc_done"], 4 * n + 4)
                pe.wait_ge(s["csg_in"], 32 * n + 32)
                pe.wait_ge(s["h_zero"], n + 1)
                for c in range(CHUNKS):
                    cols = slice(c * CHUNK, (c + 1) * CHUNK)
                    if c:
                        pe.wait_ge(s["h_done"], 8 * n + c)
                    nc.tensor.transpose(aux[:, 0, 0:128], xbc[:, 0, cols], ident[:])
                    nc.tensor.transpose(aux[:, 0, 128:256], xbc[:, 1, cols], ident[:])
                    nc.tensor.transpose(aux[:, 2, 256:384], xbc[:, 2, cols], ident[:])
                    mm(aux[:, 0, 384:512], xbc[:, 2, cols], xbc[:, 3, cols], start=True, stop=True)
                    for t in range(2):
                        mm(aux[:, 2, t * 128:128 + t * 128], selt[:, t], csg[:, cols], start=True, stop=True)
                    for r in range(R):
                        last = mm(aux[:, 1, r * 128:(r + 1) * 128], selh[:, r], csg[:, cols], start=True, stop=True)
                    last.then_inc(s["ssd_in"], 1)
                    for t in range(2):
                        last = mm(aux[:, 3, t * 128:128 + t * 128], hst[:, t * 128:(t + 1) * 128],
                                  xbc[:, 3, cols], start=True, stop=True)
                    last.then_inc(s["ssd_off"], 1)
                    pe.wait_ge(s["m_ready"], 8 * n + c + 1)
                    for r in range(R):
                        half_ = slice(64 * (r % 2), 64 * (r % 2) + 64)
                        mm(aux[half_, 1, (r // 2) * 128:(r // 2) * 128 + 128], xs[:, r * 64:(r + 1) * 64],
                           dm[:, 1, r * 128:(r + 1) * 128], start=True, stop=True)
                    pe.wait_ge(s["bt_ready"], 8 * n + c + 1)
                    mm(aux[:, 1, 256:512], bt[:], xe[:], start=True, stop=True).then_inc(s["ssd_b"], 1)
                pe.wait_ge(s["h_done"], 8 * n + 8)
                for t in range(2):
                    last = mm(aux[:, 0, t * 16:t * 16 + 16], selt[:, t], csg[:, SEQ:SEQ + 16], start=True, stop=True)
                last.then_inc(s["bcs_full"], 1)
                for b in range(NB):
                    last = mm(aux[:, 2 + b // 4, (b % 4) * 128:(b % 4) * 128 + 128],
                              xbc[:, 2, SEQ + b:SEQ + b + 1].to_broadcast([P, P]), ident[:], start=True, stop=True)
                last.then_inc(s["bb_full"], 1)
                pe.wait_ge(s["dec_ready"], n + 1)
                for b in range(NB):
                    last = mm(aux[:, b // 4, (b % 4) * 128:(b % 4) * 128 + 128],
                              xbc[:, 3, SEQ + b:SEQ + b + 1].to_broadcast([P, P]), ident[:], start=True, stop=True)
                last.then_inc(s["cb_full"], 1)
                pe.wait_ge(s["sq_sum"], n + 1)
                for c in range(NCH):
                    last = mm(aux[:, c, 0:CW], ones[:, 1], zs[:, 0, c * CW:(c + 1) * CW], start=True, stop=True)
                last.then_inc(s["rms_full"], 1)

            with pe.Fori(0, MAMBA_ITERS) as i:
                at = Place(C_MAMBA, U_MAMBA, i, MAMBA_JOBS * 3, MAMBA_UNITS)
                for par in range(2):
                    n = 2 * i + par
                    jobs(at, 6, KD, xh, xl)
                    scan_group(n)
                    pe.wait_ge(s["y_lo"], 2 * n + 4)
                    jobs(at, 8, 2, yh, yl)

            def layer_norm(l):
                pe.wait_ge(s["ln_sum"], l + 1)
                for c in range(NCH):
                    last = mm(aux[:, c, 0:CW], ones[:, 0], ln0[:, c * CW:(c + 1) * CW], start=True, stop=True)
                last.then_inc(s["ln_mu"], 1)
                pe.wait_ge(s["ln_add"], 8 * l + 8)
                for c in range(NCH):
                    last = mm(aux[:, c, 0:CW], ones[:, 0], ln0[:, c * CW:(c + 1) * CW], start=True, stop=True)
                last.then_inc(s["ln_var"], 1)

            def mlp(layer):
                c0, u0 = ((C_MLP0, U_MLP0), (C_MLP1, U_MLP1))[layer]
                l = 2 * layer
                pe.wait_ge(s["ln_lo"], 8 * (l + 1))
                hb = layer * FFB

                def up(at):
                    jobs(at, 4, KD, xh, xl)

                def down(at, b, nth):
                    pe.wait_ge(s["h_ready"], nth)
                    jobs(at, 8, 4, hh[b], hl[b])

                up(Place(c0, u0))
                with pe.Fori(0, FFB // 2 - 1) as i:
                    at = Place(c0 + 12, u0 + 4, i, 72, 16)
                    up(at)
                    down(at, 0, (hb + 2 * i) * 12 + 12)
                    up(at)
                    down(at, 1, (hb + 2 * i) * 12 + 24)
                at = Place(c0 + 12 + 72 * (FFB // 2 - 1), u0 + 4 + 16 * (FFB // 2 - 1))
                up(at)
                down(at, 0, (hb + FFB - 1) * 12)
                down(at, 1, (hb + FFB) * 12)

            layer_norm(0)
            mlp(0)
            layer_norm(1)

            def attend(n):
                pe.wait_ge(s["raw_v"], n + 1)
                for c in range(8):
                    last = nc.tensor.transpose(aux[:, c // 4, (c % 4) * 128:(c % 4) * 128 + 128],
                                               raw[:, c * 128:(c + 1) * 128], ident[:])
                last.then_inc(s["vt_ps"], 1)
                pe.wait_ge(s["vt_ready"], n + 1)
                for i in range(8):
                    rows = slice(i * 128, (i + 1) * 128)
                    width = (i + 1) * 128
                    for mm_ in range(2):
                        if i:
                            pe.wait_ge(s["p_ready"], 16 * n + 2 * i + mm_ - 1)
                        part = slice(64 * mm_, 64 * mm_ + 64)
                        for c0 in range(0, width, 512):
                            w = min(512, width - c0)
                            out = aux[:, 2 * mm_ + c0 // 512, 0:w]
                            diag = c0 + w == width
                            for p, (qq, kk) in enumerate(((qh, kh), (ql, kh), (qh, kl))):
                                last = mm(out, qq[part, rows], kk[part, c0:c0 + w], start=(p == 0),
                                          stop=(p == 2 and not diag))
                            if diag:
                                last = mm(aux[:, 2 * mm_ + c0 // 512, w - 128:w], mbf[:, 0], mbf[:, 1],
                                          start=False, stop=True)
                        last.then_inc(s["s_full"], 1)
                    pe.wait_ge(s["w_ready"], 8 * n + i + 1)
                    for k in range(i + 1):
                        last = nc.tensor.transpose(jb[:, k // 4, (k % 4) * 128:(k % 4) * 128 + 128],
                                                   pp[:, k * 128:(k + 1) * 128], ident[:])
                    last.then_inc(s["wt_ps"], 1)
                    pe.wait_ge(s["wt_ready"], 8 * n + i + 1)
                    for k in range(i + 1):
                        for p, (vv, ww) in enumerate(((vth, wth), (vtl, wth), (vth, wtl))):
                            last = mm(jb[:, 2, 0:128], vv[:, k], ww[:, k], start=(k == 0 and p == 0),
                                      stop=(k == i and p == 2))
                    last.then_inc(s["pv_full"], 1)
                for b in range(NB):
                    last = mm(aux[:, b // 4, (b % 4) * 128:(b % 4) * 128 + 128],
                              smp[:, 0, b:b + 1].to_broadcast([P, P]), ident[:], start=True, stop=True)
                last.then_inc(s["qb_full"], 1)
                pe.wait_ge(s["qkn_ready"], n + 1)
                mm(aux[0:16, 2, 256:257], qkn[:].rearrange("p m b -> p (m b)"), ones[:, 2, 0:1] , start=True, stop=True)
                pe.wait_ge(s["ssc_ready"], n + 1)
                for g in range(PAGES):
                    last = nc.tensor.transpose(aux[0:16, 2, g * 128:(g + 1) * 128],
                                               ssc[:, g].rearrange("p m b -> p (m b)"), ident[:])
                last.then_inc(s["srow_full"], 1)
                pe.wait_ge(s["sp_ready"], n + 1)
                for g in range(PAGES):
                    mm(aux[:, 3, g * 8:g * 8 + 8], srow[0:16, g * 128:(g + 1) * 128], pair[0:16, 0:8], start=True, stop=True)
                mm(aux[:, 3, 16:24], srow[0:16, 256:257].to_broadcast([16, P]), pair[0:16, 0:8], start=True,
                   stop=True).then_inc(s["wsm_full"], 1)
                pe.wait_ge(s["wsm_ready"], n + 1)
                pe.wait_ge(s["pv_in"], 16 * n + 16)
                for b in range(NB):
                    for g in range(PAGES):
                        last = mm(aux[:, 3, 32 + b:33 + b], past[:, b * PAGES + g], wsm[:, g, b:b + 1],
                                  start=(g == 0), stop=(g == PAGES - 1))
                last.then_inc(s["so_full"], 1)
                pe.wait_ge(s["osq_done"], n + 1)
                for c in range(NCH):
                    last = mm(aux[:, c, 0:CW], ones[:, 2], rot[:, c * CW:(c + 1) * CW], start=True, stop=True)
                last.then_inc(s["orms_full"], 1)

            pe.wait_ge(s["ln_lo"], 16)
            pe.wait_ge(s["attc_in"], 16 * N_ATTC)
            with pe.Fori(0, ATT_ITERS) as i:
                at = Place(C_ATT, U_ATT, i, ATT_JOBS * 3, ATT_UNITS)
                for par in range(4):
                    n = 4 * i + par
                    for j in range(3):
                        jobs(at, 1, KD, xh, xl)
                        if j < 2:
                            pe.wait_ge(s["raw_full"], 2 * n + j + 1)
                            for c in range(NCH):
                                last = mm(aux[:, c, 0:CW], perm[:], raw[:, c * CW:(c + 1) * CW], start=True, stop=True)
                            last.then_inc(s["perm_full"], 1)
                    attend(n)
                    if par % 2:
                        pe.wait_ge(s["y_lo"], 2 * GROUPS + n + 3)
                        jobs(at, 8, 2, yh, yl)

            layer_norm(2)
            pe.wait_ge(s["ln_lo"], 24)
            mlp(1)
            layer_norm(3)

        @block.scalar
        def _(act):
            af = nc.scalar.activation

            for b in range(4):
                act.sem_inc(bank_free[b], 1)
            act.sem_inc(s["s_out"], 32)
            act.sem_inc(s["h_out"], 16)
            act.sem_inc(s["cnew_out"], 16)
            for k in range(NB * PAGES):
                    pv = act.value_load(a["ptab"][0:1, k:k + 1], min_val=0, max_val=PHYS - 1)
                    act.dma_start(kgat[k], a["cache_k"][bass.ds(pv, 1)].rearrange("a p d -> (a p) d")).then_inc(s["gathered"], 16)
                    act.dma_start(vgat[k], a["cache_v"][bass.ds(pv, 1)].rearrange("a p d -> (a p) d")).then_inc(s["gathered"], 16)
            act.dma_start(o["conv_old"], a["conv_keep"]).then_inc(s["outs"], 16)
            act.wait_ge(s["x_in"], 16)
            for k in range(KD):
                af(xh[:, k], acc[:, k], ACT.Copy).then_inc(s["x_hi"], 1)
            act.wait_ge(s["const_in"], 16 * N_CONST)
            af(selh[:], pre[0:8, 0, 4:516].rearrange("p (r c) -> p r c", r=R), ACT.Copy)
            af(selt[:], pre[0:8, 0, 516:772].rearrange("p (r c) -> p r c", r=2), ACT.Copy).then_inc(s["sel_done"], 1)

            at = Place(0, 0)
            for c in range(NCH):
                bank, _, nth = at.chunk()
                act.wait_ge(chunk_full, nth)
                last = af(dtx[:, c * CW:(c + 1) * CW], jb[0:HEADS_A, bank, 0:CW], ACT.Identity, bias=a32[:, 0:1])
                last.then_inc(bank_free[bank], 1)
            af(a32[:, 2:3], a32[:, 1:2], ACT.Exp).then_inc(s["dt_raw"], 1)
            act.wait_ge(s["dt_abs"], 1)
            af(dtt[:], dtt[:], ACT.Exp, scale=-1.0)
            act.drain()
            af(dtt[:], dtt[:], ACT.Ln, bias=1.0).then_inc(s["dt_exp"], 1)
            act.wait_ge(s["dt_soft"], 1)
            af(csh[:], cs[:], ACT.Copy).then_inc(s["cs_hi"], 1)
            act.wait_ge(s["tok_ps"], 1)
            af(tok[:, 0:2], aux[:, 0].rearrange("p (k c h) -> p k c h", k=2, c=CHUNKS), ACT.Copy).then_inc(s["tok_cp"], 1)
            act.wait_ge(s["end_ps"], 1)
            af(tok[:, 3], aux[:, 1, 0:256].rearrange("p (c h) -> p c h", c=CHUNKS), ACT.Exp).then_inc(s["cd_done"], 1)
            act.wait_ge(s["dte_arg"], 1)
            af(tok[:, 2], tok[:, 2], ACT.Exp).then_inc(s["dte_exp"], 1)
            act.wait_ge(s["cs_lo"], 1)
            act.dma_start(csd[0], csh[:].bitcast(F32)).then_inc(s["cs_stored"], 16)
            act.dma_start(csd[1], csl[:].bitcast(F32)).then_inc(s["cs_stored"], 16)
            act.wait_ge(s["cs_stored"], 32)
            act.wait_ge(s["tok_done"], 1)

            def group(at, n):
                act.wait_ge(s["y_lo"], 2 * n + 2)
                for k in range(2):
                    act.dma_start(csg[4 * k:4 * k + 4].bitcast(F32), csd[k, bass.ds(n * R, R)]).then_inc(s["csg_in"], 16)
                act.dma_start(scv[:], a["sconv"][:, bass.ds(n, 1)].rearrange("p a t k b -> p (a t) k b")).then_inc(s["scv_in"], 16)
                act.wait_ge(s["s_out"], 32 * n + 32)
                for t in range(4):
                    if t >= 2:
                        act.wait_ge(s["xbc_done"], 4 * n + t - 1)
                    for c in range(NCH):
                        bank, _, nth = at.chunk()
                        act.wait_ge(chunk_full, nth)
                        last = af(pre[:, t % 2, 4 + c * CW:4 + (c + 1) * CW], jb[:, bank, 0:CW], ACT.Copy)
                        last.then_inc(bank_free[bank], 1)
                    act.drain()
                    if t == 0:
                        act.wait_ge(s["cnew_out"], 16 * n + 16)
                    af(cnew[:, t], pre[:, t % 2, 4 + SEQ - 3:4 + T], ACT.Copy).then_inc(s["pre_full"], 1)
                    act.wait_ge(s["conv_done"], 4 * n + t + 1)
                    af(pre[:, t % 2, 4:4 + T], y[:, 0], ACT.Tanh).then_inc(s["tanh_done"], 1)
                act.wait_ge(s["pre_full"], 4 * n + 4)
                act.dma_start(o["conv_new"][:, bass.ds(n, 1)].rearrange("p a t k -> p (a t) k"), cnew[:]).then_inc(s["cnew_out"], 16)
                for t in range(2):
                    act.wait_ge(s["xbc_done"], 4 * n + 3 + t)
                    for c in range(NCH):
                        bank, _, nth = at.chunk()
                        cols = slice(c * CW, (c + 1) * CW)
                        act.wait_ge(chunk_full, nth)
                        af(pre[:, t, 4 + c * CW:4 + (c + 1) * CW], jb[:, bank, 0:CW], ACT.Tanh, scale=0.5)
                        last = af(zs[:, t, cols], jb[:, bank, 0:CW], ACT.Copy, scale=0.5)
                        last.then_inc(bank_free[bank], 1)
                    act.drain().then_inc(s["z_full"], 1)
                act.wait_ge(s["z_done"], n + 1)
                for t in range(2):
                    act.dma_start(pre[:, t, 4:4 + SEQ].rearrange("p (b n) -> p b n", b=NB),
                                  a["state"][:, bass.ds(2 * n + t, 1)].rearrange("p a b n -> p (a b) n")).then_inc(s["s_in"], 16)
                for c in range(CHUNKS):
                    x = 8 * n + c
                    act.wait_ge(s["ssd_in"], x + 1)
                    if c:
                        act.wait_ge(s["h_done"], x)
                    af(bt[:], aux[:, 2, 256:384], ACT.Copy).then_inc(s["bt_ready"], 1)
                    af(e2[:], aux[:, 2, 0:256], ACT.Exp).then_inc(s["e2_ready"], 1)
                    act.wait_ge(s["d_ready"], x + 1)
                    af(dm[:, 0], dm[:, 0], ACT.Exp).then_inc(s["e_ready"], 1)
                act.wait_ge(s["h_done"], 8 * n + 8)
                act.dma_start(o["ssm_p"][:, bass.ds(n, 1)].rearrange("p a q -> p (a q)"), hst[:]).then_inc(s["h_out"], 16)
                act.wait_ge(s["bcs_full"], n + 1)
                v = aux[:, 0, 0:32].rearrange("p (t c) -> p t c", t=2)
                af(dec[:], v[:, :, 0:8], ACT.Exp)
                af(dts[:], v[:, :, 8:16], ACT.Copy).then_inc(s["dec_ready"], 1)
                for t in range(2):
                    act.wait_ge(s["s_new"], 2 * n + t + 1)
                    act.dma_start(o["ssm_s"][:, bass.ds(2 * n + t, 1)].rearrange("p a b n -> p (a b) n"),
                                  pre[:, t, 4:4 + SEQ].rearrange("p (b n) -> p b n", b=NB)).then_inc(s["s_out"], 16)
                for t in range(2):
                    act.wait_ge(s["yg_ready"], 2 * n + t + 1)
                    af(zs[:, t], y[:, t], ACT.Square).then_inc(s["sq_done"], 1)
                act.wait_ge(s["rms_full"], n + 1)
                af(zs[:, 1].rearrange("p (c w) -> p c w", c=NCH), aux[:, 0:3, 0:CW], ACT.Sqrt, bias=eps[:]).then_inc(s["rms_sqrt"], 1)
                for t in range(2):
                    act.wait_ge(s["yn_ready"], 2 * n + t + 1)
                    af(yh[:, t], y[:, t], ACT.Copy).then_inc(s["y_hi"], 1)

            with act.Fori(0, MAMBA_ITERS) as i:
                at = Place(C_MAMBA, U_MAMBA, i, MAMBA_JOBS * 3, MAMBA_UNITS)
                for par in range(2):
                    group(at, 2 * i + par)
                    for _ in range(8 * NCH):
                        at.chunk()

            def layer_norm(l):
                for k in range(KD):
                    act.wait_ge(s["ln_cent"], 8 * l + k + 1)
                    if k >= 2:
                        act.wait_ge(s["ln_add"], 8 * l + k - 1)
                    af(lnq[:, k % 2], acc[:, k], ACT.Square).then_inc(s["ln_sq"], 1)
                act.wait_ge(s["ln_var"], l + 1)
                af(lnq[:, 0].rearrange("p (c w) -> p c w", c=NCH), aux[:, 0:3, 0:CW], ACT.Sqrt, bias=eps[:]).then_inc(s["ln_std"], 1)
                for k in range(KD):
                    act.wait_ge(s["ln_norm"], 8 * l + k + 1)
                    af(acc[:, k], acc[:, k], ACT.Identity, scale=lnp[:, l, 0, k:k + 1], bias=lnp[:, l, 1, k:k + 1]).then_inc(s["ln_aff"], 1)
                    if l < 3:
                        act.drain()
                        af(xh[:, k], acc[:, k], ACT.Copy).then_inc(s["ln_hi"], 1)
                    else:
                        act.wait_ge(s["ln_aff"], 8 * l + k + 1)
                        act.dma_start(o["yT"][:, k], acc[:, k]).then_inc(s["outs"], 16)

            def mlp(layer):
                c0, u0 = ((C_MLP0, U_MLP0), (C_MLP1, U_MLP1))[layer]
                hb = layer * FFB

                def up(at, b, block_):
                    for j in range(4):
                        for c in range(NCH):
                            bank, _, nth = at.chunk()
                            e = block_ * 12 + j * 3 + c
                            cols = slice(c * CW, (c + 1) * CW)
                            act.wait_ge(chunk_full, nth)
                            slot = (j * 3 + c) % 4
                            act.wait_ge(s["h_ready"], e - 3 if not isinstance(e, int) else max(e - 3, 0))
                            af(rl[:, slot], jb[:, bank, 0:CW], ACT.Relu).then_inc(bank_free[bank], 1)
                            act.drain()
                            af(hh[b][:, j, cols], rl[:, slot], ACT.Square).then_inc(s["h_sq"], 1)

                def down(at):
                    for _ in range(8 * NCH):
                        at.chunk()

                up(Place(c0, u0), 0, hb)
                with act.Fori(0, FFB // 2 - 1) as i:
                    at = Place(c0 + 12, u0 + 4, i, 72, 16)
                    up(at, 1, hb + 2 * i + 1)
                    down(at)
                    act.wait_ge(s["relu_done"], layer * FFB + 2 * i + 1)
                    up(at, 0, hb + 2 * i + 2)
                    down(at)
                    act.wait_ge(s["relu_done"], layer * FFB + 2 * i + 2)
                at = Place(c0 + 12 + 72 * (FFB // 2 - 1), u0 + 4 + 16 * (FFB // 2 - 1))
                up(at, 1, hb + FFB - 1)

            act.wait_ge(s["h_out"], 16 * GROUPS + 16)
            act.wait_ge(s["s_out"], 32 * GROUPS + 32)
            act.wait_ge(s["cnew_out"], 16 * GROUPS + 16)
            layer_norm(0)
            mlp(0)
            layer_norm(1)

            act.wait_ge(s["ln_lo"], 16)
            for dst, name in ((cos, "cos"), (sin, "sin"), (perm, "perm"), (mbf, "mbf"), (subg, "subg"),
                              (half, "half"), (pair, "pair")):
                act.dma_start(dst[:], a[name]).then_inc(s["attc_in"], 16)
            act.dma_start(lamv[:], a["lamv"].partition_broadcast(P)).then_inc(s["attc_in"], 16)
            act.wait_ge(s["gathered"], 16 * 2 * NB * PAGES)
            act.wait_ge(s["lam_sum"], 1)
            af(lam[:, 0:2], lam[:, 0:2], ACT.Exp).then_inc(s["lam_exp"], 1)

            def head(at, n, par):
                act.wait_ge(s["o_smp"], n + 1)
                act.dma_start(past[:], kgat[:, :, bass.ds(n * P, P)].rearrange("g t d -> t g d")).then_inc(s["pk_in"], 16)
                for j in range(2):
                    if j == 0:
                        act.wait_ge(s["y_lo"], 2 * GROUPS + n + 2)
                    else:
                        act.wait_ge(s["rope_done"], 2 * n + 1)
                    for c in range(NCH):
                        bank, _, nth = at.chunk()
                        act.wait_ge(chunk_full, nth)
                        af(raw[:, c * CW:(c + 1) * CW], jb[:, bank, 0:CW], ACT.Copy).then_inc(bank_free[bank], 1)
                    act.drain().then_inc(s["raw_full"], 1)
                    act.wait_ge(s["rope_done"], 2 * n + j + 1)
                    af((qh, kh)[j][:], rot[:], ACT.Copy).then_inc(s["qk_hi"], 1)
                    if j:
                        act.dma_start(o["kT"][:, bass.ds(n, 1)].rearrange("p a t -> p (a t)"), rot[:]).then_inc(s["k_out"], 16)
                for c in range(NCH):
                    bank, _, nth = at.chunk()
                    act.wait_ge(chunk_full, nth)
                    af(raw[:, c * CW:(c + 1) * CW], jb[:, bank, 0:CW], ACT.Copy).then_inc(bank_free[bank], 1)
                act.drain().then_inc(s["raw_v"], 1)
                act.wait_ge(s["raw_v"], n + 1)
                act.dma_start(o["vT"][:, bass.ds(n, 1)].rearrange("p a t -> p (a t)"), raw[:]).then_inc(s["v_out"], 16)
                act.wait_ge(s["vt_ps"], n + 1)
                af(vth[:], aux[:, 0:2].rearrange("p a (b c) -> p (a b) c", b=4), ACT.Copy).then_inc(s["vt_hi"], 1)
                act.wait_ge(s["v_out"], 16 * n + 16)
                for i in range(8):
                    width = (i + 1) * 128
                    for m_ in range(2):
                        e = 16 * n + 2 * i + m_
                        act.wait_ge(s["nmax_ready"], e + 1)
                        if i and not m_:
                            act.wait_ge(s["wt_ps"], 8 * n + i)
                        src = aux[:, 2 * m_:2 * m_ + 2].rearrange("p a b -> p (a b)")[:, 0:width]
                        af(pp[:, m_ * 1024:m_ * 1024 + width], src, ACT.Exp, scale=SCALE,
                           bias=st[:, m_:m_ + 1], accum_out=st[:, 2 + m_:3 + m_]).then_inc(s["p_ready"], 1)
                    act.wait_ge(s["wt_ps"], 8 * n + i + 1)
                    if i:
                        act.wait_ge(s["pv_full"], 8 * n + i)
                    af(wth[:, 0:i + 1], jb[:, 0:2].rearrange("p a (b c) -> p (a b) c", b=4)[:, 0:i + 1],
                       ACT.Copy).then_inc(s["wt_hi"], 1)
                    act.wait_ge(s["pv_full"], 8 * n + i + 1)
                    af(raw[:, i * 128:(i + 1) * 128], jb[:, 2, 0:128], ACT.Copy).then_inc(s["o_ready"], 1)
                act.wait_ge(s["ssc_ready"], n + 1)
                act.dma_start(past[:], vgat[:, :, bass.ds(n * P, P)].rearrange("g t d -> t g d")).then_inc(s["pv_in"], 16)
                act.wait_ge(s["snm_ready"], n + 1)
                af(srow[0:16, 0:257], srow[0:16, 0:257], ACT.Exp, scale=SCALE, bias=st[0:16, 4:5],
                   accum_out=st[0:16, 5:6]).then_inc(s["sexp_ready"], 1)
                act.wait_ge(s["o_smp"], n + 2)
                act.wait_ge(s["k_out"], 16 * n + 16)
                af(rot[:], raw[:], ACT.Square).then_inc(s["osq_done"], 1)
                act.wait_ge(s["orms_full"], n + 1)
                af(rot[:].rearrange("p (c w) -> p c w", c=NCH), aux[:, 0:3, 0:CW], ACT.Sqrt, bias=eps[:]).then_inc(s["orms_sqrt"], 1)
                act.wait_ge(s["on_ready"], n + 1)
                af(yh[:, par % 2], raw[:], ACT.Copy).then_inc(s["y_hi"], 1)

            with act.Fori(0, ATT_ITERS) as i:
                at = Place(C_ATT, U_ATT, i, ATT_JOBS * 3, ATT_UNITS)
                for par in range(4):
                    head(at, 4 * i + par, par)
                    if par % 2:
                        for _ in range(8 * NCH):
                            at.chunk()

            layer_norm(2)
            mlp(1)
            layer_norm(3)
            act.wait_ge(s["k_out"], 16 * HEADS_B)
            act.wait_ge(s["v_out"], 16 * HEADS_B)

        @block.vector
        def _(dve):
            tt, ts, stt = nc.vector.tensor_tensor, nc.vector.tensor_scalar, nc.vector.scalar_tensor_tensor
            drain = dve.drain

            def f(ap):
                return ap.bitcast(F32)

            dve.sem_inc(s["y_lo"], 2)
            dve.sem_inc(s["o_smp"], 1)
            nc.vector.memset(eps[:], EPS)
            nc.vector.memset(pre[:, :, 0:4], 0.0)
            dve.wait_ge(s["x_in"], 16)
            for k in range(KD):
                dve.wait_ge(s["x_hi"], k + 1)
                tt(xl[:, k], acc[:, k], f(xh[:, k]), ALU.subtract).then_inc(s["x_ready"], 1)
                drain()
                ts(acc[:, k], acc[:, k], ALPHA, None, ALU.mult)
            dve.wait_ge(s["const_in"], 16 * N_CONST)
            ts(pall[:, :, 0:20], pall[:, :, 0:20], 0.5, None, ALU.mult)
            dve.wait_ge(s["dt_raw"], 1)
            stt(dtt[:], dtx[:, 0:T], -1.0, dtx[:, 0:T], ALU.mult, ALU.max).then_inc(s["dt_abs"], 1)
            ts(a32[:, 3:4], a32[:, 2:3], -1.0, None, ALU.mult)
            dve.wait_ge(s["dt_exp"], 1)
            stt(dtx[:, 0:T], dtx[:, 0:T], 0.0, dtt[:], ALU.max, ALU.add)
            drain()
            ts(dtt[:], dtx[:, 0:T], a32[:, 3:4], None, ALU.mult)
            ts(cs[:, T:T + NB], dtx[:, SEQ:T], 1.0, None, ALU.mult)
            drain()
            nc.vector.tensor_tensor_scan(cs[:, 0:T], scanm[:], dtt[:], 0.0, ALU.mult, ALU.add)
            drain().then_inc(s["dt_soft"], 1)
            dve.wait_ge(s["cs_hi"], 1)
            tt(csl[:], cs[:], f(csh[:]), ALU.subtract).then_inc(s["cs_lo"], 1)
            dve.wait_ge(s["cd_done"], 1)
            tt(tok[:, 2], aux[:, 1, 0:256].rearrange("p (c h) -> p c h", c=CHUNKS), tok[:, 0], ALU.subtract)
            drain().then_inc(s["dte_arg"], 1)
            dve.wait_ge(s["dte_exp"], 1)
            tt(tok[:, 2], tok[:, 2], tok[:, 1], ALU.mult).then_inc(s["tok_done"], 1)
            drain()

            def accumulate(at, tiles):
                for k in range(tiles):
                    for c in range(NCH):
                        bank, _, nth = at.chunk()
                        cols = slice(c * CW, (c + 1) * CW)
                        dve.wait_ge(chunk_full, nth)
                        tt(acc[:, k, cols], jb[:, bank, 0:CW], acc[:, k, cols], ALU.add).then_inc(bank_free[bank], 1)
                drain()

            def group(at, n):
                nc.vector.tensor_copy(pg[:], pall[:, bass.ds(n, 1)].rearrange("p a k -> p (a k)"))
                nc.vector.tensor_copy(tg[:], tok[:, :, :, bass.ds(n * R, R)])
                dve.wait_ge(s["h_out"], 16 * n + 16)
                nc.vector.memset(hst[:], 0.0)
                drain().then_inc(s["h_zero"], 1)
                dve.wait_ge(s["scv_in"], 16 * n + 16)
                dve.wait_ge(s["cs_stored"], 32)
                for t in range(4):
                    dve.wait_ge(s["pre_full"], 4 * n + t + 1)
                    src = pre[:, t % 2]
                    w = lambda k: pg[:, 4 * t + k:4 * t + k + 1]
                    ts(y[:, 0], src[:, 4:4 + T], w(3), pg[:, 16 + t:17 + t], ALU.mult, ALU.add)
                    for k in range(3):
                        drain()
                        stt(y[:, 0, 0:SEQ], src[:, 1 + k:1 + k + SEQ], w(k), y[:, 0, 0:SEQ], ALU.mult, ALU.add)
                        stt(y[:, 0, SEQ:T], scv[:, t, k], w(k), y[:, 0, SEQ:T], ALU.mult, ALU.add)
                    drain().then_inc(s["conv_done"], 1)
                    dve.wait_ge(s["tanh_done"], 4 * n + t + 1)
                    stt(xbc[:, t], src[:, 4:4 + T], 1.0, y[:, 0], ALU.add, ALU.mult)
                    drain().then_inc(s["xbc_done"], 1)
                for t in range(2):
                    dve.wait_ge(s["z_full"], 2 * n + t + 1)
                    stt(zs[:, t], pre[:, t, 4:4 + T], 1.0, zs[:, t], ALU.add, ALU.mult)
                drain().then_inc(s["z_done"], 1)
                hd = lambda ap: ap.unsqueeze(2).to_broadcast([P, R, HD])
                v4 = lambda ap: ap.rearrange("p (r q) -> p r q", r=R)
                for c in range(CHUNKS):
                    x = 8 * n + c
                    cols = slice(c * CHUNK, (c + 1) * CHUNK)
                    dve.wait_ge(s["ssd_in"], x + 1)
                    for r in range(R):
                        last = stt(dm[:, 0, r * 128:(r + 1) * 128], aux[:, 1, r * 128:(r + 1) * 128],
                                   tg[:, 0, c, r:r + 1], capm[:], ALU.subtract, ALU.min)
                    last.then_inc(s["d_ready"], 1)
                    tt(v4(xs[:]), v4(aux[:, 0, 0:256]), hd(tg[:, 1, c]), ALU.mult)
                    tt(v4(xe[:]), v4(aux[:, 0, 0:256]), hd(tg[:, 2, c]), ALU.mult)
                    dve.wait_ge(s["e_ready"], x + 1)
                    tt(v4(dm[:, 1]), v4(dm[:, 0]), aux[:, 0, 384:512].unsqueeze(1).to_broadcast([P, R, P]),
                       ALU.mult).then_inc(s["m_ready"], 1)
                    dve.wait_ge(s["ssd_off"], x + 1)
                    dve.wait_ge(s["e2_ready"], x + 1)
                    two = lambda ap: ap.rearrange("p (t l) -> p t l", t=2)
                    tt(y[:, :, cols], two(aux[:, 3, 0:256]), two(e2[:]), ALU.mult)
                    tt(v4(hst[:]), v4(hst[:]), hd(tg[:, 3, c]), ALU.mult)
                    drain()
                    dve.wait_ge(s["ssd_b"], x + 1)
                    tt(y[:, :, cols], two(aux[:, 1, 0:256]), y[:, :, cols], ALU.add)
                    tt(hst[:], aux[:, 1, 256:512], hst[:], ALU.add)
                    drain().then_inc(s["h_done"], 1)
                dve.wait_ge(s["dec_ready"], n + 1)
                tt(xdt[:], xbc[:, 0:2, SEQ:T], dts[:], ALU.mult)
                drain()
                dve.wait_ge(s["bb_full"], n + 1)
                dve.wait_ge(s["s_in"], 32 * n + 32)
                bn = lambda ap: ap.unsqueeze(2).to_broadcast([P, NB, P])
                v8 = lambda ap: ap.rearrange("p (b n) -> p b n", b=NB)
                t2 = dm[:].rearrange("p a b -> p (a b)")
                for t in range(2):
                    sv = v8(pre[:, t, 4:4 + SEQ])
                    tt(sv, sv, bn(dec[:, t]), ALU.mult)
                    tt(v8(t2), v8(aux[:, 2:4].rearrange("p a b -> p (a b)")), bn(xdt[:, t]), ALU.mult)
                    drain()
                    tt(sv, sv, v8(t2), ALU.add)
                    drain().then_inc(s["s_new"], 1)
                    dve.wait_ge(s["cb_full"], n + 1)
                    tt(v8(t2), v8(aux[:, 0:2].rearrange("p a b -> p (a b)")), sv, ALU.mult)
                    drain()
                    nc.vector.tensor_reduce(y[:, t, SEQ:T], v8(t2), AX.X, ALU.add)
                    drain()
                for t in range(2):
                    stt(y[:, t], xbc[:, t], pg[:, 20 + t:21 + t], y[:, t], ALU.mult, ALU.add)
                    drain()
                    tt(y[:, t], y[:, t], zs[:, t], ALU.mult)
                    drain().then_inc(s["yg_ready"], 1)
                dve.wait_ge(s["sq_done"], 2 * n + 2)
                tt(zs[:, 0], zs[:, 0], zs[:, 1], ALU.add)
                drain().then_inc(s["sq_sum"], 1)
                dve.wait_ge(s["rms_sqrt"], n + 1)
                nc.vector.reciprocal(zs[:, 1], zs[:, 1])
                drain()
                for t in range(2):
                    stt(y[:, t], y[:, t], pg[:, 22 + t:23 + t], zs[:, 1], ALU.mult, ALU.mult)
                    drain().then_inc(s["yn_ready"], 1)
                for t in range(2):
                    dve.wait_ge(s["y_hi"], 2 * n + t + 1)
                    tt(yl[:, t], y[:, t], f(yh[:, t]), ALU.subtract).then_inc(s["y_lo"], 1)
                accumulate(at, KD)

            with dve.Fori(0, MAMBA_ITERS) as i:
                at = Place(C_MAMBA, U_MAMBA, i, MAMBA_JOBS * 3, MAMBA_UNITS)
                for par in range(2):
                    for _ in range(6 * NCH):
                        at.chunk()
                    group(at, 2 * i + par)

            def layer_norm(l):
                tt(ln0[:], acc[:, 0], acc[:, 1], ALU.add)
                for k in range(2, KD):
                    drain()
                    tt(ln0[:], ln0[:], acc[:, k], ALU.add)
                drain().then_inc(s["ln_sum"], 1)
                dve.wait_ge(s["ln_mu"], l + 1)
                cv = lambda ap: ap.rearrange("p (c w) -> p c w", c=NCH)
                for k in range(KD):
                    tt(cv(acc[:, k]), cv(acc[:, k]), aux[:, 0:3, 0:CW], ALU.subtract).then_inc(s["ln_cent"], 1)
                for k in range(KD):
                    dve.wait_ge(s["ln_sq"], 8 * l + k + 1)
                    if k == 0:
                        nc.vector.tensor_copy(ln0[:], lnq[:, 0])
                    else:
                        tt(ln0[:], ln0[:], lnq[:, k % 2], ALU.add)
                    drain().then_inc(s["ln_add"], 1)
                dve.wait_ge(s["ln_std"], l + 1)
                nc.vector.reciprocal(lnq[:, 1], lnq[:, 0])
                drain()
                for k in range(KD):
                    tt(acc[:, k], acc[:, k], lnq[:, 1], ALU.mult).then_inc(s["ln_norm"], 1)
                if l < 3:
                    for k in range(KD):
                        dve.wait_ge(s["ln_hi"], 8 * l + k + 1)
                        tt(xl[:, k], acc[:, k], f(xh[:, k]), ALU.subtract)
                        drain().then_inc(s["ln_lo"], 1)
                        ts(acc[:, k], acc[:, k], ALPHA, None, ALU.mult)
                    drain()

            def mlp(layer):
                c0, u0 = ((C_MLP0, U_MLP0), (C_MLP1, U_MLP1))[layer]
                hb = layer * FFB

                def up(at, b, block_):
                    for j in range(4):
                        for c in range(NCH):
                            at.chunk()
                            e = block_ * 12 + j * 3 + c
                            cols = slice(c * CW, (c + 1) * CW)
                            slot = (j * 3 + c) % 4
                            dve.wait_ge(s["h_sq"], e + 1)
                            tt(rl[:, slot], rl[:, slot], rl[:, slot], ALU.mult)
                            drain()
                            tt(hl[b][:, j, cols], rl[:, slot], f(hh[b][:, j, cols]), ALU.subtract).then_inc(s["h_ready"], 1)

                def down(at):
                    accumulate(at, KD)
                    drain().then_inc(s["relu_done"], 1)

                up(Place(c0, u0), 0, hb)
                with dve.Fori(0, FFB // 2 - 1) as i:
                    at = Place(c0 + 12, u0 + 4, i, 72, 16)
                    up(at, 1, hb + 2 * i + 1)
                    down(at)
                    up(at, 0, hb + 2 * i + 2)
                    down(at)
                at = Place(c0 + 12 + 72 * (FFB // 2 - 1), u0 + 4 + 16 * (FFB // 2 - 1))
                up(at, 1, hb + FFB - 1)
                down(at)
                down(at)

            layer_norm(0)
            mlp(0)
            layer_norm(1)

            dve.wait_ge(s["attc_in"], 16 * N_ATTC)
            tt(lamv[:, 0:2], lamv[:, 0:2], lamv[:, 2:4], ALU.mult)
            drain()
            nc.vector.tensor_reduce(lam[:, 0:2], lamv[:, 0:2], AX.X, ALU.add)
            ts(subg[:], subg[:], 1.0 - LAM_INIT, None, ALU.mult)
            drain().then_inc(s["lam_sum"], 1)
            dve.wait_ge(s["lam_exp"], 1)
            tt(lam[:, 2:3], lam[:, 1:2], lam[:, 0:1], ALU.subtract)
            drain()
            ts(lam[:, 2:3], lam[:, 2:3], LAM_INIT, None, ALU.subtract)
            drain()
            stt(pair[:, 10:11], pair[:, 9:10], lam[0:16, 2:3], pair[:, 8:9], ALU.mult, ALU.add)
            drain()

            def head(at, n, par):
                for j in range(2):
                    at.chunk(), at.chunk(), at.chunk()
                    dve.wait_ge(s["raw_full"], 2 * n + j + 1)
                    if j:
                        dve.wait_ge(s["qk_hi"], 2 * n + 1)
                    tt(rot[:], raw[:], cos[:], ALU.mult)
                    drain()
                    dve.wait_ge(s["perm_full"], 2 * n + j + 1)
                    cv = lambda ap: ap.rearrange("p (c w) -> p c w", c=NCH)
                    tt(cv(raw[:]), aux[:, 0:3, 0:CW], cv(sin[:]), ALU.mult)
                    drain()
                    tt(rot[:], rot[:], raw[:], ALU.add)
                    drain().then_inc(s["rope_done"], 1)
                    nc.vector.tensor_copy(smp[:, j], rot[:, SEQ:T])
                    dve.wait_ge(s["qk_hi"], 2 * n + j + 1)
                    tt((ql, kl)[j][:], rot[:], f((qh, kh)[j][:]), ALU.subtract)
                    drain()
                at.chunk(), at.chunk(), at.chunk()
                dve.wait_ge(s["raw_v"], n + 1)
                nc.vector.tensor_copy(smp[:, 2], raw[:, SEQ:T])
                dve.wait_ge(s["vt_hi"], n + 1)
                tt(vtl[:], aux[:, 0:2].rearrange("p a (b c) -> p (a b) c", b=4), f(vth[:]), ALU.subtract)
                drain().then_inc(s["vt_ready"], 1)
                for i in range(8):
                    width = (i + 1) * 128
                    for m_ in range(2):
                        e = 16 * n + 2 * i + m_
                        dve.wait_ge(s["s_full"], e + 1)
                        src = aux[:, 2 * m_:2 * m_ + 2].rearrange("p a b -> p (a b)")[:, 0:width]
                        nc.vector.tensor_reduce(st[:, 6 + m_:7 + m_], src, AX.X, ALU.max)
                        drain()
                        ts(st[:, m_:m_ + 1], st[:, 6 + m_:7 + m_], -SCALE, None, ALU.mult).then_inc(s["nmax_ready"], 1)
                    dve.wait_ge(s["p_ready"], 16 * n + 2 * i + 2)
                    nc.vector.reciprocal(st[:, 2:4], st[:, 2:4])
                    drain()
                    ts(pp[:, 1024:1024 + width], pp[:, 1024:1024 + width], st[:, 3:4], lam[:, 2:3], ALU.mult, ALU.mult)
                    drain()
                    stt(pp[:, 0:width], pp[:, 0:width], st[:, 2:3], pp[:, 1024:1024 + width], ALU.mult, ALU.add)
                    drain().then_inc(s["w_ready"], 1)
                    dve.wait_ge(s["wt_hi"], 8 * n + i + 1)
                    tt(wtl[:, 0:i + 1], jb[:, 0:2].rearrange("p a (b c) -> p (a b) c", b=4)[:, 0:i + 1],
                       f(wth[:, 0:i + 1]), ALU.subtract)
                    drain().then_inc(s["wt_ready"], 1)
                dve.wait_ge(s["qb_full"], n + 1)
                dve.wait_ge(s["pk_in"], 16 * n + 16)
                dve.wait_ge(s["wt_ps"], 8 * n + 8)
                for g in range(PAGES):
                    tt(pp[:].rearrange("p (b g d) -> p g b d", b=NB, g=PAGES)[:, g],
                       past[:].rearrange("p (b g) d -> p g b d", g=PAGES)[:, g],
                       aux[:, 0:2].rearrange("p a (b d) -> p (a b) d", b=4), ALU.mult)
                tt(qkn[:, 0], smp[:, 0], smp[:, 1], ALU.mult)
                drain()
                for g in range(PAGES):
                    for m_ in range(2):
                        v = pp[:].rearrange("p (b g m d) -> p g m b d", b=NB, g=PAGES, m=2)[:, g, m_]
                        nc.vector.tensor_reduce(ssc[:, g, m_], v, AX.X, ALU.add)
                tt(qkn[:, 1], qkn[:, 0], half[:, 1], ALU.mult)
                drain()
                tt(qkn[:, 0], qkn[:, 0], half[:, 0], ALU.mult)
                drain().then_inc(s["qkn_ready"], 1)
                drain().then_inc(s["ssc_ready"], 1)
                dve.wait_ge(s["srow_full"], n + 1)
                nc.vector.tensor_copy(srow[:, 0:257], aux[0:16, 2, 0:257])
                drain()
                nc.vector.tensor_reduce(st[0:16, 6:7], srow[:, 0:257], AX.X, ALU.max)
                drain()
                ts(st[0:16, 4:5], st[0:16, 6:7], -SCALE, None, ALU.mult)
                drain().then_inc(s["snm_ready"], 1)
                dve.wait_ge(s["sexp_ready"], n + 1)
                nc.vector.reciprocal(st[0:16, 5:6], st[0:16, 5:6])
                drain()
                ts(srow[:, 0:257], srow[:, 0:257], st[0:16, 5:6], pair[:, 10:11], ALU.mult, ALU.mult)
                drain().then_inc(s["sp_ready"], 1)
                dve.wait_ge(s["wsm_full"], n + 1)
                nc.vector.tensor_copy(wsm[:].rearrange("p k b -> p (k b)"), aux[:, 3, 0:24])
                drain().then_inc(s["wsm_ready"], 1)
                tt(smp[:, 2], smp[:, 2], wsm[:, 2], ALU.mult)
                drain()
                dve.wait_ge(s["so_full"], n + 1)
                dve.wait_ge(s["o_ready"], 8 * n + 8)
                tt(raw[:, SEQ:T], aux[:, 3, 32:40], smp[:, 2], ALU.add)
                drain().then_inc(s["o_smp"], 1)
                dve.wait_ge(s["orms_sqrt"], n + 1)
                nc.vector.reciprocal(rot[:], rot[:])
                drain()
                stt(raw[:], raw[:], subg[:, 0:1], rot[:], ALU.mult, ALU.mult)
                drain().then_inc(s["on_ready"], 1)
                dve.wait_ge(s["y_hi"], 2 * GROUPS + n + 1)
                tt(yl[:, par % 2], raw[:], f(yh[:, par % 2]), ALU.subtract)
                drain().then_inc(s["y_lo"], 1)

            with dve.Fori(0, ATT_ITERS) as i:
                at = Place(C_ATT, U_ATT, i, ATT_JOBS * 3, ATT_UNITS)
                for par in range(4):
                    head(at, 4 * i + par, par)
                    if par % 2:
                        accumulate(at, KD)

            layer_norm(2)
            mlp(1)
            layer_norm(3)


_OUT_SHAPES = {
    "yT": (P, KD, T), "kT": (P, HEADS_B, T), "vT": (P, HEADS_B, T), "conv_new": (P, GROUPS, 4, 11),
    "conv_old": (NB, CONV_W - 2, CONV_DIM), "ssm_p": (P, GROUPS, 256), "ssm_s": (P, 2 * GROUPS, NB, P),
}


def _tiles(w):
    k, m = w.shape
    return w.reshape(k // P, P, m // P, P).transpose(2, 1, 0, 3)


def _stream(w_in, w_out, w_up, w_down, w_kv, w_q, w_o):
    units = np.zeros((UNITS, P, 8, P), np.float32)
    at = [0]

    def put(block):
        units[at[0]:at[0] + len(block)] = block
        at[0] += len(block)

    def rows(w, k0, kt):
        t = _tiles(w[k0 * P:(k0 + kt) * P])
        m = t.shape[0]
        put(t.reshape(m * kt // 8, 8 // kt, P, kt, P).transpose(0, 2, 1, 3, 4).reshape(-1, P, 8, P))

    dt = np.zeros((D, P), np.float32)
    dt[:, :HEADS_A] = w_in[:, D_INNER + CONV_DIM:]
    put(_tiles(dt))
    t_in = _tiles(w_in[:, :D_INNER + CONV_DIM])
    z, x, b, c = t_in[:16], t_in[16:32], t_in[32:40], t_in[40:48]
    for g in range(GROUPS):
        put(np.stack([x[2 * g], x[2 * g + 1], b[g], c[g], z[2 * g], z[2 * g + 1]]))
        rows(w_out, 2 * g, 2)

    def mlp(layer):
        up = _tiles(w_up[layer])
        put(up[0:4])
        for b_ in range(1, FFB):
            put(up[4 * b_:4 * b_ + 4])
            rows(w_down[layer], 4 * (b_ - 1), 4)
        rows(w_down[layer], 4 * (FFB - 1), 4)

    mlp(0)
    q, kv = _tiles(w_q), _tiles(w_kv)
    for h in range(HEADS_B):
        put(np.stack([q[h], kv[h], kv[HEADS_B + h]]))
        if h % 2:
            rows(w_o, h - 1, 2)
    mlp(1)
    assert at[0] == UNITS
    return units


def _layout(v):
    f = lambda n: np.asarray(v[n], np.float32) if np.asarray(v[n]).dtype == np.float32 else np.asarray(v[n])
    d = {}
    d["wstream"] = _stream(f("w_in_a")[0], f("w_out_a")[0], f("w_up"), f("w_down"), f("w_kv"), f("w_q_b")[0], f("w_o_b")[0])
    x = np.concatenate([f("x_prompt")[0], f("x_sample")[:, 0]])
    d["xT"] = x.T.reshape(KD, P, T).transpose(1, 0, 2)

    def by_tile(w):
        t = w.reshape(*w.shape[:-1], CONV_DIM // P, P)
        order = [[2 * g, 2 * g + 1, 16 + g, 24 + g] for g in range(GROUPS)]
        t = t[..., np.array(order), :]
        return np.moveaxis(t, (-1, -3, -2), (0, 1, 2))

    par = np.zeros((P, GROUPS, 24), np.float32)
    par[:, :, 0:16] = by_tile(f("conv_w_a")[0]).reshape(P, GROUPS, 16)
    par[:, :, 16:20] = by_tile(f("conv_b_a")[0])
    par[:, :, 20:22] = np.repeat(f("d_skip_a")[0].reshape(GROUPS, 2, 2), 64, axis=2).transpose(2, 0, 1)
    par[:, :, 22:24] = f("norm_a")[0].reshape(GROUPS, 2, P).transpose(2, 0, 1)
    d["par"] = par
    d["sconv"] = by_tile(f("state_conv")[0]).transpose(0, 1, 2, 4, 3)
    d["conv_keep"] = f("state_conv")[0][:, 1:]
    d["state"] = f("state_ssm")[0].reshape(NB, 2 * GROUPS, P, P).transpose(2, 1, 0, 3)
    a32 = np.zeros((HEADS_A, 4), np.float32)
    a32[:, 0] = f("dt_bias_a")[0]
    a32[:, 1] = f("a_log_a")[0]
    d["a32"] = a32
    lnp = np.stack([f("ln_g").reshape(4, D), f("ln_b").reshape(4, D)], 1)
    d["lnp"] = lnp.reshape(4, 2, KD, P).transpose(3, 0, 1, 2)
    d["lamv"] = np.stack([f("lambda_q1_b")[0], f("lambda_q2_b")[0], f("lambda_k1_b")[0], f("lambda_k2_b")[0]])
    d["subg"] = f("subln_b")[0].reshape(P, 1)
    d["cache_k"] = f("cache_k").reshape(PHYS, P, D)
    d["cache_v"] = f("cache_v").reshape(PHYS, P, D)
    d["ptab"] = f("page_table").reshape(1, NB * PAGES).astype(np.int32)

    eye = np.eye(P, dtype=np.float32)
    d["ident"] = eye
    ones = np.zeros((P, 3, P), np.float32)
    ones[:, 0], ones[:, 1], ones[:, 2] = 1 / D, 1 / 256, 1 / P
    d["ones"] = ones
    d["row127"] = np.zeros((P, P), np.float32)
    d["row127"][P - 1] = 1
    i = np.arange(P)
    d["capm"] = np.where(i[None, :] >= i[:, None], 0, -1e30).astype(np.float32)
    scanm = np.ones((HEADS_A, T), np.float32)
    scanm[:, 0:SEQ:CHUNK] = 0
    scanm[:, SEQ:] = 0
    d["scanm"] = scanm
    sel = np.zeros((8, 6, P), np.float32)
    for r in range(R):
        sel[[r, R + r], r] = 1
        sel[[r, R + r], 4 + r // 2, 64 * (r % 2):64 * (r % 2) + 64] = 1
    d["sel"] = sel.reshape(8, 768)
    half = HD // 2
    inv = (np.float32(10000.0) ** (-np.arange(half, dtype=np.float32) / half)).astype(np.float32)
    pos = np.concatenate([np.arange(SEQ), np.full(NB, PAST)]).astype(np.float32)
    ang = inv[:, None] * pos[None, :]
    d["cos"] = np.tile(np.cos(ang).astype(np.float32), (4, 1))
    d["sin"] = np.tile(np.sin(ang).astype(np.float32), (4, 1))
    perm = np.zeros((P, P), np.float32)
    for m_ in range(P):
        if m_ % HD < half:
            perm[m_ + half, m_] = -1
        else:
            perm[m_ - half, m_] = 1
    d["perm"] = perm
    mbf = np.zeros((P, 2, P), mybir.dt.np(BF16))
    mbf[:, 0] = eye
    mbf[:, 1] = np.where(i[None, :] <= i[:, None], 0, -1e30)
    d["mbf"] = mbf
    hf = np.zeros((P, 2, NB), np.float32)
    hf[0:64, 0] = P
    hf[64:128, 1] = P
    d["half"] = hf
    pair = np.zeros((16, 12), np.float32)
    for r in range(16):
        pair[r, r % 8] = 1
        pair[r, 8 + r // 8] = 1
    d["pair"] = pair
    return {k: np.ascontiguousarray(w) for k, w in d.items()}


def kernel(**inputs):
    import concourse.bacc as _bacc
    from concourse.bass_utils import run_bass_kernel_spmd as _run

    nc = _bacc.Bacc("TRN2", target_bir_lowering=False, num_devices=1)
    arrays = {f"in_{k}": w for k, w in _layout(inputs).items()}
    a = {k[3:]: nc.dram_tensor(k, w.shape, mybir.dt.from_np(w.dtype), kind="ExternalInput").ap() for k, w in arrays.items()}
    o = {k: nc.dram_tensor(f"out_{k}", shape, F32, kind="ExternalOutput").ap() for k, shape in _OUT_SHAPES.items()}
    program(nc, a, o)
    r = _run(nc, [arrays], core_ids=[0]).results[0]
    g = {k: np.asarray(r[f"out_{k}"]) for k in _OUT_SHAPES}

    def tokens(t):
        return t.transpose(2, 1, 0).reshape(T, D)

    yt, kt, vt = tokens(g["yT"]), tokens(g["kT"]), tokens(g["vT"])
    new = np.zeros((CONV_DIM // P, P, 11), np.float32)
    for gr in range(GROUPS):
        for j, tile in enumerate((2 * gr, 2 * gr + 1, 16 + gr, 24 + gr)):
            new[tile] = g["conv_new"][:, gr, j]
    new = new.reshape(CONV_DIM, 11)
    conv_p = new[:, 0:3].T.reshape(1, 1, 3, CONV_DIM)
    conv_s = np.concatenate([g["conv_old"], new[:, 3:].T[:, None]], 1)[None]
    ssm_p = g["ssm_p"].reshape(P, HEADS_A, HD).transpose(1, 2, 0)[None, None]
    ssm_s = g["ssm_s"].reshape(2, HD, 16, NB, P).transpose(3, 2, 0, 1, 4).reshape(1, NB, HEADS_A, HD, P)
    c = np.ascontiguousarray
    return (c(yt[:SEQ][None]), c(yt[SEQ:][:, None]), c(conv_p), c(ssm_p),
            c(kt[:SEQ].reshape(1, SEQ, HEADS_B, 2, HD)), c(vt[:SEQ].reshape(1, SEQ, HEADS_B, 2 * HD)),
            c(conv_s), c(ssm_s),
            c(kt[SEQ:].reshape(NB, 1, HEADS_B, 2, HD)), c(vt[SEQ:].reshape(NB, 1, HEADS_B, 2 * HD)))
```

```python
import math
from contextlib import ExitStack

import numpy as np

import concourse.bass as bass
from concourse import mybir

F32 = mybir.dt.float32
F32R = mybir.dt.float32r
BF16 = mybir.dt.bfloat16
I32 = mybir.dt.int32
ALU = mybir.AluOpType
ACT = mybir.ActivationFunctionType
AX = mybir.AxisListType

P = 128
D = 1024
SEQ = 1024
NB = 8
T = SEQ + NB
NCH = 3
CW = T // NCH
KD = D // P
D_INNER = 2048
GN = 1024
HEADS_A = 32
GROUPS = 8
R = HEADS_A // GROUPS
CHUNK = 128
CHUNKS = SEQ // CHUNK
CONV_DIM = D_INNER + 2 * GN
CONV_W = 4
HEADS_B = 8
HD = 64
D_FF = 4096
PAST = 256
PAGES = PAST // P
PHYS = NB * PAGES * 5 // 4
ALPHA = 4.0 ** 0.25
EPS = 1e-5
LAM_INIT = 0.8 - 0.6 * math.exp(-0.3)
SCALE = HD ** -0.5
FFB = D_FF // 512

MIX_HEAD_JOBS, MIX_HEAD_UNITS = 6, 6
MIX_JOBS, MIX_UNITS = 4 + 8 + 2, 4 + 2 + 2
ATT_JOBS, ATT_UNITS = 3 + 8, 3 + 1
MLP_JOBS, MLP_UNITS = FFB * 12, FFB * 8
J_MIX, U_MIX = 1, 1
J_MLP0, U_MLP0 = J_MIX + GROUPS * MIX_JOBS, U_MIX + GROUPS * MIX_UNITS
J_ATT, U_ATT = J_MLP0 + MLP_JOBS, U_MLP0 + MLP_UNITS
J_MLP1, U_MLP1 = J_ATT + HEADS_B * ATT_JOBS, U_ATT + HEADS_B * ATT_UNITS
UNITS = U_MLP1 + MLP_UNITS
Z_FILL = {3: ((0, 0),), 4: ((0, 1), (0, 2)), 5: ((1, 0),), 6: ((1, 1),), 7: ((1, 2),)}
S_STEP = 2
N_CONST = 9
N_ATTC = 8
N_OUTS = 1 + KD


class Place:

    def __init__(self, job0, unit0, i=0, jobs=0, units=0):
        assert units % 2 == 0
        self.j, self.u = job0, unit0
        self.i, self.dj, self.du = i, jobs, units

    def job(self, n=1):
        j = self.i * self.dj + self.j
        self.j += n
        return j + 1, 3 * j

    def unit(self):
        u = self.u
        self.u += 1
        return u % 2, self.i * self.du + u + 1


def program(nc, a, o):
    with ExitStack() as ctx:
        def sb(name, shape, dt=F32, into=None):
            return (into or ctx).enter_context(nc.sbuf_tensor(name, shape, dt))

        def sem(name):
            return ctx.enter_context(nc.semaphore(name))

        xh = sb("xh", [P, KD, T], F32R)
        xl = sb("xl", [P, KD, T], F32R)
        acc = sb("acc", [P, KD, T])
        wraw = sb("wraw", [P, 2, 8, P])
        wh0 = sb("wh0", [P, 8, P], F32R)
        wh1 = sb("wh1", [P, 8, P], F32R)
        wl0 = sb("wl0", [P, 8, P], F32R)
        wl1 = sb("wl1", [P, 8, P], F32R)
        wh, wl = [wh0, wh1], [wl0, wl1]
        ident = sb("ident", [P, P])
        ones = sb("ones", [P, 3, P])
        lnp = sb("lnp", [P, 4, 2, KD])
        eps = sb("eps", [P, 1])
        one = sb("one", [P, 1])
        m = ctx.enter_context(ExitStack())
        yh = sb("yh", [P, 2, T], F32R, m)
        yl = sb("yl", [P, 2, T], F32R, m)
        xbc = sb("xbc", [P, 4, T], F32, m)
        zs = sb("zs", [P, 2, T], F32, m)
        y = sb("y", [P, 2, T], F32, m)
        pre = sb("pre", [P, 2, 4 + T], F32, m)
        csg = sb("csg", [8, T + NB], F32R, m)
        dm = sb("dm", [P, 2, 512], F32, m)
        bt = sb("bt", [P, P], F32, m)
        xs = sb("xs", [P, 256], F32, m)
        xe = sb("xe", [P, 256], F32, m)
        e2 = sb("e2", [P, 256], F32, m)
        tok = sb("tok", [P, 4, CHUNKS, HEADS_A], F32, m)
        tg = sb("tg", [P, 4, CHUNKS, R], F32, m)
        hst = sb("hst", [P, 256], F32, m)
        selh = sb("selh", [8, R, P], F32R, m)
        selt = sb("selt", [8, 2, P], F32R, m)
        capm = sb("capm", [P, P], F32, m)
        scv = sb("scv", [P, 4, 3, NB], F32, m)
        pall = sb("pall", [P, GROUPS, 24], F32, m)
        pg = sb("pg", [P, 24], F32, m)
        cnew = sb("cnew", [P, 4, 11], F32, m)
        dec = sb("dec", [P, 2, 8], F32, m)
        dts = sb("dts", [P, 2, 8], F32, m)
        xdt = sb("xdt", [P, 2, 8], F32, m)
        a32 = sb("a32", [HEADS_A, 4], F32, m)
        ct = sb("ct", [P, T], F32, m)
        st2 = sb("st2", [P, 512], F32, m)
        gn = sb("gn", [P, 2], F32, m)
        m.close()
        m = ctx.enter_context(ExitStack())
        dtx = sb("dtx", [HEADS_A, T + NB], F32, m)
        dtt = sb("dtt", [HEADS_A, T], F32, m)
        scanm = sb("scanm", [HEADS_A, T], F32, m)
        cs = sb("cs", [HEADS_A, T + NB], F32, m)
        csh = sb("csh", [HEADS_A, T + NB], F32R, m)
        csl = sb("csl", [HEADS_A, T + NB], F32R, m)
        row127 = sb("row127", [P, P], F32, m)
        m.close()
        m = ctx.enter_context(ExitStack())
        ah = sb("ah", [P, 1, T], F32R, m)
        al = sb("al", [P, 1, T], F32R, m)
        ob = sb("ob", [P, T], F32, m)
        qh = sb("qh", [P, T], F32R, m)
        ql = sb("ql", [P, T], F32R, m)
        kh = sb("kh", [P, T], F32R, m)
        kl = sb("kl", [P, T], F32R, m)
        raw = sb("raw", [P, T], F32, m)
        rot = sb("rot", [P, T], F32, m)
        cos = sb("cos", [P, T], F32, m)
        sin = sb("sin", [P, T], F32, m)
        pp = sb("pp", [P, 2048], F32, m)
        wth = sb("wth", [P, KD, P], F32R, m)
        wtl = sb("wtl", [P, KD, P], F32R, m)
        vth = sb("vth", [P, KD, P], F32R, m)
        vtl = sb("vtl", [P, KD, P], F32R, m)
        past = sb("past", [P, NB * PAGES, P], F32, m)
        perm = sb("perm", [P, P], F32, m)
        mbf = sb("mbf", [P, 2, P], BF16, m)
        lamv = sb("lamv", [P, 4, HD], F32, m)
        lam = sb("lam", [P, 4], F32, m)
        subg = sb("subg", [P, 1], F32, m)
        half = sb("half", [P, 2, NB], F32, m)
        pair = sb("pair", [16, 12], F32, m)
        smp = sb("smp", [P, 3, NB], F32, m)
        qkn = sb("qkn", [P, 2, NB], F32, m)
        st = sb("st", [P, 8], F32, m)
        srow = sb("srow", [16, 264], F32, m)
        ssc = sb("ssc", [P, PAGES, 2, NB], F32, m)
        wsm = sb("wsm", [P, 3, NB], F32, m)
        m.close()
        m = ctx.enter_context(ExitStack())
        hh = [sb(f"hh{b}", [P, 4, T], F32R, m) for b in range(2)]
        hl = [sb(f"hl{b}", [P, 4, T], F32R, m) for b in range(2)]
        rl = sb("rl", [P, 4, CW], F32, m)
        m.close()
        m = ctx.enter_context(ExitStack())
        ln0 = sb("ln0", [P, T], F32, m)
        lnq = sb("lnq", [P, 2, T], F32, m)
        m.close()

        jb = ctx.enter_context(nc.psum_tensor("jb", [P, NCH, 512], F32))
        aux = ctx.enter_context(nc.psum_tensor("aux", [P, 5, 512], F32))

        csd = nc.dram_tensor("csd", [2, HEADS_A, T + NB], F32, kind="Internal").ap()
        kgat = nc.dram_tensor("kgat", [NB * PAGES, P, D], F32, kind="Internal").ap()
        vgat = nc.dram_tensor("vgat", [NB * PAGES, P, D], F32, kind="Internal").ap()

        raw_in = [sem("raw_in0"), sem("raw_in1")]
        w_split = sem("w_split")
        unit_begun = sem("unit_begun")
        chunk_full = sem("chunk_full")
        bank_free = [sem(f"bank_free{c}") for c in range(NCH)]
        names = """const_in attc_in x_in x_hi x_ready outs ptab_in gathered
            dt_raw dt_abs dt_exp dt_soft a_neg cs_hi cs_lo cs_stored tok_ps tok_cp end_ps cd_done dte_arg dte_exp tok_done
            sel_done par_half csg_in scv_in cnew_full cnew_out pre_full conv_done tanh_done xbc_done z_full z_done bc_full bc_used a_hi a_lo
            h_zero ssd_in ssd_off ssd_b bt_ready e2_ready d_ready e_ready m_ready h_done h_out
            s_in bcs_full dec_ready bb_full cb_full s_new s_out
            yg_ready sq_done sq_sum rms_full rms_sqrt yn_ready y_hi y_lo
            relu_done h_sq h_ready
            ln_sum ln_mu ln_cent ln_sq ln_add ln_var ln_std ln_norm ln_aff ln_hi ln_lo
            lam_sum lam_exp lam_done raw_full perm_full rope_done qk_hi qk_lo k_out raw_v vt_ps vt_hi vt_ready v_out
            s_full nmax_ready p_ready w_ready wt_ps wt_hi wt_ready pv_full o_ready
            qb_full pk_in ssc_ready qkn_ready srow_full snm_ready sexp_ready sp_ready wsm_full wsm_ready pv_in so_full o_smp
            osq_done orms_full orms_sqrt on_ready""".split()
        s = {n: sem(n) for n in names}

        block = ctx.enter_context(nc.Block())

        @block.sync
        def _(sp):
            for u in range(2):
                sp.dma_start(wraw[:, u], a["wstream"][u]).then_inc(raw_in[u], 16)
            sp.dma_start(acc[:], a["xT"]).then_inc(s["x_in"], 16)
            for dst, name in ((ident, "ident"), (ones, "ones"), (lnp, "lnp"), (row127, "row127"),
                              (capm, "capm"), (pall, "par"), (a32, "a32"), (scanm, "scanm")):
                sp.dma_start(dst[:], a[name]).then_inc(s["const_in"], 16)
            sp.dma_start(pre[0:8, 0, 4:772], a["sel"]).then_inc(s["const_in"], 16)
            with sp.Fori(0, (UNITS - 3) // 2) as i:
                for k in range(2):
                    sp.wait_ge(w_split, 2 * i + k + 1)
                    sp.dma_start(wraw[:, k], a["wstream"][2 * i + (k + 2)]).then_inc(raw_in[k], 16)
            sp.wait_ge(w_split, UNITS - 2)
            sp.dma_start(wraw[:, 0], a["wstream"][UNITS - 1]).then_inc(raw_in[0], 16)
            sp.wait_ge(s["outs"], 16 * N_OUTS)

        @block.gpsimd
        def _(pool):
            def split(slot, loaded, begun):
                pool.wait_ge(raw_in[slot], loaded)
                if begun is not None:
                    pool.wait_ge(unit_begun, begun)
                nc.gpsimd.tensor_tensor(wh[slot][:].rearrange("p k m -> p (k m)"), wraw[:, slot].rearrange("p k m -> p (k m)"),
                                        one[:].to_broadcast([P, 8 * P]), ALU.mult)
                pool.drain()
                nc.gpsimd.tensor_tensor(wl[slot][:], wraw[:, slot], wh[slot][:].bitcast(F32),
                                        ALU.subtract).then_inc(w_split, 1)

            nc.gpsimd.memset(one[:], 1.0)
            pool.drain()
            split(0, 16, None)
            split(1, 16, None)
            with pool.Fori(1, (UNITS - 1) // 2) as i:
                split(0, 16 * i + 16, 2 * i)
                split(1, 16 * i + 16, 2 * i + 1)
            split(0, 16 * ((UNITS - 1) // 2) + 16, UNITS - 1)

        @block.tensor
        def _(pe):
            mm = nc.tensor.matmul

            def chunk_of(place, c, j, kt, rh, rlo):
                slot, credits, _ = place
                pe.wait_ge(bank_free[c], credits)
                cols = slice(c * CW, (c + 1) * CW)
                for k in range(kt):
                    for w, x, p in ((wh, rh, 0), (wh, rlo, 1), (wl, rh, 2)):
                        last = mm(jb[:, c, 0:CW], w[slot][:, j * kt + k], x[:, k, cols],
                                  start=(k == 0 and p == 0), stop=(k == kt - 1 and p == 2))
                        if c == 0 and j == 0 and k == 0 and p == 0:
                            last.then_inc(unit_begun, 1)
                last.then_inc(chunk_full, 1)

            def unit(at):
                slot, nth = at.unit()
                pe.wait_ge(w_split, nth)
                return slot

            def jobs(at, n, kt, rh, rlo):
                for j in range(n):
                    if (j * kt) % 8 == 0:
                        slot = unit(at)
                    credits, done = at.job()
                    for c in range(NCH):
                        chunk_of((slot, credits, done), c, j % (8 // kt), kt, rh, rlo)

            pe.wait_ge(s["x_ready"], KD)
            pe.wait_ge(s["const_in"], 16 * N_CONST)
            pe.wait_ge(s["sel_done"], 1)
            at = Place(0, 0)
            jobs(at, 1, KD, xh, xl)
            pe.wait_ge(s["cs_hi"], 1)
            for k, src in enumerate((cs, dtx)):
                for c in range(CHUNKS):
                    last = nc.tensor.transpose(aux[:, 0, (k * CHUNKS + c) * HEADS_A:(k * CHUNKS + c + 1) * HEADS_A],
                                               src[:, c * CHUNK:(c + 1) * CHUNK], ident[0:HEADS_A, 0:HEADS_A])
            last.then_inc(s["tok_ps"], 1)
            pe.wait_ge(s["tok_cp"], 1)
            mm(aux[:, 1, 0:256], row127[:], tok[:, 0].rearrange("p c h -> p (c h)"), start=True,
               stop=True).then_inc(s["end_ps"], 1)

            def rms(p, full, summed, src, k):
                pe.wait_ge(s[summed], p + 1)
                for c in range(NCH):
                    last = mm(aux[:, c, 0:CW], ones[:, k], src[:, c * CW:(c + 1) * CW], start=True, stop=True)
                last.then_inc(s[full], 1)

            def project_group(at, n, fin):
                jobs(at, 1, KD, xh, xl)
                if fin:
                    rms(n - 1, "rms_full", "sq_sum", zs[:, 0], 1)
                jobs(at, 3, KD, xh, xl)

            def scan_group(at, n, out):
                if out:
                    pe.wait_ge(s["y_lo"], 2 * n)
                    slot = unit(at)
                outs = []

                def out_jobs(first):
                    for j in (first, first + 1):
                        if j == 4:
                            outs.append(unit(at))
                        sl = outs[0] if outs else slot
                        credits, done = at.job()
                        for c in range(NCH):
                            chunk_of((sl, credits, done), c, j % 4, 2, yh, yl)

                if out:
                    out_jobs(0)
                pe.wait_ge(s["xbc_done"], 4 * n + 4)
                pe.wait_ge(s["csg_in"], 32 * n + 32)
                for c in range(CHUNKS):
                    cols = slice(c * CHUNK, (c + 1) * CHUNK)
                    nc.tensor.transpose(aux[:, 0, 0:128], xbc[:, 0, cols], ident[:])
                    nc.tensor.transpose(aux[:, 0, 128:256], xbc[:, 1, cols], ident[:])
                    mm(aux[:, 0, 384:512], xbc[:, 2, cols], xbc[:, 3, cols], start=True, stop=True)
                    for r in range(R):
                        mm(aux[:, 1, r * 128:(r + 1) * 128], selh[:, r], csg[:, cols], start=True, stop=True)
                    for t in range(2):
                        mm(aux[:, 2, t * 128:128 + t * 128], selt[:, t], csg[:, cols], start=True, stop=True)
                    nc.tensor.transpose(aux[:, 2, 256:384], xbc[:, 2, cols], ident[:]).then_inc(s["ssd_in"], 1)
                    if c:
                        pe.wait_ge(s["h_done"], 8 * n + c)
                    else:
                        pe.wait_ge(s["h_zero"], n + 1)
                    for t in range(2):
                        last = mm(aux[:, 3, t * 128:128 + t * 128], hst[:, t * 128:(t + 1) * 128],
                                  xbc[:, 3, cols], start=True, stop=True)
                    last.then_inc(s["ssd_off"], 1)
                    if out and c < 3:
                        out_jobs(2 + 2 * c)
                    for t, zc in Z_FILL.get(c, ()):
                        if zc == 0:
                            zp = (unit(at), *at.job())
                        chunk_of(zp, zc, 0, KD, xh, xl)
                    pe.wait_ge(s["m_ready"], 8 * n + c + 1)
                    for r in range(R):
                        half_ = slice(64 * (r % 2), 64 * (r % 2) + 64)
                        mm(aux[half_, 3, (r // 2) * 128:(r // 2) * 128 + 128], xs[:, r * 64:(r + 1) * 64],
                           dm[:, 1, r * 128:(r + 1) * 128], start=True, stop=True)
                    pe.wait_ge(s["bt_ready"], 8 * n + c + 1)
                    mm(aux[:, 3, 256:512], bt[:], xe[:], start=True, stop=True).then_inc(s["ssd_b"], 1)
                    if c == S_STEP:
                        for t in range(2):
                            last = mm(aux[:, 4, t * 16:t * 16 + 16], selt[:, t], csg[:, SEQ:SEQ + 16], start=True, stop=True)
                        last.then_inc(s["bcs_full"], 1)
                    if S_STEP < c <= S_STEP + 4:
                        k = c - S_STEP - 1
                        if k:
                            pe.wait_ge(s["bc_used"], 4 * n + k)
                        else:
                            pe.wait_ge(s["dec_ready"], n + 1)
                        for b in range(4):
                            col = SEQ + 4 * (k // 2) + b
                            last = mm(aux[:, 4, b * 128:(b + 1) * 128], xbc[:, 2 + k % 2, col:col + 1].to_broadcast([P, P]),
                                      ident[:], start=True, stop=True)
                        last.then_inc(s["bc_full"], 1)

            at = Place(J_MIX, U_MIX)
            project_group(at, 0, False)
            scan_group(at, 0, False)
            with pe.Fori(1, GROUPS) as n:
                at = Place(J_MIX + 6 - MIX_JOBS, U_MIX + 6 - MIX_UNITS, n, MIX_JOBS, MIX_UNITS)
                project_group(at, n, True)
                scan_group(at, n, True)
            rms(GROUPS - 1, "rms_full", "sq_sum", zs[:, 0], 1)
            pe.wait_ge(s["y_lo"], 2 * GROUPS)
            jobs(Place(J_MLP0 - 8, U_MLP0 - 2), 8, 2, yh, yl)

            def layer_norm(l):
                pe.wait_ge(s["ln_sum"], l + 1)
                for c in range(NCH):
                    last = mm(aux[:, c, 0:CW], ones[:, 0], ln0[:, c * CW:(c + 1) * CW], start=True, stop=True)
                last.then_inc(s["ln_mu"], 1)
                pe.wait_ge(s["ln_add"], 8 * l + 8)
                for c in range(NCH):
                    last = mm(aux[:, c, 0:CW], ones[:, 0], ln0[:, c * CW:(c + 1) * CW], start=True, stop=True)
                last.then_inc(s["ln_var"], 1)

            def mlp(layer):
                j0, u0 = ((J_MLP0, U_MLP0), (J_MLP1, U_MLP1))[layer]
                pe.wait_ge(s["ln_lo"], 8 * (2 * layer + 1))
                hb = layer * FFB

                def up(at):
                    jobs(at, 4, KD, xh, xl)

                def down(at, b, nth):
                    pe.wait_ge(s["h_ready"], nth)
                    jobs(at, 8, 4, hh[b], hl[b])

                up(Place(j0, u0))
                with pe.Fori(0, FFB // 2 - 1) as i:
                    at = Place(j0 + 4, u0 + 4, i, 24, 16)
                    up(at)
                    down(at, 0, (hb + 2 * i) * 12 + 12)
                    up(at)
                    down(at, 1, (hb + 2 * i) * 12 + 24)
                at = Place(j0 + 4 + 24 * (FFB // 2 - 1), u0 + 4 + 16 * (FFB // 2 - 1))
                up(at)
                down(at, 0, (hb + FFB - 1) * 12)
                down(at, 1, (hb + FFB) * 12)

            layer_norm(0)
            mlp(0)
            layer_norm(1)

            def perm_of(nth):
                pe.wait_ge(s["raw_full"], nth)
                for c in range(NCH):
                    last = mm(aux[:, 2 + c, 0:CW], perm[:], raw[:, c * CW:(c + 1) * CW], start=True, stop=True)
                last.then_inc(s["perm_full"], 1)

            def project_head(at, n, new, fin):
                p = n - 1
                if fin:
                    for b in range(NB):
                        last = mm(aux[:, b // 4, (b % 4) * 128:(b % 4) * 128 + 128],
                                  smp[:, 0, b:b + 1].to_broadcast([P, P]), ident[:], start=True, stop=True)
                    last.then_inc(s["qb_full"], 1)
                if new:
                    jobs(at, 1, KD, xh, xl)
                    perm_of(2 * n + 1)
                if fin:
                    pe.wait_ge(s["ssc_ready"], p + 1)
                    mm(aux[0:16, 0, 256:257], qkn[:].rearrange("p m b -> p (m b)"), ones[:, 2, 0:1], start=True, stop=True)
                    for g in range(PAGES):
                        last = nc.tensor.transpose(aux[0:16, 0, g * 128:(g + 1) * 128],
                                                   ssc[:, g].rearrange("p m b -> p (m b)"), ident[:])
                    last.then_inc(s["srow_full"], 1)
                if new:
                    jobs(at, 1, KD, xh, xl)
                if fin:
                    pe.wait_ge(s["sp_ready"], p + 1)
                    for g in range(PAGES):
                        mm(aux[:, 1, g * 8:g * 8 + 8], srow[0:16, g * 128:(g + 1) * 128], pair[0:16, 0:8], start=True, stop=True)
                    mm(aux[:, 1, 16:24], srow[0:16, 256:257].to_broadcast([16, P]), pair[0:16, 0:8], start=True,
                       stop=True).then_inc(s["wsm_full"], 1)
                if new:
                    perm_of(2 * n + 2)
                if fin:
                    pe.wait_ge(s["wsm_ready"], p + 1)
                    pe.wait_ge(s["pv_in"], 16 * p + 16)
                    for b in range(NB):
                        for g in range(PAGES):
                            last = mm(aux[:, 1, 32 + b:33 + b], past[:, b * PAGES + g], wsm[:, g, b:b + 1],
                                      start=(g == 0), stop=(g == PAGES - 1))
                    last.then_inc(s["so_full"], 1)
                if new:
                    vp = (unit(at), *at.job())
                    chunk_of(vp, 0, 0, KD, xh, xl)
                if fin:
                    rms(p, "orms_full", "osq_done", pp, 2)
                if new:
                    chunk_of(vp, 1, 0, KD, xh, xl)
                    chunk_of(vp, 2, 0, KD, xh, xl)
                    pe.wait_ge(s["raw_v"], n + 1)
                    for c in range(8):
                        last = nc.tensor.transpose(aux[:, 3 + c // 4, (c % 4) * 128:(c % 4) * 128 + 128],
                                                   raw[:, c * 128:(c + 1) * 128], ident[:])
                    last.then_inc(s["vt_ps"], 1)
                if fin:
                    pe.wait_ge(s["a_lo"], p + 1)
                    jobs(at, 8, 1, ah, al)

            def attend(n):
                def scores(i):
                    rows = slice(i * 128, (i + 1) * 128)
                    width = (i + 1) * 128
                    for m_ in range(2):
                        if i:
                            pe.wait_ge(s["p_ready"], 16 * n + 2 * i + m_ - 1)
                        part = slice(64 * m_, 64 * m_ + 64)
                        for c0 in range(0, width, 512):
                            w = min(512, width - c0)
                            out = aux[:, 2 * m_ + c0 // 512, 0:w]
                            diag = c0 + w == width
                            for p, (qq, kk) in enumerate(((qh, kh), (ql, kh), (qh, kl))):
                                last = mm(out, qq[part, rows], kk[part, c0:c0 + w], start=(p == 0),
                                          stop=(p == 2 and not diag))
                            if diag:
                                last = mm(aux[:, 2 * m_ + c0 // 512, w - 128:w], mbf[:, 0], mbf[:, 1],
                                          start=False, stop=True)
                        last.then_inc(s["s_full"], 1)

                def turn(i):
                    pe.wait_ge(s["w_ready"], 8 * n + i + 1)
                    for k in range(i + 1):
                        last = nc.tensor.transpose(jb[:, k // 4, (k % 4) * 128:(k % 4) * 128 + 128],
                                                   pp[:, k * 128:(k + 1) * 128], ident[:])
                    last.then_inc(s["wt_ps"], 1)

                def values(i):
                    pe.wait_ge(s["wt_ready"], 8 * n + i + 1)
                    for k in range(i + 1):
                        for p, (vv, ww) in enumerate(((vth, wth), (vtl, wth), (vth, wtl))):
                            last = mm(jb[:, 2, 0:128], vv[:, k], ww[:, k], start=(k == 0 and p == 0),
                                      stop=(k == i and p == 2))
                    last.then_inc(s["pv_full"], 1)

                pe.wait_ge(s["vt_ready"], n + 1)
                scores(0)
                for i in range(8):
                    if i < 7:
                        scores(i + 1)
                    if i:
                        values(i - 1)
                    turn(i)
                values(7)
                pe.wait_ge(s["o_ready"], 8 * n + 8)

            pe.wait_ge(s["ln_lo"], 16)
            pe.wait_ge(s["attc_in"], 16 * N_ATTC)
            at = Place(J_ATT, U_ATT)
            project_head(at, 0, True, False)
            attend(0)
            with pe.Fori(1, HEADS_B) as n:
                at = Place(J_ATT + 3 - ATT_JOBS, U_ATT + 3 - ATT_UNITS, n, ATT_JOBS, ATT_UNITS)
                project_head(at, n, True, True)
                attend(n)
            project_head(Place(J_MLP1 - 8, U_MLP1 - 1), HEADS_B, False, True)

            layer_norm(2)
            mlp(1)
            layer_norm(3)

        @block.scalar
        def _(act):
            af = nc.scalar.activation

            for b in range(NCH):
                act.sem_inc(bank_free[b], 1)
            for k in range(NB * PAGES):
                    pv = act.value_load(a["ptab"][0:1, k:k + 1], min_val=0, max_val=PHYS - 1)
                    act.dma_start(kgat[k], a["cache_k"][bass.ds(pv, 1)].rearrange("a p d -> (a p) d")).then_inc(s["gathered"], 16)
                    act.dma_start(vgat[k], a["cache_v"][bass.ds(pv, 1)].rearrange("a p d -> (a p) d")).then_inc(s["gathered"], 16)
            act.dma_start(o["conv_old"], a["conv_keep"]).then_inc(s["outs"], 16)
            act.wait_ge(s["x_in"], 16)
            for k in range(KD):
                af(xh[:, k], acc[:, k], ACT.Copy).then_inc(s["x_hi"], 1)
            act.wait_ge(s["const_in"], 16 * N_CONST)
            af(selh[:], pre[0:8, 0, 4:516].rearrange("p (r c) -> p r c", r=R), ACT.Copy)
            af(selt[:], pre[0:8, 0, 516:772].rearrange("p (r c) -> p r c", r=2), ACT.Copy).then_inc(s["sel_done"], 1)

            for c in range(NCH):
                act.wait_ge(chunk_full, c + 1)
                last = af(dtx[:, c * CW:(c + 1) * CW], jb[0:HEADS_A, c, 0:CW], ACT.Identity, bias=a32[:, 0:1])
                last.then_inc(bank_free[c], 1)
            af(a32[:, 2:3], a32[:, 1:2], ACT.Exp).then_inc(s["dt_raw"], 1)
            act.wait_ge(s["dt_abs"], 1)
            af(dtt[:], dtt[:], ACT.Exp, scale=-1.0)
            act.drain()
            af(dtt[:], dtt[:], ACT.Ln, bias=1.0).then_inc(s["dt_exp"], 1)
            act.wait_ge(s["dt_soft"], 1)
            af(csh[:], cs[:], ACT.Copy).then_inc(s["cs_hi"], 1)
            act.wait_ge(s["tok_ps"], 1)
            af(tok[:, 0:2], aux[:, 0].rearrange("p (k c h) -> p k c h", k=2, c=CHUNKS), ACT.Copy).then_inc(s["tok_cp"], 1)
            act.wait_ge(s["end_ps"], 1)
            af(tok[:, 3], aux[:, 1, 0:256].rearrange("p (c h) -> p c h", c=CHUNKS), ACT.Exp).then_inc(s["cd_done"], 1)
            act.wait_ge(s["dte_arg"], 1)
            af(tok[:, 2], tok[:, 2], ACT.Exp).then_inc(s["dte_exp"], 1)
            act.wait_ge(s["cs_lo"], 1)
            act.dma_start(csd[0], csh[:].bitcast(F32)).then_inc(s["cs_stored"], 16)
            act.dma_start(csd[1], csl[:].bitcast(F32)).then_inc(s["cs_stored"], 16)
            act.wait_ge(s["cs_stored"], 32)
            act.wait_ge(s["tok_done"], 1)

            def take(c, done, dst, func, **kw):
                act.wait_ge(chunk_full, done + c + 1)
                af(dst, jb[:, c, 0:CW], func, **kw).then_inc(bank_free[c], 1)

            def norm_sums(p):
                for t in range(2):
                    act.wait_ge(s["yg_ready"], 2 * p + t + 1)
                    af(zs[:, t], y[:, t], ACT.Square).then_inc(s["sq_done"], 1)

            def norm_root(p):
                act.wait_ge(s["rms_full"], p + 1)
                af(zs[:, 1].rearrange("p (c w) -> p c w", c=NCH), aux[:, 0:3, 0:CW], ACT.Sqrt, bias=eps[:]).then_inc(s["rms_sqrt"], 1)

            def norm_hi(p):
                for t in range(2):
                    act.wait_ge(s["yn_ready"], 2 * p + t + 1)
                    af(yh[:, t], y[:, t], ACT.Copy).then_inc(s["y_hi"], 1)

            def project_group(at, n, fin):
                if fin:
                    norm_sums(n - 1)
                    act.wait_ge(s["ssd_b"], 8 * n)
                    act.wait_ge(s["s_out"], 32 * n)
                for k in range(2):
                    act.dma_start(csg[4 * k:4 * k + 4].bitcast(F32), csd[k, bass.ds(n * R, R)]).then_inc(s["csg_in"], 16)
                act.dma_start(scv[:], a["sconv"][:, bass.ds(n, 1)].rearrange("p a t k b -> p (a t) k b")).then_inc(s["scv_in"], 16)
                for t in range(4):
                    _, done = at.job()
                    if t >= 2:
                        act.wait_ge(s["xbc_done"], 4 * n + t - 1)
                    for c in range(NCH):
                        take(c, done, pre[:, t % 2, 4 + c * CW:4 + (c + 1) * CW], ACT.Copy)
                    act.drain()
                    if t == 0 and fin:
                        act.wait_ge(s["cnew_out"], 16 * n)
                    af(cnew[:, t], pre[:, t % 2, 4 + SEQ - 3:4 + T], ACT.Copy).then_inc(s["pre_full"], 1)
                    if t == 0 and fin:
                        norm_root(n - 1)
                    act.wait_ge(s["conv_done"], 4 * n + t + 1)
                    af(pre[:, t % 2, 4:4 + T], ct[:], ACT.Tanh).then_inc(s["tanh_done"], 1)
                    if t == 0 and fin:
                        norm_hi(n - 1)
                act.wait_ge(s["pre_full"], 4 * n + 4)
                act.dma_start(o["conv_new"][:, bass.ds(n, 1)].rearrange("p a t k -> p (a t) k"), cnew[:]).then_inc(s["cnew_out"], 16)

            def scan_group(at, n, out):
                if out:
                    at.job(8)
                act.wait_ge(s["xbc_done"], 4 * n + 4)
                for t in range(2):
                    act.dma_start(pre[:, t, 4:4 + SEQ].rearrange("p (b n) -> p b n", b=NB),
                                  a["state"][:, bass.ds(2 * n + t, 1)].rearrange("p a b n -> p (a b) n")).then_inc(s["s_in"], 16)
                for c in range(CHUNKS):
                    x = 8 * n + c
                    act.wait_ge(s["ssd_in"], x + 1)
                    af(e2[:], aux[:, 2, 0:256], ACT.Exp).then_inc(s["e2_ready"], 1)
                    af(bt[:], aux[:, 2, 256:384], ACT.Copy).then_inc(s["bt_ready"], 1)
                    act.wait_ge(s["d_ready"], x + 1)
                    af(dm[:, 0], dm[:, 0], ACT.Exp).then_inc(s["e_ready"], 1)
                    for t, zc in Z_FILL.get(c, ()):
                        if zc == 0:
                            _, done = at.job()
                            if t:
                                act.wait_ge(s["z_done"], 2 * n + 1)
                            elif out:
                                act.wait_ge(s["y_lo"], 2 * n)
                        cols = slice(zc * CW, (zc + 1) * CW)
                        act.wait_ge(chunk_full, done + zc + 1)
                        af(ct[:, cols], jb[:, zc, 0:CW], ACT.Tanh, scale=0.5)
                        take(zc, done, zs[:, t, cols], ACT.Copy, scale=0.5)
                        if zc == 2:
                            act.drain().then_inc(s["z_full"], 1)
                    if c == S_STEP:
                        act.wait_ge(s["bcs_full"], n + 1)
                        v = aux[:, 4, 0:32].rearrange("p (t c) -> p t c", t=2)
                        af(dec[:], v[:, :, 0:8], ACT.Exp)
                        af(dts[:], v[:, :, 8:16], ACT.Copy).then_inc(s["dec_ready"], 1)
                    if c == 7:
                        act.wait_ge(s["s_new"], n + 1)
                        for t in range(2):
                            act.dma_start(o["ssm_s"][:, bass.ds(2 * n + t, 1)].rearrange("p a b n -> p (a b) n"),
                                          pre[:, t, 4:4 + SEQ].rearrange("p (b n) -> p b n", b=NB)).then_inc(s["s_out"], 16)
                act.wait_ge(s["h_done"], 8 * n + 8)
                act.dma_start(o["ssm_p"][:, bass.ds(n, 1)].rearrange("p a q -> p (a q)"), hst[:]).then_inc(s["h_out"], 16)

            at = Place(J_MIX, U_MIX)
            project_group(at, 0, False)
            scan_group(at, 0, False)
            with act.Fori(1, GROUPS) as n:
                at = Place(J_MIX + 6 - MIX_JOBS, 0, n, MIX_JOBS, 0)
                project_group(at, n, True)
                scan_group(at, n, True)
            norm_sums(GROUPS - 1)
            norm_root(GROUPS - 1)
            norm_hi(GROUPS - 1)

            def layer_norm(l):
                for k in range(KD):
                    act.wait_ge(s["ln_cent"], 8 * l + k + 1)
                    if k >= 2:
                        act.wait_ge(s["ln_add"], 8 * l + k - 1)
                    af(lnq[:, k % 2], acc[:, k], ACT.Square).then_inc(s["ln_sq"], 1)
                act.wait_ge(s["ln_var"], l + 1)
                af(lnq[:, 0].rearrange("p (c w) -> p c w", c=NCH), aux[:, 0:3, 0:CW], ACT.Sqrt, bias=eps[:]).then_inc(s["ln_std"], 1)
                for k in range(KD):
                    act.wait_ge(s["ln_norm"], 8 * l + k + 1)
                    af(acc[:, k], acc[:, k], ACT.Identity, scale=lnp[:, l, 0, k:k + 1], bias=lnp[:, l, 1, k:k + 1]).then_inc(s["ln_aff"], 1)
                    if l < 3:
                        act.drain()
                        af(xh[:, k], acc[:, k], ACT.Copy).then_inc(s["ln_hi"], 1)
                    else:
                        act.wait_ge(s["ln_aff"], 8 * l + k + 1)
                        act.dma_start(o["yT"][:, k], acc[:, k]).then_inc(s["outs"], 16)

            def mlp(layer):
                j0 = (J_MLP0, J_MLP1)[layer]
                hb = layer * FFB

                def up(at, b, block_):
                    for j in range(4):
                        _, done = at.job()
                        for c in range(NCH):
                            e = block_ * 12 + j * 3 + c
                            slot = (j * 3 + c) % 4
                            if not isinstance(e, int) or e >= 4:
                                act.wait_ge(s["h_ready"], e - 3)
                            take(c, done, rl[:, slot], ACT.Relu)
                            act.drain()
                            af(hh[b][:, j, c * CW:(c + 1) * CW], rl[:, slot], ACT.Square).then_inc(s["h_sq"], 1)

                up(Place(j0, 0), 0, hb)
                with act.Fori(0, FFB // 2 - 1) as i:
                    at = Place(j0 + 4, 0, i, 24, 0)
                    up(at, 1, hb + 2 * i + 1)
                    at.job(8)
                    act.wait_ge(s["relu_done"], hb + 2 * i + 1)
                    up(at, 0, hb + 2 * i + 2)
                    at.job(8)
                    act.wait_ge(s["relu_done"], hb + 2 * i + 2)
                up(Place(j0 + 4 + 24 * (FFB // 2 - 1), 0), 1, hb + FFB - 1)

            act.wait_ge(s["h_out"], 16 * GROUPS)
            act.wait_ge(s["s_out"], 32 * GROUPS)
            act.wait_ge(s["cnew_out"], 16 * GROUPS)
            layer_norm(0)
            mlp(0)
            layer_norm(1)

            act.wait_ge(s["ln_lo"], 16)
            for dst, name in ((cos, "cos"), (sin, "sin"), (perm, "perm"), (mbf, "mbf"), (subg, "subg"),
                              (half, "half"), (pair, "pair")):
                act.dma_start(dst[:], a[name]).then_inc(s["attc_in"], 16)
            act.dma_start(lamv[:], a["lamv"].partition_broadcast(P)).then_inc(s["attc_in"], 16)
            act.wait_ge(s["gathered"], 16 * 2 * NB * PAGES)
            act.wait_ge(s["lam_sum"], 1)
            af(lam[:, 0:2], lam[:, 0:2], ACT.Exp).then_inc(s["lam_exp"], 1)

            def project_head(at, n, new, fin):
                p = n - 1
                if new:
                    _, done = at.job()
                    for c in range(NCH):
                        take(c, done, raw[:, c * CW:(c + 1) * CW], ACT.Copy)
                    act.drain().then_inc(s["raw_full"], 1)
                if fin:
                    act.wait_ge(s["ssc_ready"], p + 1)
                    act.dma_start(past[:], vgat[:, :, bass.ds(p * P, P)].rearrange("g t d -> t g d")).then_inc(s["pv_in"], 16)
                if new:
                    act.wait_ge(s["rope_done"], 2 * n + 1)
                    af(qh[:], rot[:], ACT.Copy).then_inc(s["qk_hi"], 1)
                if fin:
                    act.wait_ge(s["snm_ready"], p + 1)
                    af(srow[0:16, 0:257], srow[0:16, 0:257], ACT.Exp, scale=SCALE, bias=st[0:16, 4:5],
                       accum_out=st[0:16, 5:6]).then_inc(s["sexp_ready"], 1)
                if new:
                    _, done = at.job()
                    for c in range(NCH):
                        take(c, done, raw[:, c * CW:(c + 1) * CW], ACT.Copy)
                    act.drain().then_inc(s["raw_full"], 1)
                    act.wait_ge(s["rope_done"], 2 * n + 2)
                    af(kh[:], rot[:], ACT.Copy).then_inc(s["qk_hi"], 1)
                    act.dma_start(o["kT"][:, bass.ds(n, 1)].rearrange("p a t -> p (a t)"), rot[:]).then_inc(s["k_out"], 16)
                if fin:
                    act.wait_ge(s["o_smp"], p + 1)
                    af(pp[:, 0:T], ob[:], ACT.Square).then_inc(s["osq_done"], 1)
                if new:
                    _, done = at.job()
                    take(0, done, raw[:, 0:CW], ACT.Copy)
                if fin:
                    act.wait_ge(s["orms_full"], p + 1)
                    af(pp[:, 0:T].rearrange("p (c w) -> p c w", c=NCH), aux[:, 0:3, 0:CW], ACT.Sqrt, bias=eps[:]).then_inc(s["orms_sqrt"], 1)
                if new:
                    for c in (1, 2):
                        take(c, done, raw[:, c * CW:(c + 1) * CW], ACT.Copy)
                    act.drain().then_inc(s["raw_v"], 1)
                    act.wait_ge(s["raw_v"], n + 1)
                    act.dma_start(o["vT"][:, bass.ds(n, 1)].rearrange("p a t -> p (a t)"), raw[:]).then_inc(s["v_out"], 16)
                    act.wait_ge(s["vt_ps"], n + 1)
                    af(vth[:], aux[:, 3:5].rearrange("p a (b c) -> p (a b) c", b=4), ACT.Copy).then_inc(s["vt_hi"], 1)
                if fin:
                    act.wait_ge(s["on_ready"], p + 1)
                    af(ah[:, 0], ob[:], ACT.Copy).then_inc(s["a_hi"], 1)
                    at.job(8)

            def attend(n):
                act.dma_start(past[:], kgat[:, :, bass.ds(n * P, P)].rearrange("g t d -> t g d")).then_inc(s["pk_in"], 16)

                def output(i):
                    act.wait_ge(s["pv_full"], 8 * n + i + 1)
                    af(ob[:, i * 128:(i + 1) * 128], jb[:, 2, 0:128], ACT.Copy).then_inc(s["o_ready"], 1)

                for i in range(8):
                    width = (i + 1) * 128
                    if i:
                        act.wait_ge(s["wt_ps"], 8 * n + i)
                    for m_ in range(2):
                        e = 16 * n + 2 * i + m_
                        act.wait_ge(s["nmax_ready"], e + 1)
                        src = aux[:, 2 * m_:2 * m_ + 2].rearrange("p a b -> p (a b)")[:, 0:width]
                        af(pp[:, m_ * 1024:m_ * 1024 + width], src, ACT.Exp, scale=SCALE,
                           bias=st[:, m_:m_ + 1], accum_out=st[:, 2 + m_:3 + m_]).then_inc(s["p_ready"], 1)
                    if i:
                        if i >= 2:
                            output(i - 2)
                        af(wth[:, 0:i], jb[:, 0:2].rearrange("p a (b c) -> p (a b) c", b=4)[:, 0:i],
                           ACT.Copy).then_inc(s["wt_hi"], 1)
                output(6)
                act.wait_ge(s["wt_ps"], 8 * n + 8)
                af(wth[:], jb[:, 0:2].rearrange("p a (b c) -> p (a b) c", b=4), ACT.Copy).then_inc(s["wt_hi"], 1)
                output(7)

            at = Place(J_ATT, 0)
            project_head(at, 0, True, False)
            attend(0)
            with act.Fori(1, HEADS_B) as n:
                at = Place(J_ATT + 3 - ATT_JOBS, 0, n, ATT_JOBS, 0)
                act.wait_ge(s["v_out"], 16 * n)
                act.wait_ge(s["k_out"], 16 * n)
                project_head(at, n, True, True)
                attend(n)
            project_head(Place(J_MLP1 - 8, 0), HEADS_B, False, True)

            layer_norm(2)
            mlp(1)
            layer_norm(3)
            act.wait_ge(s["k_out"], 16 * HEADS_B)
            act.wait_ge(s["v_out"], 16 * HEADS_B)

        @block.vector
        def _(dve):
            tt, ts, stt = nc.vector.tensor_tensor, nc.vector.tensor_scalar, nc.vector.scalar_tensor_tensor
            drain = dve.drain

            def f(ap):
                return ap.bitcast(F32)

            nc.vector.memset(eps[:], EPS)
            nc.vector.memset(pre[:, :, 0:4], 0.0)
            dve.wait_ge(s["x_in"], 16)
            for k in range(KD):
                dve.wait_ge(s["x_hi"], k + 1)
                tt(xl[:, k], acc[:, k], f(xh[:, k]), ALU.subtract).then_inc(s["x_ready"], 1)
                drain()
                ts(acc[:, k], acc[:, k], ALPHA, None, ALU.mult)
            dve.wait_ge(s["const_in"], 16 * N_CONST)
            ts(pall[:, :, 0:20], pall[:, :, 0:20], 0.5, None, ALU.mult)
            dve.wait_ge(s["dt_raw"], 1)
            stt(dtt[:], dtx[:, 0:T], -1.0, dtx[:, 0:T], ALU.mult, ALU.max).then_inc(s["dt_abs"], 1)
            ts(a32[:, 3:4], a32[:, 2:3], -1.0, None, ALU.mult)
            dve.wait_ge(s["dt_exp"], 1)
            stt(dtx[:, 0:T], dtx[:, 0:T], 0.0, dtt[:], ALU.max, ALU.add)
            drain()
            ts(dtt[:], dtx[:, 0:T], a32[:, 3:4], None, ALU.mult)
            ts(cs[:, T:T + NB], dtx[:, SEQ:T], 1.0, None, ALU.mult)
            drain()
            nc.vector.tensor_tensor_scan(cs[:, 0:T], scanm[:], dtt[:], 0.0, ALU.mult, ALU.add)
            drain().then_inc(s["dt_soft"], 1)
            dve.wait_ge(s["cs_hi"], 1)
            tt(csl[:], cs[:], f(csh[:]), ALU.subtract).then_inc(s["cs_lo"], 1)
            dve.wait_ge(s["cd_done"], 1)
            tt(tok[:, 2], aux[:, 1, 0:256].rearrange("p (c h) -> p c h", c=CHUNKS), tok[:, 0], ALU.subtract)
            drain().then_inc(s["dte_arg"], 1)
            dve.wait_ge(s["dte_exp"], 1)
            tt(tok[:, 2], tok[:, 2], tok[:, 1], ALU.mult).then_inc(s["tok_done"], 1)
            drain()

            def add_job(at, k):
                _, done = at.job()
                for c in range(NCH):
                    cols = slice(c * CW, (c + 1) * CW)
                    dve.wait_ge(chunk_full, done + c + 1)
                    tt(acc[:, k, cols], jb[:, c, 0:CW], acc[:, k, cols], ALU.add).then_inc(bank_free[c], 1)

            def accumulate(at):
                for k in range(KD):
                    add_job(at, k)
                drain()

            def conv(n, t):
                dve.wait_ge(s["pre_full"], 4 * n + t + 1)
                src = pre[:, t % 2]
                w = lambda k: pg[:, 4 * t + k:4 * t + k + 1]
                ts(ct[:], src[:, 4:4 + T], w(3), pg[:, 16 + t:17 + t], ALU.mult, ALU.add)
                for k in range(3):
                    drain()
                    stt(ct[:, 0:SEQ], src[:, 1 + k:1 + k + SEQ], w(k), ct[:, 0:SEQ], ALU.mult, ALU.add)
                    stt(ct[:, SEQ:T], scv[:, t, k], w(k), ct[:, SEQ:T], ALU.mult, ALU.add)
                drain().then_inc(s["conv_done"], 1)

            def silu(n, t):
                dve.wait_ge(s["tanh_done"], 4 * n + t + 1)
                stt(xbc[:, t], pre[:, t % 2, 4:4 + T], 1.0, ct[:], ALU.add, ALU.mult)
                drain().then_inc(s["xbc_done"], 1)

            def gate(p):
                for t in range(2):
                    tt(y[:, t], y[:, t], zs[:, t], ALU.mult)
                    drain().then_inc(s["yg_ready"], 1)
                dve.wait_ge(s["sq_done"], 2 * p + 2)
                tt(zs[:, 0], zs[:, 0], zs[:, 1], ALU.add)
                drain().then_inc(s["sq_sum"], 1)

            def norm(p):
                dve.wait_ge(s["rms_sqrt"], p + 1)
                nc.vector.reciprocal(zs[:, 1], zs[:, 1])
                drain()
                for t in range(2):
                    stt(y[:, t], y[:, t], gn[:, t:t + 1], zs[:, 1], ALU.mult, ALU.mult)
                    drain().then_inc(s["yn_ready"], 1)

            def norm_lo(p):
                for t in range(2):
                    dve.wait_ge(s["y_hi"], 2 * p + t + 1)
                    tt(yl[:, t], y[:, t], f(yh[:, t]), ALU.subtract).then_inc(s["y_lo"], 1)

            def project_group(n, fin):
                if fin:
                    gate(n - 1)
                nc.vector.tensor_copy(pg[:], pall[:, bass.ds(n, 1)].rearrange("p a k -> p (a k)"))
                drain()
                dve.wait_ge(s["scv_in"], 16 * n + 16)
                for t in range(4):
                    conv(n, t)
                    if t == 0 and fin:
                        norm(n - 1)
                    silu(n, t)
                    if t == 0 and fin:
                        norm_lo(n - 1)

            hd = lambda ap: ap.unsqueeze(2).to_broadcast([P, R, HD])
            v4 = lambda ap: ap.rearrange("p (r q) -> p r q", r=R)
            two = lambda ap: ap.rearrange("p (t l) -> p t l", t=2)
            b4 = lambda ap: ap.unsqueeze(2).to_broadcast([P, 4, P])

            def sample_step(n, k):
                b0 = 4 * (k // 2)
                dve.wait_ge(s["bc_full"], 4 * n + k + 1)
                for t in range(2):
                    sv = v4(pre[:, t, 4 + b0 * P:4 + (b0 + 4) * P])
                    if k % 2 == 0:
                        tt(v4(st2[:]), v4(aux[:, 4]), b4(xdt[:, t, b0:b0 + 4]), ALU.mult)
                        drain()
                        tt(sv, sv, v4(st2[:]), ALU.add)
                    else:
                        tt(v4(st2[:]), v4(aux[:, 4]), sv, ALU.mult)
                        drain()
                        nc.vector.tensor_reduce(y[:, t, SEQ + b0:SEQ + b0 + 4], v4(st2[:]), AX.X, ALU.add)
                    drain()
                if k == 2:
                    drain().then_inc(s["s_new"], 1)
                drain().then_inc(s["bc_used"], 1)

            def scan_group(at, n, out):
                nc.vector.tensor_copy(tg[:], tok[:, :, :, bass.ds(n * R, R)])
                if out:
                    dve.wait_ge(s["h_out"], 16 * n)
                nc.vector.memset(hst[:], 0.0)
                drain().then_inc(s["h_zero"], 1)
                if out:
                    add_job(at, 0)
                    add_job(at, 1)
                for c in range(CHUNKS):
                    x = 8 * n + c
                    cols = slice(c * CHUNK, (c + 1) * CHUNK)
                    dve.wait_ge(s["ssd_in"], x + 1)
                    for r in range(R):
                        last = stt(dm[:, 0, r * 128:(r + 1) * 128], aux[:, 1, r * 128:(r + 1) * 128],
                                   tg[:, 0, c, r:r + 1], capm[:], ALU.subtract, ALU.min)
                    last.then_inc(s["d_ready"], 1)
                    tt(v4(xs[:]), v4(aux[:, 0, 0:256]), hd(tg[:, 1, c]), ALU.mult)
                    tt(v4(xe[:]), v4(aux[:, 0, 0:256]), hd(tg[:, 2, c]), ALU.mult)
                    dve.wait_ge(s["ssd_off"], x + 1)
                    dve.wait_ge(s["e2_ready"], x + 1)
                    tt(y[:, :, cols], two(aux[:, 3, 0:256]), two(e2[:]), ALU.mult)
                    tt(v4(hst[:]), v4(hst[:]), hd(tg[:, 3, c]), ALU.mult)
                    dve.wait_ge(s["e_ready"], x + 1)
                    tt(v4(dm[:, 1]), v4(dm[:, 0]), aux[:, 0, 384:512].unsqueeze(1).to_broadcast([P, R, P]), ALU.mult)
                    drain().then_inc(s["m_ready"], 1)
                    if out and c < 3:
                        add_job(at, 2 + 2 * c)
                        add_job(at, 3 + 2 * c)
                    dve.wait_ge(s["ssd_b"], x + 1)
                    tt(y[:, :, cols], two(aux[:, 3, 0:256]), y[:, :, cols], ALU.add)
                    tt(hst[:], aux[:, 3, 256:512], hst[:], ALU.add)
                    drain().then_inc(s["h_done"], 1)
                    for t, zc in Z_FILL.get(c, ()):
                        if zc == 2:
                            dve.wait_ge(s["z_full"], 2 * n + t + 1)
                            stt(zs[:, t], ct[:], 1.0, zs[:, t], ALU.add, ALU.mult)
                            drain().then_inc(s["z_done"], 1)
                    if c == S_STEP:
                        dve.wait_ge(s["dec_ready"], n + 1)
                        dve.wait_ge(s["s_in"], 32 * n + 32)
                        tt(xdt[:], xbc[:, 0:2, SEQ:T], dts[:], ALU.mult)
                        for t in range(2):
                            sv = pre[:, t, 4:4 + SEQ].rearrange("p (b n) -> p b n", b=NB)
                            tt(sv, sv, dec[:, t].unsqueeze(2).to_broadcast([P, NB, P]), ALU.mult)
                        drain()
                    if S_STEP < c <= S_STEP + 4:
                        sample_step(n, c - S_STEP - 1)
                for t in range(2):
                    stt(y[:, t], xbc[:, t], pg[:, 20 + t:21 + t], y[:, t], ALU.mult, ALU.add)
                nc.vector.tensor_copy(gn[:], pg[:, 22:24])
                drain()

            dve.wait_ge(s["cs_stored"], 32)
            at = Place(J_MIX + 4, 0)
            project_group(0, False)
            scan_group(at, 0, False)
            with dve.Fori(1, GROUPS) as n:
                at = Place(J_MIX + 6 + 4 - MIX_JOBS, 0, n, MIX_JOBS, 0)
                project_group(n, True)
                scan_group(at, n, True)
            gate(GROUPS - 1)
            norm(GROUPS - 1)
            norm_lo(GROUPS - 1)
            accumulate(Place(J_MLP0 - 8, 0))

            def layer_norm(l):
                tt(ln0[:], acc[:, 0], acc[:, 1], ALU.add)
                for k in range(2, KD):
                    drain()
                    tt(ln0[:], ln0[:], acc[:, k], ALU.add)
                drain().then_inc(s["ln_sum"], 1)
                dve.wait_ge(s["ln_mu"], l + 1)
                cv = lambda ap: ap.rearrange("p (c w) -> p c w", c=NCH)
                for k in range(KD):
                    tt(cv(acc[:, k]), cv(acc[:, k]), aux[:, 0:3, 0:CW], ALU.subtract).then_inc(s["ln_cent"], 1)
                for k in range(KD):
                    dve.wait_ge(s["ln_sq"], 8 * l + k + 1)
                    if k == 0:
                        nc.vector.tensor_copy(ln0[:], lnq[:, 0])
                    else:
                        tt(ln0[:], ln0[:], lnq[:, k % 2], ALU.add)
                    drain().then_inc(s["ln_add"], 1)
                dve.wait_ge(s["ln_std"], l + 1)
                nc.vector.reciprocal(lnq[:, 1], lnq[:, 0])
                drain()
                for k in range(KD):
                    tt(acc[:, k], acc[:, k], lnq[:, 1], ALU.mult).then_inc(s["ln_norm"], 1)
                if l < 3:
                    for k in range(KD):
                        dve.wait_ge(s["ln_hi"], 8 * l + k + 1)
                        tt(xl[:, k], acc[:, k], f(xh[:, k]), ALU.subtract)
                        drain().then_inc(s["ln_lo"], 1)
                        ts(acc[:, k], acc[:, k], ALPHA, None, ALU.mult)
                    drain()

            def mlp(layer):
                j0 = (J_MLP0, J_MLP1)[layer]
                hb = layer * FFB

                def up(at, b, block_):
                    at.job(4)
                    for j in range(4):
                        for c in range(NCH):
                            e = block_ * 12 + j * 3 + c
                            slot = (j * 3 + c) % 4
                            dve.wait_ge(s["h_sq"], e + 1)
                            tt(rl[:, slot], rl[:, slot], rl[:, slot], ALU.mult)
                            drain()
                            tt(hl[b][:, j, c * CW:(c + 1) * CW], rl[:, slot], f(hh[b][:, j, c * CW:(c + 1) * CW]),
                               ALU.subtract).then_inc(s["h_ready"], 1)

                def down(at):
                    accumulate(at)
                    drain().then_inc(s["relu_done"], 1)

                up(Place(j0, 0), 0, hb)
                with dve.Fori(0, FFB // 2 - 1) as i:
                    at = Place(j0 + 4, 0, i, 24, 0)
                    up(at, 1, hb + 2 * i + 1)
                    down(at)
                    up(at, 0, hb + 2 * i + 2)
                    down(at)
                at = Place(j0 + 4 + 24 * (FFB // 2 - 1), 0)
                up(at, 1, hb + FFB - 1)
                down(at)
                down(at)

            layer_norm(0)
            mlp(0)
            layer_norm(1)

            dve.wait_ge(s["attc_in"], 16 * N_ATTC)
            tt(lamv[:, 0:2], lamv[:, 0:2], lamv[:, 2:4], ALU.mult)
            drain()
            nc.vector.tensor_reduce(lam[:, 0:2], lamv[:, 0:2], AX.X, ALU.add)
            ts(subg[:], subg[:], 1.0 - LAM_INIT, None, ALU.mult)
            drain().then_inc(s["lam_sum"], 1)
            dve.wait_ge(s["lam_exp"], 1)
            tt(lam[:, 2:3], lam[:, 1:2], lam[:, 0:1], ALU.subtract)
            drain()
            ts(lam[:, 2:3], lam[:, 2:3], LAM_INIT, None, ALU.subtract)
            drain()
            stt(pair[:, 10:11], pair[:, 9:10], lam[0:16, 2:3], pair[:, 8:9], ALU.mult, ALU.add)
            drain()

            cv = lambda ap: ap.rearrange("p (c w) -> p c w", c=NCH)

            def rope(n, j):
                e = 2 * n + j + 1
                dve.wait_ge(s["raw_full"], e)
                tt(rot[:], raw[:], cos[:], ALU.mult)
                drain()
                dve.wait_ge(s["perm_full"], e)
                tt(cv(raw[:]), aux[:, 2:5, 0:CW], cv(sin[:]), ALU.mult)
                drain()
                tt(rot[:], rot[:], raw[:], ALU.add)
                drain().then_inc(s["rope_done"], 1)
                nc.vector.tensor_copy(smp[:, j], rot[:, SEQ:T])
                dve.wait_ge(s["qk_hi"], e)
                tt((ql, kl)[j][:], rot[:], f((qh, kh)[j][:]), ALU.subtract)
                drain()

            def project_head(at, n, new, fin):
                p = n - 1
                if fin:
                    dve.wait_ge(s["qb_full"], p + 1)
                    dve.wait_ge(s["pk_in"], 16 * p + 16)
                    for g in range(PAGES):
                        tt(pp[:].rearrange("p (b g d) -> p g b d", b=NB, g=PAGES)[:, g],
                           past[:].rearrange("p (b g) d -> p g b d", g=PAGES)[:, g],
                           aux[:, 0:2].rearrange("p a (b d) -> p (a b) d", b=4), ALU.mult)
                    tt(qkn[:, 0], smp[:, 0], smp[:, 1], ALU.mult)
                    drain()
                    for g in range(PAGES):
                        for m_ in range(2):
                            v = pp[:].rearrange("p (b g m d) -> p g m b d", b=NB, g=PAGES, m=2)[:, g, m_]
                            nc.vector.tensor_reduce(ssc[:, g, m_], v, AX.X, ALU.add)
                    tt(qkn[:, 1], qkn[:, 0], half[:, 1], ALU.mult)
                    drain()
                    tt(qkn[:, 0], qkn[:, 0], half[:, 0], ALU.mult)
                    drain().then_inc(s["ssc_ready"], 1)
                if new:
                    rope(n, 0)
                if fin:
                    dve.wait_ge(s["srow_full"], p + 1)
                    nc.vector.tensor_copy(srow[:, 0:257], aux[0:16, 0, 0:257])
                    drain()
                    nc.vector.tensor_reduce(st[0:16, 6:7], srow[:, 0:257], AX.X, ALU.max)
                    drain()
                    ts(st[0:16, 4:5], st[0:16, 6:7], -SCALE, None, ALU.mult)
                    drain().then_inc(s["snm_ready"], 1)
                    dve.wait_ge(s["sexp_ready"], p + 1)
                    nc.vector.reciprocal(st[0:16, 5:6], st[0:16, 5:6])
                    drain()
                    ts(srow[:, 0:257], srow[:, 0:257], st[0:16, 5:6], pair[:, 10:11], ALU.mult, ALU.mult)
                    drain().then_inc(s["sp_ready"], 1)
                    dve.wait_ge(s["wsm_full"], p + 1)
                    nc.vector.tensor_copy(wsm[:].rearrange("p k b -> p (k b)"), aux[:, 1, 0:24])
                    drain().then_inc(s["wsm_ready"], 1)
                    tt(smp[:, 2], smp[:, 2], wsm[:, 2], ALU.mult)
                    drain()
                if new and not fin:
                    rope(n, 1)
                if fin:
                    dve.wait_ge(s["o_ready"], 8 * p + 8)
                    if new:
                        rope(n, 1)
                    dve.wait_ge(s["so_full"], p + 1)
                    tt(ob[:, SEQ:T], aux[:, 1, 32:40], smp[:, 2], ALU.add)
                    drain().then_inc(s["o_smp"], 1)
                if new:
                    at.job(3)
                    dve.wait_ge(s["raw_v"], n + 1)
                    nc.vector.tensor_copy(smp[:, 2], raw[:, SEQ:T])
                if fin:
                    dve.wait_ge(s["orms_sqrt"], p + 1)
                    nc.vector.reciprocal(pp[:, 0:T], pp[:, 0:T])
                    drain()
                    stt(ob[:], ob[:], subg[:, 0:1], pp[:, 0:T], ALU.mult, ALU.mult)
                    drain().then_inc(s["on_ready"], 1)
                if new:
                    dve.wait_ge(s["vt_hi"], n + 1)
                    tt(vtl[:], aux[:, 3:5].rearrange("p a (b c) -> p (a b) c", b=4), f(vth[:]), ALU.subtract)
                    drain().then_inc(s["vt_ready"], 1)
                if fin:
                    dve.wait_ge(s["a_hi"], p + 1)
                    tt(al[:, 0], ob[:], f(ah[:, 0]), ALU.subtract)
                    drain().then_inc(s["a_lo"], 1)
                    accumulate(at)

            def attend(n):
                def low(i):
                    dve.wait_ge(s["wt_hi"], 8 * n + i + 1)
                    tt(wtl[:, 0:i + 1], jb[:, 0:2].rearrange("p a (b c) -> p (a b) c", b=4)[:, 0:i + 1],
                       f(wth[:, 0:i + 1]), ALU.subtract)
                    drain().then_inc(s["wt_ready"], 1)

                for i in range(8):
                    width = (i + 1) * 128
                    for m_ in range(2):
                        e = 16 * n + 2 * i + m_
                        dve.wait_ge(s["s_full"], e + 1)
                        src = aux[:, 2 * m_:2 * m_ + 2].rearrange("p a b -> p (a b)")[:, 0:width]
                        nc.vector.tensor_reduce(st[:, 6 + m_:7 + m_], src, AX.X, ALU.max)
                        drain()
                        ts(st[:, m_:m_ + 1], st[:, 6 + m_:7 + m_], -SCALE, None, ALU.mult).then_inc(s["nmax_ready"], 1)
                    dve.wait_ge(s["p_ready"], 16 * n + 2 * i + 2)
                    nc.vector.reciprocal(st[:, 2:4], st[:, 2:4])
                    drain()
                    ts(pp[:, 1024:1024 + width], pp[:, 1024:1024 + width], st[:, 3:4], lam[:, 2:3], ALU.mult, ALU.mult)
                    drain()
                    stt(pp[:, 0:width], pp[:, 0:width], st[:, 2:3], pp[:, 1024:1024 + width], ALU.mult, ALU.add)
                    drain().then_inc(s["w_ready"], 1)
                    if i:
                        low(i - 1)
                low(7)

            project_head(Place(J_ATT, 0), 0, True, False)
            attend(0)
            with dve.Fori(1, HEADS_B) as n:
                project_head(Place(J_ATT + 3 - ATT_JOBS, 0, n, ATT_JOBS, 0), n, True, True)
                attend(n)
            project_head(Place(J_MLP1 - 8, 0), HEADS_B, False, True)

            layer_norm(2)
            mlp(1)
            layer_norm(3)


_OUT_SHAPES = {
    "yT": (P, KD, T), "kT": (P, HEADS_B, T), "vT": (P, HEADS_B, T), "conv_new": (P, GROUPS, 4, 11),
    "conv_old": (NB, CONV_W - 2, CONV_DIM), "ssm_p": (P, GROUPS, 256), "ssm_s": (P, 2 * GROUPS, NB, P),
}


def _tiles(w):
    k, m = w.shape
    return w.reshape(k // P, P, m // P, P).transpose(2, 1, 0, 3)


def _stream(w_in, w_out, w_up, w_down, w_kv, w_q, w_o):
    units = np.zeros((UNITS, P, 8, P), np.float32)
    at = [0]

    def put(block):
        units[at[0]:at[0] + len(block)] = block
        at[0] += len(block)

    def rows(w, k0, kt):
        t = _tiles(w[k0 * P:(k0 + kt) * P])
        m = t.shape[0]
        put(t.reshape(m * kt // 8, 8 // kt, P, kt, P).transpose(0, 2, 1, 3, 4).reshape(-1, P, 8, P))

    dt = np.zeros((D, P), np.float32)
    dt[:, :HEADS_A] = w_in[:, D_INNER + CONV_DIM:]
    put(_tiles(dt))
    t_in = _tiles(w_in[:, :D_INNER + CONV_DIM])
    z, x, b, c = t_in[:16], t_in[16:32], t_in[32:40], t_in[40:48]
    for g in range(GROUPS):
        put(np.stack([x[2 * g], x[2 * g + 1], b[g], c[g]]))
        if g:
            rows(w_out, 2 * (g - 1), 2)
        put(z[2 * g:2 * g + 2])
    rows(w_out, 2 * (GROUPS - 1), 2)

    def mlp(layer):
        up = _tiles(w_up[layer])
        put(up[0:4])
        for b_ in range(1, FFB):
            put(up[4 * b_:4 * b_ + 4])
            rows(w_down[layer], 4 * (b_ - 1), 4)
        rows(w_down[layer], 4 * (FFB - 1), 4)

    mlp(0)
    q, kv = _tiles(w_q), _tiles(w_kv)
    for h in range(HEADS_B):
        put(np.stack([q[h], kv[h], kv[HEADS_B + h]]))
        if h:
            rows(w_o, h - 1, 1)
    rows(w_o, HEADS_B - 1, 1)
    mlp(1)
    assert at[0] == UNITS
    return units


def _layout(v):
    f = lambda n: np.asarray(v[n], np.float32) if np.asarray(v[n]).dtype == np.float32 else np.asarray(v[n])
    d = {}
    d["wstream"] = _stream(f("w_in_a")[0], f("w_out_a")[0], f("w_up"), f("w_down"), f("w_kv"), f("w_q_b")[0], f("w_o_b")[0])
    x = np.concatenate([f("x_prompt")[0], f("x_sample")[:, 0]])
    d["xT"] = x.T.reshape(KD, P, T).transpose(1, 0, 2)

    def by_tile(w):
        t = w.reshape(*w.shape[:-1], CONV_DIM // P, P)
        order = [[2 * g, 2 * g + 1, 16 + g, 24 + g] for g in range(GROUPS)]
        t = t[..., np.array(order), :]
        return np.moveaxis(t, (-1, -3, -2), (0, 1, 2))

    par = np.zeros((P, GROUPS, 24), np.float32)
    par[:, :, 0:16] = by_tile(f("conv_w_a")[0]).reshape(P, GROUPS, 16)
    par[:, :, 16:20] = by_tile(f("conv_b_a")[0])
    par[:, :, 20:22] = np.repeat(f("d_skip_a")[0].reshape(GROUPS, 2, 2), 64, axis=2).transpose(2, 0, 1)
    par[:, :, 22:24] = f("norm_a")[0].reshape(GROUPS, 2, P).transpose(2, 0, 1)
    d["par"] = par
    d["sconv"] = by_tile(f("state_conv")[0]).transpose(0, 1, 2, 4, 3)
    d["conv_keep"] = f("state_conv")[0][:, 1:]
    d["state"] = f("state_ssm")[0].reshape(NB, 2 * GROUPS, P, P).transpose(2, 1, 0, 3)
    a32 = np.zeros((HEADS_A, 4), np.float32)
    a32[:, 0] = f("dt_bias_a")[0]
    a32[:, 1] = f("a_log_a")[0]
    d["a32"] = a32
    lnp = np.stack([f("ln_g").reshape(4, D), f("ln_b").reshape(4, D)], 1)
    d["lnp"] = lnp.reshape(4, 2, KD, P).transpose(3, 0, 1, 2)
    d["lamv"] = np.stack([f("lambda_q1_b")[0], f("lambda_q2_b")[0], f("lambda_k1_b")[0], f("lambda_k2_b")[0]])
    d["subg"] = f("subln_b")[0].reshape(P, 1)
    d["cache_k"] = f("cache_k").reshape(PHYS, P, D)
    d["cache_v"] = f("cache_v").reshape(PHYS, P, D)
    d["ptab"] = f("page_table").reshape(1, NB * PAGES).astype(np.int32)

    eye = np.eye(P, dtype=np.float32)
    d["ident"] = eye
    ones = np.zeros((P, 3, P), np.float32)
    ones[:, 0], ones[:, 1], ones[:, 2] = 1 / D, 1 / 256, 1 / P
    d["ones"] = ones
    d["row127"] = np.zeros((P, P), np.float32)
    d["row127"][P - 1] = 1
    i = np.arange(P)
    d["capm"] = np.where(i[None, :] >= i[:, None], 0, -1e30).astype(np.float32)
    scanm = np.ones((HEADS_A, T), np.float32)
    scanm[:, 0:SEQ:CHUNK] = 0
    scanm[:, SEQ:] = 0
    d["scanm"] = scanm
    sel = np.zeros((8, 6, P), np.float32)
    for r in range(R):
        sel[[r, R + r], r] = 1
        sel[[r, R + r], 4 + r // 2, 64 * (r % 2):64 * (r % 2) + 64] = 1
    d["sel"] = sel.reshape(8, 768)
    half = HD // 2
    inv = (np.float32(10000.0) ** (-np.arange(half, dtype=np.float32) / half)).astype(np.float32)
    pos = np.concatenate([np.arange(SEQ), np.full(NB, PAST)]).astype(np.float32)
    ang = inv[:, None] * pos[None, :]
    d["cos"] = np.tile(np.cos(ang).astype(np.float32), (4, 1))
    d["sin"] = np.tile(np.sin(ang).astype(np.float32), (4, 1))
    perm = np.zeros((P, P), np.float32)
    for m_ in range(P):
        if m_ % HD < half:
            perm[m_ + half, m_] = -1
        else:
            perm[m_ - half, m_] = 1
    d["perm"] = perm
    mbf = np.zeros((P, 2, P), mybir.dt.np(BF16))
    mbf[:, 0] = eye
    mbf[:, 1] = np.where(i[None, :] <= i[:, None], 0, -1e30)
    d["mbf"] = mbf
    hf = np.zeros((P, 2, NB), np.float32)
    hf[0:64, 0] = P
    hf[64:128, 1] = P
    d["half"] = hf
    pair = np.zeros((16, 12), np.float32)
    for r in range(16):
        pair[r, r % 8] = 1
        pair[r, 8 + r // 8] = 1
    d["pair"] = pair
    return {k: np.ascontiguousarray(w) for k, w in d.items()}


def kernel(**inputs):
    import concourse.bacc as _bacc
    from concourse.bass_utils import run_bass_kernel_spmd as _run

    nc = _bacc.Bacc("TRN2", target_bir_lowering=False, num_devices=1)
    arrays = {f"in_{k}": w for k, w in _layout(inputs).items()}
    a = {k[3:]: nc.dram_tensor(k, w.shape, mybir.dt.from_np(w.dtype), kind="ExternalInput").ap() for k, w in arrays.items()}
    o = {k: nc.dram_tensor(f"out_{k}", shape, F32, kind="ExternalOutput").ap() for k, shape in _OUT_SHAPES.items()}
    program(nc, a, o)
    r = _run(nc, [arrays], core_ids=[0]).results[0]
    g = {k: np.asarray(r[f"out_{k}"]) for k in _OUT_SHAPES}

    def tokens(t):
        return t.transpose(2, 1, 0).reshape(T, D)

    yt, kt, vt = tokens(g["yT"]), tokens(g["kT"]), tokens(g["vT"])
    new = np.zeros((CONV_DIM // P, P, 11), np.float32)
    for gr in range(GROUPS):
        for j, tile in enumerate((2 * gr, 2 * gr + 1, 16 + gr, 24 + gr)):
            new[tile] = g["conv_new"][:, gr, j]
    new = new.reshape(CONV_DIM, 11)
    conv_p = new[:, 0:3].T.reshape(1, 1, 3, CONV_DIM)
    conv_s = np.concatenate([g["conv_old"], new[:, 3:].T[:, None]], 1)[None]
    ssm_p = g["ssm_p"].reshape(P, HEADS_A, HD).transpose(1, 2, 0)[None, None]
    ssm_s = g["ssm_s"].reshape(2, HD, 16, NB, P).transpose(3, 2, 0, 1, 4).reshape(1, NB, HEADS_A, HD, P)
    c = np.ascontiguousarray
    return (c(yt[:SEQ][None]), c(yt[SEQ:][:, None]), c(conv_p), c(ssm_p),
            c(kt[:SEQ].reshape(1, SEQ, HEADS_B, 2, HD)), c(vt[:SEQ].reshape(1, SEQ, HEADS_B, 2 * HD)),
            c(conv_s), c(ssm_s),
            c(kt[SEQ:].reshape(NB, 1, HEADS_B, 2, HD)), c(vt[SEQ:].reshape(NB, 1, HEADS_B, 2 * HD)))
```

```python
import math
from contextlib import ExitStack

import numpy as np

import concourse.bass as bass
from concourse import mybir

F32 = mybir.dt.float32
F32R = mybir.dt.float32r
BF16 = mybir.dt.bfloat16
I32 = mybir.dt.int32
ALU = mybir.AluOpType
ACT = mybir.ActivationFunctionType
AX = mybir.AxisListType

P = 128
D = 1024
SEQ = 1024
NB = 8
T = SEQ + NB
NCH = 3
CW = T // NCH
KD = D // P
D_INNER = 2048
GN = 1024
HEADS_A = 32
GROUPS = 8
R = HEADS_A // GROUPS
CHUNK = 128
CHUNKS = SEQ // CHUNK
CONV_DIM = D_INNER + 2 * GN
CONV_W = 4
HEADS_B = 8
HD = 64
D_FF = 4096
PAST = 256
PAGES = PAST // P
PHYS = NB * PAGES * 5 // 4
ALPHA = 4.0 ** 0.25
EPS = 1e-5
LAM_INIT = 0.8 - 0.6 * math.exp(-0.3)
SCALE = HD ** -0.5
FFB = D_FF // 512

MIX_JOBS, MIX_UNITS = 4 + 8 + 2, 4 + 2 + 2
ATT_JOBS, ATT_UNITS = 3 + 8, 3 + 1
ATT_HEAD_JOBS, ATT_HEAD_UNITS = 5, 5
MLP_JOBS, MLP_UNITS = FFB * 12, FFB * 8
J_MIX, U_MIX = 1, 1
J_MLP0, U_MLP0 = J_MIX + GROUPS * MIX_JOBS, U_MIX + GROUPS * MIX_UNITS
J_ATT, U_ATT = J_MLP0 + MLP_JOBS, U_MLP0 + MLP_UNITS
J_MLP1, U_MLP1 = J_ATT + HEADS_B * ATT_JOBS, U_ATT + HEADS_B * ATT_UNITS
UNITS = U_MLP1 + MLP_UNITS
QK_FILL = {2: ((0, 0),), 3: ((0, 1),), 4: ((0, 2),), 5: ((1, 0),), 6: ((1, 1),), 7: ((1, 2),)}
Z_FILL_FIRST = {0: ((0, 0),), 1: ((0, 1),), 3: ((0, 2),), 5: ((1, 0),), 6: ((1, 1),), 7: ((1, 2),)}
Z_FILL = {3: ((0, 0),), 4: ((0, 1),), 5: ((0, 2),), 6: ((1, 0), (1, 1)), 7: ((1, 2),)}
S_STEP = 2
UP_ORDER = [(j, c) for j in range(4) for c in range(NCH)]
UP_ORDER_AFTER_NORM = [(j, c) for c in range(NCH) for j in range(2)] + UP_ORDER[6:]
N_CONST = 9
N_ATTC = 7
N_OUTS = 1 + NCH


def half_of(m):
    return slice(HD * m, HD * m + HD)


class Place:

    def __init__(self, job0, unit0, i=0, jobs=0, units=0):
        assert units % 2 == 0
        self.j, self.u = job0, unit0
        self.i, self.dj, self.du = i, jobs, units

    def job(self, n=1):
        j = self.i * self.dj + self.j
        self.j += n
        return j + 1, 3 * j

    def unit(self):
        u = self.u
        self.u += 1
        return u % 2, self.i * self.du + u + 1


def program(nc, a, o):
    with ExitStack() as ctx:
        def sb(name, shape, dt=F32, into=None):
            return (into or ctx).enter_context(nc.sbuf_tensor(name, shape, dt))

        def sem(name):
            return ctx.enter_context(nc.semaphore(name))

        xh = sb("xh", [P, KD, T], F32R)
        xl = sb("xl", [P, KD, T], F32R)
        acc = sb("acc", [P, KD, T])
        wraw = sb("wraw", [P, 2, 8, P])
        wh0 = sb("wh0", [P, 8, P], F32R)
        wh1 = sb("wh1", [P, 8, P], F32R)
        wl0 = sb("wl0", [P, 8, P], F32R)
        wl1 = sb("wl1", [P, 8, P], F32R)
        wh, wl = [wh0, wh1], [wl0, wl1]
        ident = sb("ident", [P, P])
        ones = sb("ones", [P, P + 2])
        lnp = sb("lnp", [P, 4, 2, KD])
        eps = sb("eps", [P, 1])
        one = sb("one", [P, 1])
        rstd = sb("rstd", [P, 2, 9])
        m = ctx.enter_context(ExitStack())
        yh = sb("yh", [P, 2, T], F32R, m)
        yl = sb("yl", [P, 2, T], F32R, m)
        xbc = sb("xbc", [P, 4, T], F32, m)
        zs = sb("zs", [P, 2, T], F32, m)
        y = sb("y", [P, 2, T], F32, m)
        pre = sb("pre", [P, 2, 4 + T], F32, m)
        csg = sb("csg", [8, T + NB], F32R, m)
        dm = sb("dm", [P, 2, 512], F32, m)
        bt = sb("bt", [P, P], F32, m)
        xs = sb("xs", [P, 256], F32, m)
        xe = sb("xe", [P, 256], F32, m)
        e2 = sb("e2", [P, 256], F32, m)
        tok = sb("tok", [P, 4, CHUNKS, HEADS_A], F32, m)
        tg = sb("tg", [P, 4, CHUNKS, R], F32, m)
        hst = sb("hst", [P, 256], F32, m)
        selh = sb("selh", [8, R, P], F32R, m)
        selt = sb("selt", [8, 2, P], F32R, m)
        capm = sb("capm", [P, P], F32, m)
        scv = sb("scv", [P, 4, 3, NB], F32, m)
        pall = sb("pall", [P, GROUPS, 24], F32, m)
        pg = sb("pg", [P, 24], F32, m)
        cnew = sb("cnew", [P, 4, 11], F32, m)
        dec = sb("dec", [P, 2, 8], F32, m)
        dts = sb("dts", [P, 2, 8], F32, m)
        xdt = sb("xdt", [P, 2, 8], F32, m)
        ct = sb("ct", [P, T], F32, m)
        st2 = sb("st2", [P, 512], F32, m)
        gn = sb("gn", [P, 2], F32, m)
        m.close()
        m = ctx.enter_context(ExitStack())
        dtx = sb("dtx", [HEADS_A, T + NB], F32, m)
        dtt = sb("dtt", [HEADS_A, T], F32, m)
        scanm = sb("scanm", [HEADS_A, T], F32, m)
        cs = sb("cs", [HEADS_A, T + NB], F32, m)
        csh = sb("csh", [HEADS_A, T + NB], F32R, m)
        csl = sb("csl", [HEADS_A, T + NB], F32R, m)
        a32 = sb("a32", [HEADS_A, 4], F32, m)
        row127 = sb("row127", [P, P], F32, m)
        m.close()
        m = ctx.enter_context(ExitStack())
        mk = m.enter_context(ExitStack())
        raw_k = sb("raw_k", [P, T], F32, mk)
        mk.close()
        ah = sb("ah", [P, 1, T], F32R, m)
        al = sb("al", [P, 1, T], F32R, m)
        ob = sb("ob", [P, T], F32, m)
        q2 = [sb(f"q2{i}", [P, SEQ], F32R, m) for i in range(2)]
        k2h = [sb(f"k2h{i}", [P, SEQ], F32R, m) for i in range(2)]
        k2l = [sb(f"k2l{i}", [P, SEQ], F32R, m) for i in range(2)]
        raw = sb("raw", [P, T], F32, m)
        rot = sb("rot", [P, T], F32, m)
        cos = sb("cos", [P, T], F32, m)
        sin = sb("sin", [P, T], F32, m)
        pp = sb("pp", [P, 2048], F32, m)
        wt = sb("wt", [P, KD, 2, P], F32R, m)
        vth = sb("vth", [P, KD, P], F32R, m)
        vtl = sb("vtl", [P, KD, P], F32R, m)
        past = sb("past", [P, NB * PAGES, P], F32, m)
        perm = sb("perm", [P, P], F32, m)
        mbf = sb("mbf", [P, 2, P], BF16, m)
        lam = sb("lam", [P, 4], F32, m)
        subg = sb("subg", [P, 1], F32, m)
        pair = sb("pair", [16, 12], F32, m)
        smp = sb("smp", [P, 3, NB], F32, m)
        qkn = sb("qkn", [P, 2, NB], F32, m)
        st = sb("st", [P, 8], F32, m)
        lamv = pp[:, 0:4 * HD].rearrange("p (a d) -> p a d", a=4)
        srow = pp[0:16]
        ssc = sb("ssc", [P, PAGES, 2, NB], F32, m)
        wsm = ssc[:].rearrange("p g m b -> p (g m) b")[:, 0:3]
        m.close()
        m = ctx.enter_context(ExitStack())
        hh = [sb(f"hh{b}", [P, 4, T], F32R, m) for b in range(2)]
        hl = [sb(f"hl{b}", [P, 4, T], F32R, m) for b in range(2)]
        rl = sb("rl", [P, 4, CW], F32, m)
        ln0 = sb("ln0", [P, T], F32, m)
        m.close()
        m = ctx.enter_context(ExitStack())
        lnq = sb("lnq", [P, 2, KD, CW], F32, m)
        m.close()

        jb = ctx.enter_context(nc.psum_tensor("jb", [P, NCH, 512], F32))
        aux = ctx.enter_context(nc.psum_tensor("aux", [P, 5, 512], F32))

        csd = nc.dram_tensor("csd", [2, HEADS_A, T + NB], F32, kind="Internal").ap()
        kgat = nc.dram_tensor("kgat", [NB * PAGES, P, D], F32, kind="Internal").ap()
        vgat = nc.dram_tensor("vgat", [NB * PAGES, P, D], F32, kind="Internal").ap()

        raw_in = [sem("raw_in0"), sem("raw_in1")]
        x_in = [sem(f"x_in{k}") for k in range(KD)]
        w_split = sem("w_split")
        unit_begun = sem("unit_begun")
        chunk_full = sem("chunk_full")
        bank_free = [sem(f"bank_free{c}") for c in range(NCH)]
        names = """const_in attc_in x_hi x_ready outs gathered dt_raw dt_abs dt_exp dt_soft cs_hi cs_lo cs_stored tok_ps
            tok_cp end_ps cd_done dte_arg dte_exp tok_done sel_done pg_ready csg_in scv_in cnew_out pre_full
            conv_done tanh_done xbc_done z_full z_done bc_full bc_used a_hi a_lo h_zero ssd_in ssd_off ssd_b
            bt_ready xs_ready xe_ready e2_ready d_ready e_ready m_ready h_done h_out s_in bcs_full dec_ready
            s_new s_out yg_ready sq_done sq_sum rms_full rms_sqrt rms_inv rms_scale yn_ready y_hi y_lo relu_done
            h_sq h_ready ln_sum ln_mu ln_cent ln_sq ln_add ln_var ln_std ln_inv ln_scale ln_norm ln_hi ln_lo
            lam_sum lam_exp raw_full perm_full rope_done qk_hi k_low k_twin k_out raw_v vt_ps vt_hi vt_ready
            v_out s_full nmax_ready p_ready w_ready wt_ps wt_hi wt_ready pv_full o_half o_ready qb_full pk_in
            ssc_ready srow_full snm_ready sexp_ready sp_ready wsm_full wsm_ready pv_in so_full o_smp osq_done
            orms_full orms_sqrt orms_inv orms_scale on_ready""".split()
        s = {n: sem(n) for n in names}

        block = ctx.enter_context(nc.Block())

        @block.sync
        def _(sp):
            def constants():
                for dst, name in ((ident, "ident"), (ones, "ones"), (lnp, "lnp"), (row127, "row127"),
                                  (capm, "capm"), (pall, "par"), (a32, "a32"), (scanm, "scanm")):
                    sp.dma_start(dst[:], a[name]).then_inc(s["const_in"], 16)
                sp.dma_start(pre[0:8, 0, 4:772], a["sel"]).then_inc(s["const_in"], 16)

            for k in range(KD):
                if k < 2:
                    sp.dma_start(wraw[:, k], a["wstream"][k]).then_inc(raw_in[k], 16)
                sp.dma_start(acc[:, k], a["xT"][:, k]).then_inc(x_in[k], 16)
                if k == 1:
                    constants()
            pages = [sp.value_load(a["ptab"][0:1, k:k + 1], min_val=0, max_val=PHYS - 1) for k in range(NB * PAGES)]
            for k, page in enumerate(pages):
                sp.wait_ge(w_split, k + 1)
                sp.dma_start(wraw[:, k % 2], a["wstream"][k + 2]).then_inc(raw_in[k % 2], 16)
                for gathered, cache in ((kgat, a["cache_k"]), (vgat, a["cache_v"])):
                    sp.dma_start(gathered[k], cache[bass.ds(page, 1)].rearrange("a p d -> (a p) d")).then_inc(s["gathered"], 16)
            with sp.Fori(NB * PAGES // 2, (UNITS - 3) // 2) as i:
                for k in range(2):
                    sp.wait_ge(w_split, 2 * i + k + 1)
                    sp.dma_start(wraw[:, k], a["wstream"][2 * i + (k + 2)]).then_inc(raw_in[k], 16)
            sp.wait_ge(w_split, UNITS - 2)
            sp.dma_start(wraw[:, 0], a["wstream"][UNITS - 1]).then_inc(raw_in[0], 16)
            sp.wait_ge(s["outs"], 16 * N_OUTS)

        @block.gpsimd
        def _(pool):
            def split(slot, loaded, begun):
                pool.wait_ge(raw_in[slot], loaded)
                if begun is not None:
                    pool.wait_ge(unit_begun, begun)
                nc.gpsimd.tensor_tensor(wh[slot][:].rearrange("p k m -> p (k m)"), wraw[:, slot].rearrange("p k m -> p (k m)"),
                                        one[:].to_broadcast([P, 8 * P]), ALU.mult)
                pool.drain()
                nc.gpsimd.tensor_tensor(wl[slot][:], wraw[:, slot], wh[slot][:].bitcast(F32),
                                        ALU.subtract).then_inc(w_split, 1)

            nc.gpsimd.memset(one[:], 1.0)
            pool.drain()
            split(0, 16, None)
            split(1, 16, None)
            with pool.Fori(1, (UNITS - 1) // 2) as i:
                split(0, 16 * i + 16, 2 * i)
                split(1, 16 * i + 16, 2 * i + 1)
            split(0, 16 * ((UNITS - 1) // 2) + 16, UNITS - 1)

        @block.tensor
        def _(pe):
            mm = nc.tensor.matmul

            def chunk_of(place, c, j, kt, rh, rlo):
                slot, credits, _ = place
                pe.wait_ge(bank_free[c], credits)
                cols = slice(c * CW, (c + 1) * CW)
                for k in range(kt):
                    for w, x, p in ((wh, rh, 0), (wh, rlo, 1), (wl, rh, 2)):
                        last = mm(jb[:, c, 0:CW], w[slot][:, j * kt + k], x[:, k, cols],
                                  start=(k == 0 and p == 0), stop=(k == kt - 1 and p == 2))
                        if c == 0 and j == 0 and k == 0 and p == 0:
                            last.then_inc(unit_begun, 1)
                last.then_inc(chunk_full, 1)

            def unit(at):
                slot, nth = at.unit()
                pe.wait_ge(w_split, nth)
                return slot

            def jobs(at, n, kt, rh, rlo):
                for j in range(n):
                    if (j * kt) % 8 == 0:
                        slot = unit(at)
                    credits, done = at.job()
                    for c in range(NCH):
                        chunk_of((slot, credits, done), c, j % (8 // kt), kt, rh, rlo)

            slot = unit(Place(0, 0))
            for k in range(KD):
                pe.wait_ge(s["x_ready"], k + 1)
                for c in range(NCH):
                    if k == 0:
                        pe.wait_ge(bank_free[c], 1)
                    for w, x, p in ((wh, xh, 0), (wh, xl, 1), (wl, xh, 2)):
                        last = mm(jb[:, c, 0:CW], w[slot][:, k], x[:, k, c * CW:(c + 1) * CW],
                                  start=(k == 0 and p == 0), stop=(k == KD - 1 and p == 2))
                        if k == 0 and c == 0 and p == 0:
                            last.then_inc(unit_begun, 1)
                    if k == KD - 1:
                        last.then_inc(chunk_full, 1)

            def dt_by_token():
                pe.wait_ge(s["const_in"], 16 * N_CONST)
                pe.wait_ge(s["sel_done"], 1)
                pe.wait_ge(s["cs_hi"], 1)
                for k, src in enumerate((cs, dtx)):
                    for c in range(CHUNKS):
                        last = nc.tensor.transpose(aux[:, 0, (k * CHUNKS + c) * HEADS_A:(k * CHUNKS + c + 1) * HEADS_A],
                                                   src[:, c * CHUNK:(c + 1) * CHUNK], ident[0:HEADS_A, 0:HEADS_A])
                last.then_inc(s["tok_ps"], 1)
                pe.wait_ge(s["tok_cp"], 1)
                mm(aux[:, 1, 0:256], row127[:], tok[:, 0].rearrange("p c h -> p (c h)"), start=True,
                   stop=True).then_inc(s["end_ps"], 1)

            def rms_sums(p, full, summed, src, k):
                pe.wait_ge(s[summed], p + 1)
                for b in range(9):
                    t0 = min(b * P, T - P)
                    last = mm(aux[:, 0, b:b + 1], src[:, t0:t0 + P], ones[:, P + k:P + k + 1], start=True, stop=True)
                last.then_inc(s[full], 1)

            def rms_spread(p, scale, inv):
                pe.wait_ge(s[inv], p + 1)
                for b in range(9):
                    first = 0 if b < 8 else P - NB
                    last = mm(aux[:, b // 4, (b % 4) * P:(b % 4) * P + P - first],
                              rstd[:, 1, b:b + 1].to_broadcast([P, P]), ident[:, first:P], start=True, stop=True)
                last.then_inc(s[scale], 1)

            def project_group(at, n, fin):
                jobs(at, 1, KD, xh, xl)
                if not fin:
                    dt_by_token()
                if fin:
                    rms_sums(n - 1, "rms_full", "sq_sum", zs[:, 0], 0)
                jobs(at, 1, KD, xh, xl)
                if fin:
                    rms_spread(n - 1, "rms_scale", "rms_inv")
                jobs(at, 2, KD, xh, xl)

            def scan_group(at, n, out):
                if out:
                    pe.wait_ge(s["y_lo"], 2 * n)
                    slot = unit(at)
                outs = []

                def out_jobs(first):
                    for j in (first, first + 1):
                        if j == 4:
                            outs.append(unit(at))
                        sl = outs[0] if outs else slot
                        credits, done = at.job()
                        for c in range(NCH):
                            chunk_of((sl, credits, done), c, j % 4, 2, yh, yl)

                if out:
                    out_jobs(0)
                pe.wait_ge(s["xbc_done"], 4 * n + 4)
                pe.wait_ge(s["csg_in"], 32 * n + 32)
                for c in range(CHUNKS):
                    cols = slice(c * CHUNK, (c + 1) * CHUNK)
                    nc.tensor.transpose(aux[:, 0, 0:128], xbc[:, 0, cols], ident[:])
                    nc.tensor.transpose(aux[:, 0, 128:256], xbc[:, 1, cols], ident[:])
                    mm(aux[:, 2, 384:512], xbc[:, 2, cols], xbc[:, 3, cols], start=True, stop=True)
                    for r in range(R):
                        mm(aux[:, 1, r * 128:(r + 1) * 128], selh[:, r], csg[:, cols], start=True, stop=True)
                    for t in range(2):
                        mm(aux[:, 2, t * 128:128 + t * 128], selt[:, t], csg[:, cols], start=True, stop=True)
                    nc.tensor.transpose(aux[:, 2, 256:384], xbc[:, 2, cols], ident[:]).then_inc(s["ssd_in"], 1)
                    if c:
                        pe.wait_ge(s["h_done"], 8 * n + c)
                    else:
                        pe.wait_ge(s["h_zero"], n + 1)
                    for t in range(2):
                        last = mm(aux[:, 3, t * 128:128 + t * 128], hst[:, t * 128:(t + 1) * 128],
                                  xbc[:, 3, cols], start=True, stop=True)
                    last.then_inc(s["ssd_off"], 1)
                    if out and c < 3:
                        out_jobs(2 + 2 * c)
                    for t, zc in (Z_FILL if out else Z_FILL_FIRST).get(c, ()):
                        if zc == 0:
                            zp = (unit(at), *at.job())
                        chunk_of(zp, zc, 0, KD, xh, xl)
                    pe.wait_ge(s["m_ready"], 8 * n + c + 1)
                    pe.wait_ge(s["xs_ready"], 8 * n + c + 1)
                    for r in range(R):
                        half_ = slice(64 * (r % 2), 64 * (r % 2) + 64)
                        mm(aux[half_, 3, (r // 2) * 128:(r // 2) * 128 + 128], xs[:, r * 64:(r + 1) * 64],
                           dm[:, 1, r * 128:(r + 1) * 128], start=True, stop=True)
                    pe.wait_ge(s["bt_ready"], 8 * n + c + 1)
                    pe.wait_ge(s["xe_ready"], 8 * n + c + 1)
                    mm(aux[:, 3, 256:512], bt[:], xe[:], start=True, stop=True).then_inc(s["ssd_b"], 1)
                    if c == S_STEP:
                        for t in range(2):
                            last = mm(aux[:, 4, t * 16:t * 16 + 16], selt[:, t], csg[:, SEQ:SEQ + 16], start=True, stop=True)
                        last.then_inc(s["bcs_full"], 1)
                    if S_STEP < c <= S_STEP + 4:
                        k = c - S_STEP - 1
                        if k:
                            pe.wait_ge(s["bc_used"], 4 * n + k)
                        else:
                            pe.wait_ge(s["dec_ready"], n + 1)
                        for b in range(4):
                            col = SEQ + 4 * (k // 2) + b
                            last = mm(aux[:, 4, b * 128:(b + 1) * 128], xbc[:, 2 + k % 2, col:col + 1].to_broadcast([P, P]),
                                      ident[:], start=True, stop=True)
                        last.then_inc(s["bc_full"], 1)

            at = Place(J_MIX, U_MIX)
            project_group(at, 0, False)
            scan_group(at, 0, False)
            with pe.Fori(1, GROUPS) as n:
                at = Place(J_MIX + 6 - MIX_JOBS, U_MIX + 6 - MIX_UNITS, n, MIX_JOBS, MIX_UNITS)
                project_group(at, n, True)
                scan_group(at, n, True)
            rms_sums(GROUPS - 1, "rms_full", "sq_sum", zs[:, 0], 0)
            rms_spread(GROUPS - 1, "rms_scale", "rms_inv")
            pe.wait_ge(s["y_lo"], 2 * GROUPS)
            jobs(Place(J_MLP0 - 8, U_MLP0 - 2), 8, 2, yh, yl)

            blocks = ((0, 0), (P, 0), (CW - P, 3 * P - CW))

            def layer_norm(l):
                for c in range(NCH):
                    pe.wait_ge(s["ln_sum"], 3 * l + c + 1)
                    mm(aux[:, c, 0:CW], ones[:, 0:P], ln0[:, c * CW:(c + 1) * CW], start=True, stop=True).then_inc(s["ln_mu"], 1)

                def variance(c):
                    pe.wait_ge(s["ln_add"], 3 * l + c + 1)
                    for b, (t0, _) in enumerate(blocks):
                        for k in range(4):
                            last = mm(aux[:, c, 500 + b:501 + b], lnq[:, c % 2, k, t0:t0 + P], ones[:, 0:1],
                                      start=(k == 0), stop=(k == 3))
                    last.then_inc(s["ln_var"], 1)

                def spread(c):
                    pe.wait_ge(s["ln_inv"], 3 * l + c + 1)
                    for b, (t0, skip) in enumerate(blocks):
                        last = mm(aux[:, c, t0 + skip:t0 + P], rstd[:, 1, 3 * c + b:3 * c + b + 1].to_broadcast([P, P]),
                                  ident[:, skip:P], start=True, stop=True)
                    last.then_inc(s["ln_scale"], 1)

                variance(0)
                spread(0)
                variance(1)
                spread(1)
                variance(2)
                spread(2)

            def jobs_after_norm(at, l):
                slots = []
                credits, _ = at.job(2)
                for c in range(NCH):
                    pe.wait_ge(s["ln_lo"], 3 * l + c + 1)
                    for j in range(2):
                        if c == 0:
                            slots.append(unit(at))
                        slot = slots[j]
                        bank = (2 * c + j) % 3
                        pe.wait_ge(bank_free[bank], credits + (2 * c + j) // 3)
                        cols = slice(c * CW, (c + 1) * CW)
                        for k in range(KD):
                            for w, x, p in ((wh, xh, 0), (wh, xl, 1), (wl, xh, 2)):
                                last = mm(jb[:, bank, 0:CW], w[slot][:, k], x[:, k, cols],
                                          start=(k == 0 and p == 0), stop=(k == KD - 1 and p == 2))
                                if k == 0 and p == 0 and (c, j) in ((0, 0), (2, 1)):
                                    last.then_inc(unit_begun, 1)
                        last.then_inc(chunk_full, 1)

            def mlp(layer):
                j0, u0 = ((J_MLP0, U_MLP0), (J_MLP1, U_MLP1))[layer]
                hb = layer * FFB

                def up(at):
                    jobs(at, 4, KD, xh, xl)

                def down(at, b, nth):
                    pe.wait_ge(s["h_ready"], nth)
                    jobs(at, 8, 4, hh[b], hl[b])

                at = Place(j0, u0)
                jobs_after_norm(at, 2 * layer)
                jobs(at, 2, KD, xh, xl)
                with pe.Fori(0, FFB // 2 - 1) as i:
                    at = Place(j0 + 4, u0 + 4, i, 24, 16)
                    up(at)
                    down(at, 0, (hb + 2 * i) * 12 + 12)
                    up(at)
                    down(at, 1, (hb + 2 * i) * 12 + 24)
                at = Place(j0 + 4 + 24 * (FFB // 2 - 1), u0 + 4 + 16 * (FFB // 2 - 1))
                up(at)
                down(at, 0, (hb + FFB - 1) * 12)
                down(at, 1, (hb + FFB) * 12)

            layer_norm(0)
            mlp(0)
            layer_norm(1)

            def perm_of(nth, src):
                pe.wait_ge(s["raw_full"], nth)
                for c in range(NCH):
                    last = mm(aux[:, 2 + c, 0:CW], perm[:], src[:, c * CW:(c + 1) * CW], start=True, stop=True)
                last.then_inc(s["perm_full"], 1)

            def project_head(at, n, new, fin):
                p = n - 1
                if fin:
                    for b in range(NB):
                        last = mm(aux[:, b // 4, (b % 4) * 128:(b % 4) * 128 + 128],
                                  smp[:, 0, b:b + 1].to_broadcast([P, P]), ident[:], start=True, stop=True)
                    last.then_inc(s["qb_full"], 1)
                if new:
                    perm_of(2 * n + 1, raw)
                    vp = (unit(at), *at.job())
                    chunk_of(vp, 0, 0, KD, xh, xl)
                if fin:
                    pe.wait_ge(s["ssc_ready"], p + 1)
                    mm(aux[0:16, 0, 256:257], qkn[:].rearrange("p m b -> p (m b)"), one[:], start=True, stop=True)
                    for g in range(PAGES):
                        last = nc.tensor.transpose(aux[0:16, 0, g * 128:(g + 1) * 128],
                                                   ssc[:, g].rearrange("p m b -> p (m b)"), ident[:])
                    last.then_inc(s["srow_full"], 1)
                if new:
                    chunk_of(vp, 1, 0, KD, xh, xl)
                    pe.wait_ge(s["rope_done"], 2 * n + 1)
                    perm_of(2 * n + 2, raw_k)
                    chunk_of(vp, 2, 0, KD, xh, xl)
                if fin:
                    pe.wait_ge(s["sp_ready"], p + 1)
                    for g in range(PAGES):
                        mm(aux[:, 1, g * 8:g * 8 + 8], srow[0:16, g * 128:(g + 1) * 128], pair[0:16, 0:8], start=True, stop=True)
                    mm(aux[:, 1, 16:24], srow[0:16, 256:257].to_broadcast([16, P]), pair[0:16, 0:8], start=True,
                       stop=True).then_inc(s["wsm_full"], 1)
                    pe.wait_ge(s["wsm_ready"], p + 1)
                    pe.wait_ge(s["pv_in"], 16 * p + 16)
                    for b in range(NB):
                        for g in range(PAGES):
                            last = mm(aux[:, 1, 32 + b:33 + b], past[:, b * PAGES + g], wsm[:, g, b:b + 1],
                                      start=(g == 0), stop=(g == PAGES - 1))
                    last.then_inc(s["so_full"], 1)
                if fin:
                    rms_sums(p, "orms_full", "osq_done", pp, 1)
                if new:
                    pe.wait_ge(s["raw_v"], n + 1)
                    pe.wait_ge(s["rope_done"], 2 * n + 2)
                    for c in range(8):
                        last = nc.tensor.transpose(aux[:, 3 + c // 4, (c % 4) * 128:(c % 4) * 128 + 128],
                                                   raw[:, c * 128:(c + 1) * 128], ident[:])
                    last.then_inc(s["vt_ps"], 1)
                if fin:
                    rms_spread(p, "orms_scale", "orms_inv")
                if fin:
                    slot = unit(at)
                    place = (slot, *at.job())
                    for c in range(NCH):
                        pe.wait_ge(s["a_lo"], 3 * p + c + 1)
                        chunk_of(place, c, 0, 1, ah, al)
                    for j in range(1, KD):
                        place = (slot, *at.job())
                        for c in range(NCH):
                            chunk_of(place, c, j, 1, ah, al)

            def attend(at, n, ahead):
                def scores(i):
                    rows = slice(i * 128, (i + 1) * 128)
                    width = (i + 1) * 128
                    for m_ in range(2):
                        if i == 0 and m_ == 0:
                            pe.wait_ge(s["k_twin"], 64 * n + 64)
                        if i:
                            pe.wait_ge(s["p_ready"], 16 * n + 2 * i + m_ - 1)
                        for c0 in range(0, width, 512):
                            w = min(512, width - c0)
                            out = aux[:, 2 * m_ + c0 // 512, 0:w]
                            diag = c0 + w == width
                            for p, kk in enumerate((k2h, k2l)):
                                last = mm(out, q2[m_][:, rows], kk[m_][:, c0:c0 + w], start=(p == 0),
                                          stop=(p == 1 and not diag))
                            if diag:
                                last = mm(aux[:, 2 * m_ + c0 // 512, w - 128:w], mbf[:, 0], mbf[:, 1],
                                          start=False, stop=True)
                        last.then_inc(s["s_full"], 1)

                def turn(i):
                    pe.wait_ge(s["w_ready"], 8 * n + i + 1)
                    for k in range(i + 1):
                        last = nc.tensor.transpose(jb[:, k // 4, (k % 4) * 128:(k % 4) * 128 + 128],
                                                   pp[:, k * 128:(k + 1) * 128], ident[:])
                    last.then_inc(s["wt_ps"], 1)

                def values(i):
                    pe.wait_ge(s["wt_ready"], 8 * n + i + 1)
                    for k in range(i + 1):
                        for p, vv in enumerate((vth, vtl)):
                            last = mm(aux[:, 4, 0:256], vv[:, k], wt[:, k].rearrange("p a b -> p (a b)"),
                                      start=(k == 0 and p == 0), stop=(k == i and p == 1))
                    last.then_inc(s["pv_full"], 1)

                def fill(place, c):
                    slot, credits, _ = place
                    pe.wait_ge(bank_free[(c - 1) % NCH], credits + (c > 0))
                    for k in range(KD):
                        for w, x, p in ((wh, xh, 0), (wh, xl, 1), (wl, xh, 2)):
                            last = mm(jb[:, 2, 0:CW], w[slot][:, k], x[:, k, c * CW:(c + 1) * CW],
                                      start=(k == 0 and p == 0), stop=(k == KD - 1 and p == 2))
                            if c == 0 and k == 0 and p == 0:
                                last.then_inc(unit_begun, 1)
                    last.then_inc(chunk_full, 1)

                pe.wait_ge(s["vt_ready"], n + 1)
                scores(0)
                for i in range(8):
                    if ahead:
                        for j, c in QK_FILL.get(i, ()):
                            if c == 0:
                                place = (unit(at), *at.job())
                            fill(place, c)
                    if i < 7:
                        scores(i + 1)
                    if i:
                        values(i - 1)
                    turn(i)
                values(7)
                pe.wait_ge(s["o_ready"], 8 * n + 8)

            at = Place(J_ATT, U_ATT)
            jobs_after_norm(at, 1)
            pe.wait_ge(s["attc_in"], 16 * N_ATTC)
            project_head(at, 0, True, False)
            attend(at, 0, True)
            at0 = J_ATT + ATT_HEAD_JOBS - ATT_JOBS, U_ATT + ATT_HEAD_UNITS - ATT_UNITS
            with pe.Fori(1, HEADS_B - 1) as n:
                at = Place(*at0, n, ATT_JOBS, ATT_UNITS)
                project_head(at, n, True, True)
                attend(at, n, True)
            at = Place(*at0, HEADS_B - 1, ATT_JOBS, ATT_UNITS)
            project_head(at, HEADS_B - 1, True, True)
            attend(at, HEADS_B - 1, False)
            project_head(Place(J_MLP1 - 8, U_MLP1 - 1), HEADS_B, False, True)

            layer_norm(2)
            mlp(1)
            layer_norm(3)

        @block.scalar
        def _(act):
            af = nc.scalar.activation

            for b in range(NCH):
                act.sem_inc(bank_free[b], 1)
            for k in range(KD):
                act.wait_ge(x_in[k], 16)
                af(xh[:, k], acc[:, k], ACT.Copy).then_inc(s["x_hi"], 1)
            act.dma_start(o["conv_old"], a["conv_keep"]).then_inc(s["outs"], 16)
            act.wait_ge(s["const_in"], 16 * N_CONST)
            af(selh[:], pre[0:8, 0, 4:516].rearrange("p (r c) -> p r c", r=R), ACT.Copy)
            af(selt[:], pre[0:8, 0, 516:772].rearrange("p (r c) -> p r c", r=2), ACT.Copy).then_inc(s["sel_done"], 1)

            for c in range(NCH):
                act.wait_ge(chunk_full, c + 1)
                last = af(dtx[:, c * CW:(c + 1) * CW], jb[0:HEADS_A, c, 0:CW], ACT.Identity, bias=a32[:, 0:1])
                last.then_inc(bank_free[c], 1)
            af(a32[:, 2:3], a32[:, 1:2], ACT.Exp).then_inc(s["dt_raw"], 1)
            act.wait_ge(s["dt_abs"], 1)
            af(dtt[:], dtt[:], ACT.Exp, scale=-1.0)
            act.drain()
            af(dtt[:], dtt[:], ACT.Ln, bias=1.0).then_inc(s["dt_exp"], 1)
            act.wait_ge(s["dt_soft"], 1)
            af(csh[:], cs[:], ACT.Copy).then_inc(s["cs_hi"], 1)
            act.wait_ge(s["tok_ps"], 1)
            af(tok[:, 0:2], aux[:, 0].rearrange("p (k c h) -> p k c h", k=2, c=CHUNKS), ACT.Copy).then_inc(s["tok_cp"], 1)
            act.wait_ge(s["end_ps"], 1)
            af(tok[:, 3], aux[:, 1, 0:256].rearrange("p (c h) -> p c h", c=CHUNKS), ACT.Exp).then_inc(s["cd_done"], 1)
            act.wait_ge(s["dte_arg"], 1)
            af(tok[:, 2], tok[:, 2], ACT.Exp).then_inc(s["dte_exp"], 1)
            act.wait_ge(s["cs_lo"], 1)
            act.dma_start(csd[0], csh[:].bitcast(F32)).then_inc(s["cs_stored"], 16)
            act.dma_start(csd[1], csl[:].bitcast(F32)).then_inc(s["cs_stored"], 16)

            def take(c, done, dst, func, **kw):
                act.wait_ge(chunk_full, done + c + 1)
                af(dst, jb[:, c, 0:CW], func, **kw).then_inc(bank_free[c], 1)

            def norm_sums(p):
                for t in range(2):
                    act.wait_ge(s["yg_ready"], 2 * p + t + 1)
                    af(zs[:, t], y[:, t], ACT.Square).then_inc(s["sq_done"], 1)

            def norm_root(p):
                act.wait_ge(s["rms_full"], p + 1)
                af(rstd[:, 0], aux[:, 0, 0:9], ACT.Sqrt, bias=eps[:]).then_inc(s["rms_sqrt"], 1)

            def norm_hi(p):
                for t in range(2):
                    act.wait_ge(s["yn_ready"], 2 * p + t + 1)
                    af(yh[:, t], y[:, t], ACT.Copy).then_inc(s["y_hi"], 1)

            def load_sums(n):
                for k in range(2):
                    act.dma_start(csg[4 * k:4 * k + 4].bitcast(F32), csd[k, bass.ds(n * R, R)]).then_inc(s["csg_in"], 16)

            def project_group(at, n, fin):
                if fin:
                    norm_sums(n - 1)
                    act.wait_ge(s["ssd_b"], 8 * n)
                    act.wait_ge(s["s_out"], 32 * n)
                    load_sums(n)
                act.dma_start(scv[:], a["sconv"][:, bass.ds(n, 1)].rearrange("p a t k b -> p (a t) k b")).then_inc(s["scv_in"], 16)
                act.wait_ge(s["pg_ready"], n + 1)
                for t in range(4):
                    _, done = at.job()
                    if t:
                        act.wait_ge(s["xbc_done"], 4 * n + t)
                    for c in range(NCH):
                        act.wait_ge(chunk_full, done + c + 1)
                        af(ct[:, c * CW:(c + 1) * CW], jb[:, c, 0:CW], ACT.Identity, scale=pg[:, 4 * t + 3:4 * t + 4],
                           bias=pg[:, 16 + t:17 + t])
                        take(c, done, pre[:, t % 2, 4 + c * CW:4 + (c + 1) * CW], ACT.Copy)
                    act.drain()
                    if t == 0 and fin:
                        act.wait_ge(s["cnew_out"], 16 * n)
                    af(cnew[:, t], pre[:, t % 2, 4 + SEQ - 3:4 + T], ACT.Copy).then_inc(s["pre_full"], 1)
                    if t == 0 and fin:
                        norm_root(n - 1)
                    if t == 0 and not fin:
                        act.wait_ge(s["cs_stored"], 32)
                        load_sums(n)
                    act.wait_ge(s["conv_done"], 4 * n + t + 1)
                    af(pre[:, t % 2, 4:4 + T], ct[:], ACT.Tanh).then_inc(s["tanh_done"], 1)
                    if t == 1 and fin:
                        norm_hi(n - 1)
                act.wait_ge(s["pre_full"], 4 * n + 4)
                act.dma_start(o["conv_new"][:, bass.ds(n, 1)].rearrange("p a t k -> p (a t) k"), cnew[:]).then_inc(s["cnew_out"], 16)

            def scan_group(at, n, out):
                if out:
                    at.job(8)
                act.wait_ge(s["xbc_done"], 4 * n + 4)
                for t in range(2):
                    act.dma_start(pre[:, t, 4:4 + SEQ].rearrange("p (b n) -> p b n", b=NB),
                                  a["state"][:, bass.ds(2 * n + t, 1)].rearrange("p a b n -> p (a b) n")).then_inc(s["s_in"], 16)
                for c in range(CHUNKS):
                    x = 8 * n + c
                    act.wait_ge(s["ssd_in"], x + 1)
                    af(e2[:], aux[:, 2, 0:256], ACT.Exp).then_inc(s["e2_ready"], 1)
                    af(bt[:], aux[:, 2, 256:384], ACT.Copy).then_inc(s["bt_ready"], 1)
                    act.wait_ge(s["d_ready"], x + 1)
                    af(dm[:, 0], dm[:, 0], ACT.Exp).then_inc(s["e_ready"], 1)
                    if c == 0:
                        act.wait_ge(s["h_zero"], n + 1)
                    for k, (dst, done_) in enumerate(((xs, "xs_ready"), (xe, "xe_ready"))):
                        for r in range(R):
                            hc = slice(r * HD, (r + 1) * HD)
                            last = af(dst[:, hc], aux[:, 0, hc], ACT.Copy, scale=tg[:, 1 + k, c, r:r + 1])
                        last.then_inc(s[done_], 1)
                    for t, zc in (Z_FILL if out else Z_FILL_FIRST).get(c, ()):
                        if zc == 0:
                            _, done = at.job()
                            if t:
                                act.wait_ge(s["z_done"], 2 * n + 1)
                            elif out:
                                act.wait_ge(s["y_lo"], 2 * n)
                        cols = slice(zc * CW, (zc + 1) * CW)
                        act.wait_ge(chunk_full, done + zc + 1)
                        af(ct[:, cols], jb[:, zc, 0:CW], ACT.Tanh, scale=0.5)
                        take(zc, done, zs[:, t, cols], ACT.Copy, scale=0.5)
                        if zc == 2:
                            act.drain().then_inc(s["z_full"], 1)
                    if c == S_STEP:
                        act.wait_ge(s["bcs_full"], n + 1)
                        v = aux[:, 4, 0:32].rearrange("p (t c) -> p t c", t=2)
                        af(dec[:], v[:, :, 0:8], ACT.Exp)
                        af(dts[:], v[:, :, 8:16], ACT.Copy).then_inc(s["dec_ready"], 1)
                    if c == 7:
                        act.wait_ge(s["s_new"], n + 1)
                        for t in range(2):
                            act.dma_start(o["ssm_s"][:, bass.ds(2 * n + t, 1)].rearrange("p a b n -> p (a b) n"),
                                          pre[:, t, 4:4 + SEQ].rearrange("p (b n) -> p b n", b=NB)).then_inc(s["s_out"], 16)
                act.wait_ge(s["h_done"], 8 * n + 8)
                act.dma_start(o["ssm_p"][:, bass.ds(n, 1)].rearrange("p a q -> p (a q)"), hst[:]).then_inc(s["h_out"], 16)

            at = Place(J_MIX, U_MIX)
            project_group(at, 0, False)
            scan_group(at, 0, False)
            with act.Fori(1, GROUPS) as n:
                at = Place(J_MIX + 6 - MIX_JOBS, 0, n, MIX_JOBS, 0)
                project_group(at, n, True)
                scan_group(at, n, True)
            norm_sums(GROUPS - 1)
            norm_root(GROUPS - 1)
            norm_hi(GROUPS - 1)

            def layer_norm(l):
                def squares(c, g):
                    act.wait_ge(s["ln_cent"], 6 * l + 2 * c + g + 1)
                    if c == 2:
                        act.wait_ge(s["ln_var"], 3 * l + 1)
                    af(lnq[:, c % 2, 4 * g:4 * g + 4], acc[:, 4 * g:4 * g + 4, c * CW:(c + 1) * CW], ACT.Square).then_inc(s["ln_sq"], 1)

                def root(c):
                    act.wait_ge(s["ln_var"], 3 * l + c + 1)
                    af(rstd[:, 0, 3 * c:3 * c + 3], aux[:, c, 500:503], ACT.Sqrt, bias=eps[:]).then_inc(s["ln_std"], 1)

                def shift(c):
                    for k in range(KD):
                        act.wait_ge(s["ln_norm"], 24 * l + 8 * c + k + 1)
                        cols = slice(c * CW, (c + 1) * CW)
                        dst = xh if l < 3 else acc
                        af(dst[:, k, cols], acc[:, k, cols], ACT.Identity, bias=lnp[:, l, 1, k:k + 1]).then_inc(s["ln_hi"], 1)
                    if l == 3:
                        act.wait_ge(s["ln_hi"], 24 * l + 8 * c + 8)
                        act.dma_start(o["yT"][:, :, c * CW:(c + 1) * CW], acc[:, :, c * CW:(c + 1) * CW]).then_inc(s["outs"], 16)

                for c in (0, 1):
                    for g in (0, 1):
                        squares(c, g)
                root(0)
                root(1)
                for g in (0, 1):
                    squares(2, g)
                shift(0)
                root(2)
                if l == 1:
                    for dst, name in ((cos, "cos"), (sin, "sin"), (perm, "perm"), (mbf, "mbf"), (subg, "subg"),
                                      (pair, "pair")):
                        act.dma_start(dst[:], a[name]).then_inc(s["attc_in"], 16)
                    act.dma_start(lamv, a["lamv"].partition_broadcast(P)).then_inc(s["attc_in"], 16)
                for c in (1, 2):
                    shift(c)

            def mlp(layer):
                j0 = (J_MLP0, J_MLP1)[layer]
                hb = layer * FFB

                def up(at, b, block_, order=UP_ORDER):
                    _, done = at.job(4)
                    for x, (j, c) in enumerate(order):
                        e = block_ * 12 + x
                        if not isinstance(e, int) or e >= 4:
                            act.wait_ge(s["h_ready"], e - 3)
                        act.wait_ge(chunk_full, done + x + 1)
                        af(rl[:, x % 4], jb[:, x % 3, 0:CW], ACT.Relu).then_inc(bank_free[x % 3], 1)
                        act.drain()
                        af(hh[b][:, j, c * CW:(c + 1) * CW], rl[:, x % 4], ACT.Square).then_inc(s["h_sq"], 1)

                up(Place(j0, 0), 0, hb, UP_ORDER_AFTER_NORM)
                with act.Fori(0, FFB // 2 - 1) as i:
                    at = Place(j0 + 4, 0, i, 24, 0)
                    up(at, 1, hb + 2 * i + 1)
                    at.job(8)
                    act.wait_ge(s["relu_done"], layer * (FFB - 1) + 2 * i + 1)
                    up(at, 0, hb + 2 * i + 2)
                    at.job(8)
                    act.wait_ge(s["relu_done"], layer * (FFB - 1) + 2 * i + 2)
                up(Place(j0 + 4 + 24 * (FFB // 2 - 1), 0), 1, hb + FFB - 1)

            act.wait_ge(s["h_out"], 16 * GROUPS)
            act.wait_ge(s["s_out"], 32 * GROUPS)
            act.wait_ge(s["cnew_out"], 16 * GROUPS)
            layer_norm(0)
            mlp(0)
            layer_norm(1)


            def twin(kk):
                for m_ in range(2):
                    act.dma_start(kk[m_][half_of(1 - m_)].bitcast(F32), kk[m_][half_of(m_)].bitcast(F32)).then_inc(s["k_twin"], 16)

            def project_head(at, n, new, fin):
                p = n - 1
                if fin:
                    act.wait_ge(s["ssc_ready"], p + 1)
                    act.dma_start(past[:], vgat[:, :, bass.ds(p * P, P)].rearrange("g t d -> t g d")).then_inc(s["pv_in"], 16)
                if new:
                    act.wait_ge(s["rope_done"], 2 * n + 1)
                    for m_ in range(2):
                        af(q2[m_][half_of(m_)], rot[half_of(m_), 0:SEQ], ACT.Copy).then_inc(s["qk_hi"], 1)
                if fin:
                    act.wait_ge(s["snm_ready"], p + 1)
                    af(srow[0:16, 0:257], srow[0:16, 0:257], ACT.Exp, scale=SCALE, bias=st[0:16, 4:5],
                       accum_out=st[0:16, 5:6]).then_inc(s["sexp_ready"], 1)
                if new:
                    _, done = at.job()
                    for c in range(NCH):
                        take(c, done, raw[:, c * CW:(c + 1) * CW], ACT.Copy)
                    act.drain().then_inc(s["raw_v"], 1)
                    act.wait_ge(s["raw_v"], n + 1)
                    act.dma_start(o["vT"][:, bass.ds(n, 1)].rearrange("p a t -> p (a t)"), raw[:]).then_inc(s["v_out"], 16)
                    act.wait_ge(s["rope_done"], 2 * n + 2)
                    for m_ in range(2):
                        af(k2h[m_][half_of(m_)], rot[half_of(m_), 0:SEQ], ACT.Copy).then_inc(s["qk_hi"], 1)
                if fin:
                    act.wait_ge(s["o_smp"], p + 1)
                    af(pp[:, 0:T], ob[:], ACT.Square).then_inc(s["osq_done"], 1)
                if new:
                    act.wait_ge(s["qk_hi"], 4 * n + 4)
                    twin(k2h)
                    act.dma_start(o["kT"][:, bass.ds(n, 1)].rearrange("p a t -> p (a t)"), rot[:]).then_inc(s["k_out"], 16)
                    act.wait_ge(s["k_low"], 2 * n + 2)
                    twin(k2l)
                if fin:
                    act.wait_ge(s["orms_full"], p + 1)
                    af(rstd[:, 0], aux[:, 0, 0:9], ACT.Sqrt, bias=eps[:]).then_inc(s["orms_sqrt"], 1)
                if new:
                    act.wait_ge(s["vt_ps"], n + 1)
                    af(vth[:], aux[:, 3:5].rearrange("p a (b c) -> p (a b) c", b=4), ACT.Copy).then_inc(s["vt_hi"], 1)
                if fin:
                    for c in range(NCH):
                        act.wait_ge(s["on_ready"], 3 * p + c + 1)
                        af(ah[:, 0, c * CW:(c + 1) * CW], ob[:, c * CW:(c + 1) * CW], ACT.Copy).then_inc(s["a_hi"], 1)
                    at.job(8)

            def attend(at, n, ahead):
                act.dma_start(past[:], kgat[:, :, bass.ds(n * P, P)].rearrange("g t d -> t g d")).then_inc(s["pk_in"], 16)

                def output(i):
                    act.wait_ge(s["pv_full"], 8 * n + i + 1)
                    af(ob[:, i * 128:(i + 1) * 128], aux[:, 4, 0:128], ACT.Copy).then_inc(s["o_half"], 1)

                for i in range(8):
                    width = (i + 1) * 128
                    if i:
                        act.wait_ge(s["wt_ps"], 8 * n + i)
                    for m_ in range(2):
                        e = 16 * n + 2 * i + m_
                        act.wait_ge(s["nmax_ready"], e + 1)
                        src = aux[:, 2 * m_:2 * m_ + 2].rearrange("p a b -> p (a b)")[:, 0:width]
                        af(pp[:, m_ * 1024:m_ * 1024 + width], src, ACT.Exp, scale=SCALE,
                           bias=st[:, m_:m_ + 1], accum_out=st[:, 2 + m_:3 + m_]).then_inc(s["p_ready"], 1)
                    if i:
                        if i >= 2:
                            output(i - 2)
                        af(wt[:, 0:i, 0], jb[:, 0:2].rearrange("p a (b c) -> p (a b) c", b=4)[:, 0:i],
                           ACT.Copy).then_inc(s["wt_hi"], 1)
                    if ahead:
                        for j, c in QK_FILL.get(i, ()):
                            if (j, c) == (0, 0):
                                act.wait_ge(s["v_out"], 16 * n + 16)
                                act.wait_ge(s["k_out"], 16 * n + 16)
                            if c == 0:
                                _, done = at.job()
                            act.wait_ge(chunk_full, done + c + 1)
                            af((raw, raw_k)[j][:, c * CW:(c + 1) * CW], jb[:, 2, 0:CW], ACT.Copy).then_inc(bank_free[c], 1)
                            if c == NCH - 1:
                                act.drain().then_inc(s["raw_full"], 1)
                output(6)
                act.wait_ge(s["wt_ps"], 8 * n + 8)
                af(wt[:, :, 0], jb[:, 0:2].rearrange("p a (b c) -> p (a b) c", b=4), ACT.Copy).then_inc(s["wt_hi"], 1)
                output(7)

            at = Place(J_ATT, 0)
            _, done = at.job(2)
            for x, (j, c) in enumerate(UP_ORDER_AFTER_NORM[0:6]):
                act.wait_ge(chunk_full, done + x + 1)
                af((raw, raw_k)[j][:, c * CW:(c + 1) * CW], jb[:, x % 3, 0:CW], ACT.Copy).then_inc(bank_free[x % 3], 1)
            act.drain().then_inc(s["raw_full"], 2)
            act.wait_ge(s["gathered"], 16 * 2 * NB * PAGES)
            act.wait_ge(s["lam_sum"], 1)
            af(lam[:, 0:2], lam[:, 0:2], ACT.Exp).then_inc(s["lam_exp"], 1)
            project_head(at, 0, True, False)
            attend(at, 0, True)
            at0 = J_ATT + ATT_HEAD_JOBS - ATT_JOBS, 0
            with act.Fori(1, HEADS_B - 1) as n:
                at = Place(*at0, n, ATT_JOBS, 0)
                project_head(at, n, True, True)
                attend(at, n, True)
            at = Place(*at0, HEADS_B - 1, ATT_JOBS, 0)
            project_head(at, HEADS_B - 1, True, True)
            attend(at, HEADS_B - 1, False)
            project_head(Place(J_MLP1 - 8, 0), HEADS_B, False, True)

            layer_norm(2)
            mlp(1)
            layer_norm(3)
            act.wait_ge(s["k_out"], 16 * HEADS_B)
            act.wait_ge(s["v_out"], 16 * HEADS_B)

        @block.vector
        def _(dve):
            tt, ts, stt = nc.vector.tensor_tensor, nc.vector.tensor_scalar, nc.vector.scalar_tensor_tensor
            drain = dve.drain

            def f(ap):
                return ap.bitcast(F32)

            nc.vector.memset(eps[:], EPS)
            nc.vector.memset(pre[:, :, 0:4], 0.0)
            for k in range(KD):
                dve.wait_ge(s["x_hi"], k + 1)
                tt(xl[:, k], acc[:, k], f(xh[:, k]), ALU.subtract).then_inc(s["x_ready"], 1)
                drain()
                ts(acc[:, k], acc[:, k], ALPHA, None, ALU.mult)
            dve.wait_ge(s["const_in"], 16 * N_CONST)
            ts(pall[:, :, 0:20], pall[:, :, 0:20], 0.5, None, ALU.mult)
            dve.wait_ge(s["dt_raw"], 1)
            stt(dtt[:], dtx[:, 0:T], -1.0, dtx[:, 0:T], ALU.mult, ALU.max).then_inc(s["dt_abs"], 1)
            ts(a32[:, 3:4], a32[:, 2:3], -1.0, None, ALU.mult)
            dve.wait_ge(s["dt_exp"], 1)
            stt(dtx[:, 0:T], dtx[:, 0:T], 0.0, dtt[:], ALU.max, ALU.add)
            drain()
            ts(dtt[:], dtx[:, 0:T], a32[:, 3:4], None, ALU.mult)
            ts(cs[:, T:T + NB], dtx[:, SEQ:T], 1.0, None, ALU.mult)
            drain()
            nc.vector.tensor_tensor_scan(cs[:, 0:T], scanm[:], dtt[:], 0.0, ALU.mult, ALU.add)
            drain().then_inc(s["dt_soft"], 1)
            dve.wait_ge(s["cs_hi"], 1)
            tt(csl[:], cs[:], f(csh[:]), ALU.subtract).then_inc(s["cs_lo"], 1)
            dve.wait_ge(s["cd_done"], 1)
            tt(tok[:, 2], aux[:, 1, 0:256].rearrange("p (c h) -> p c h", c=CHUNKS), tok[:, 0], ALU.subtract)
            drain().then_inc(s["dte_arg"], 1)
            dve.wait_ge(s["dte_exp"], 1)
            tt(tok[:, 2], tok[:, 2], tok[:, 1], ALU.mult).then_inc(s["tok_done"], 1)
            drain()

            def add_job(at, k):
                _, done = at.job()
                for c in range(NCH):
                    cols = slice(c * CW, (c + 1) * CW)
                    dve.wait_ge(chunk_full, done + c + 1)
                    tt(acc[:, k, cols], jb[:, c, 0:CW], acc[:, k, cols], ALU.add).then_inc(bank_free[c], 1)

            def accumulate(at):
                for k in range(KD):
                    add_job(at, k)
                drain()

            def accumulate_last(at):
                for k in range(KD):
                    _, done = at.job()
                    for c in range(NCH):
                        cols = slice(c * CW, (c + 1) * CW)
                        dve.wait_ge(chunk_full, done + c + 1)
                        tt(acc[:, k, cols], jb[:, c, 0:CW], acc[:, k, cols], ALU.add).then_inc(bank_free[c], 1)
                        drain()
                        if k == 1:
                            tt(ln0[:, cols], acc[:, 0, cols], acc[:, 1, cols], ALU.add)
                        elif k > 1:
                            last = tt(ln0[:, cols], ln0[:, cols], acc[:, k, cols], ALU.add)
                            if k == KD - 1:
                                last.then_inc(s["ln_sum"], 1)

            def conv(n, t):
                dve.wait_ge(s["pre_full"], 4 * n + t + 1)
                src = pre[:, t % 2]
                w = lambda k: pg[:, 4 * t + k:4 * t + k + 1]
                for k in range(3):
                    if k:
                        drain()
                    stt(ct[:, 0:SEQ], src[:, 1 + k:1 + k + SEQ], w(k), ct[:, 0:SEQ], ALU.mult, ALU.add)
                    stt(ct[:, SEQ:T], scv[:, t, k], w(k), ct[:, SEQ:T], ALU.mult, ALU.add)
                drain().then_inc(s["conv_done"], 1)

            def silu(n, t):
                dve.wait_ge(s["tanh_done"], 4 * n + t + 1)
                stt(xbc[:, t], pre[:, t % 2, 4:4 + T], 1.0, ct[:], ALU.add, ALU.mult)
                drain().then_inc(s["xbc_done"], 1)

            def gate(p):
                for t in range(2):
                    tt(y[:, t], y[:, t], zs[:, t], ALU.mult)
                    drain().then_inc(s["yg_ready"], 1)
                dve.wait_ge(s["sq_done"], 2 * p + 2)
                tt(zs[:, 0], zs[:, 0], zs[:, 1], ALU.add)
                drain().then_inc(s["sq_sum"], 1)

            def invert(p, root, inv):
                dve.wait_ge(s[root], p + 1)
                nc.vector.reciprocal(rstd[:, 1], rstd[:, 0])
                drain().then_inc(s[inv], 1)

            def norm(p):
                dve.wait_ge(s["rms_scale"], p + 1)
                for t in range(2):
                    stt(y[:, t], y[:, t], gn[:, t:t + 1], aux[:, 0:3].rearrange("p a b -> p (a b)")[:, 0:T], ALU.mult, ALU.mult)
                    drain().then_inc(s["yn_ready"], 1)

            def norm_lo(p):
                for t in range(2):
                    dve.wait_ge(s["y_hi"], 2 * p + t + 1)
                    tt(yl[:, t], y[:, t], f(yh[:, t]), ALU.subtract).then_inc(s["y_lo"], 1)

            def project_group(at, n, fin):
                nc.vector.tensor_copy(pg[:], pall[:, bass.ds(n, 1)].rearrange("p a k -> p (a k)"))
                drain().then_inc(s["pg_ready"], 1)
                if fin:
                    gate(n - 1)
                dve.wait_ge(s["scv_in"], 16 * n + 16)
                for t in range(4):
                    conv(n, t)
                    if t == 0 and fin:
                        invert(n - 1, "rms_sqrt", "rms_inv")
                    if t == 1 and fin:
                        norm(n - 1)
                    if t == 3 and fin:
                        add_job(at, 0)
                    if t == 0 and not fin:
                        dve.wait_ge(s["cs_stored"], 32)
                    silu(n, t)
                    if t == 1 and fin:
                        norm_lo(n - 1)

            hd = lambda ap: ap.unsqueeze(2).to_broadcast([P, R, HD])
            v4 = lambda ap: ap.rearrange("p (r q) -> p r q", r=R)
            two = lambda ap: ap.rearrange("p (t l) -> p t l", t=2)
            b4 = lambda ap: ap.unsqueeze(2).to_broadcast([P, 4, P])

            def sample_step(n, k):
                b0 = 4 * (k // 2)
                dve.wait_ge(s["bc_full"], 4 * n + k + 1)
                for t in range(2):
                    sv = v4(pre[:, t, 4 + b0 * P:4 + (b0 + 4) * P])
                    if k % 2 == 0:
                        tt(v4(st2[:]), v4(aux[:, 4]), b4(xdt[:, t, b0:b0 + 4]), ALU.mult)
                        drain()
                        tt(sv, sv, v4(st2[:]), ALU.add)
                    else:
                        tt(v4(st2[:]), v4(aux[:, 4]), sv, ALU.mult)
                        drain()
                        nc.vector.tensor_reduce(y[:, t, SEQ + b0:SEQ + b0 + 4], v4(st2[:]), AX.X, ALU.add)
                    drain()
                if k == 2:
                    drain().then_inc(s["s_new"], 1)
                drain().then_inc(s["bc_used"], 1)

            def scan_group(at, n, out):
                nc.vector.tensor_copy(tg[:], tok[:, :, :, bass.ds(n * R, R)])
                if out:
                    dve.wait_ge(s["h_out"], 16 * n)
                nc.vector.memset(hst[:], 0.0)
                drain().then_inc(s["h_zero"], 1)
                if out:
                    add_job(at, 1)
                for c in range(CHUNKS):
                    x = 8 * n + c
                    cols = slice(c * CHUNK, (c + 1) * CHUNK)
                    dve.wait_ge(s["ssd_in"], x + 1)
                    for r in range(R):
                        last = stt(dm[:, 0, r * 128:(r + 1) * 128], aux[:, 1, r * 128:(r + 1) * 128],
                                   tg[:, 0, c, r:r + 1], capm[:], ALU.subtract, ALU.min)
                    last.then_inc(s["d_ready"], 1)
                    dve.wait_ge(s["ssd_off"], x + 1)
                    dve.wait_ge(s["e2_ready"], x + 1)
                    tt(y[:, :, cols], two(aux[:, 3, 0:256]), two(e2[:]), ALU.mult)
                    tt(v4(hst[:]), v4(hst[:]), hd(tg[:, 3, c]), ALU.mult)
                    dve.wait_ge(s["e_ready"], x + 1)
                    tt(v4(dm[:, 1]), v4(dm[:, 0]), aux[:, 2, 384:512].unsqueeze(1).to_broadcast([P, R, P]), ALU.mult)
                    drain().then_inc(s["m_ready"], 1)
                    if out and c < 3:
                        add_job(at, 2 + 2 * c)
                        add_job(at, 3 + 2 * c)
                    dve.wait_ge(s["ssd_b"], x + 1)
                    tt(y[:, :, cols], two(aux[:, 3, 0:256]), y[:, :, cols], ALU.add)
                    tt(hst[:], aux[:, 3, 256:512], hst[:], ALU.add)
                    drain().then_inc(s["h_done"], 1)
                    for t, zc in (Z_FILL if out else Z_FILL_FIRST).get(c, ()):
                        if zc == 2:
                            dve.wait_ge(s["z_full"], 2 * n + t + 1)
                            stt(zs[:, t], ct[:], 1.0, zs[:, t], ALU.add, ALU.mult)
                            drain().then_inc(s["z_done"], 1)
                    if c == S_STEP:
                        dve.wait_ge(s["dec_ready"], n + 1)
                        dve.wait_ge(s["s_in"], 32 * n + 32)
                        tt(xdt[:], xbc[:, 0:2, SEQ:T], dts[:], ALU.mult)
                        for t in range(2):
                            sv = pre[:, t, 4:4 + SEQ].rearrange("p (b n) -> p b n", b=NB)
                            tt(sv, sv, dec[:, t].unsqueeze(2).to_broadcast([P, NB, P]), ALU.mult)
                        drain()
                    if S_STEP < c <= S_STEP + 4:
                        sample_step(n, c - S_STEP - 1)
                for t in range(2):
                    stt(y[:, t], xbc[:, t], pg[:, 20 + t:21 + t], y[:, t], ALU.mult, ALU.add)
                nc.vector.tensor_copy(gn[:], pg[:, 22:24])
                drain()

            at = Place(J_MIX + 4, 0)
            project_group(at, 0, False)
            scan_group(at, 0, False)
            with dve.Fori(1, GROUPS) as n:
                at = Place(J_MIX + 6 + 4 - MIX_JOBS, 0, n, MIX_JOBS, 0)
                project_group(at, n, True)
                scan_group(at, n, True)
            gate(GROUPS - 1)
            invert(GROUPS - 1, "rms_sqrt", "rms_inv")
            norm(GROUPS - 1)
            norm_lo(GROUPS - 1)
            dve.wait_ge(s["h_out"], 16 * GROUPS)
            dve.wait_ge(s["cnew_out"], 16 * GROUPS)
            dve.wait_ge(s["s_out"], 32 * GROUPS)
            accumulate_last(Place(J_MLP0 - 8, 0))

            def layer_norm(l):
                def centre(c):
                    dve.wait_ge(s["ln_mu"], 3 * l + c + 1)
                    for g in (0, 1):
                        v = acc[:, 4 * g:4 * g + 4, c * CW:(c + 1) * CW]
                        tt(v, v, aux[:, c, 0:CW].unsqueeze(1).to_broadcast([P, 4, CW]), ALU.subtract).then_inc(s["ln_cent"], 1)

                def add_squares(c):
                    dve.wait_ge(s["ln_sq"], 6 * l + 2 * c + 2)
                    tt(lnq[:, c % 2, 0:4], lnq[:, c % 2, 0:4], lnq[:, c % 2, 4:8], ALU.add).then_inc(s["ln_add"], 1)

                def invert_root(c):
                    dve.wait_ge(s["ln_std"], 3 * l + c + 1)
                    nc.vector.reciprocal(rstd[:, 1, 3 * c:3 * c + 3], rstd[:, 0, 3 * c:3 * c + 3]).then_inc(s["ln_inv"], 1)

                def scale(c):
                    dve.wait_ge(s["ln_scale"], 3 * l + c + 1)
                    for k in range(KD):
                        v = acc[:, k, c * CW:(c + 1) * CW]
                        stt(v, v, lnp[:, l, 0, k:k + 1], aux[:, c, 0:CW], ALU.mult, ALU.mult).then_inc(s["ln_norm"], 1)

                def low(c):
                    if l < 3:
                        for k in range(KD):
                            cols = slice(c * CW, (c + 1) * CW)
                            dve.wait_ge(s["ln_hi"], 24 * l + 8 * c + k + 1)
                            last = stt(xl[:, k, cols], acc[:, k, cols], lnp[:, l, 1, k:k + 1], f(xh[:, k, cols]), ALU.add, ALU.subtract)
                        last.then_inc(s["ln_lo"], 1)

                drain()
                centre(0)
                centre(1)
                add_squares(0)
                centre(2)
                invert_root(0)
                add_squares(1)
                drain()
                scale(0)
                invert_root(1)
                add_squares(2)
                low(0)
                invert_root(2)
                scale(1)
                low(1)
                scale(2)
                low(2)
                if l < 3:
                    drain()
                    for k in range(KD):
                        ts(acc[:, k], acc[:, k], lnp[:, l, 1, k:k + 1], ALPHA, ALU.add, ALU.mult)
                    drain()

            def mlp(layer):
                j0 = (J_MLP0, J_MLP1)[layer]
                hb = layer * FFB

                def up(at, b, block_, order=UP_ORDER):
                    at.job(4)
                    for x, (j, c) in enumerate(order):
                        cols = slice(c * CW, (c + 1) * CW)
                        dve.wait_ge(s["h_sq"], block_ * 12 + x + 1)
                        tt(rl[:, x % 4], rl[:, x % 4], rl[:, x % 4], ALU.mult)
                        drain()
                        tt(hl[b][:, j, cols], rl[:, x % 4], f(hh[b][:, j, cols]), ALU.subtract).then_inc(s["h_ready"], 1)

                def down(at):
                    accumulate(at)
                    drain().then_inc(s["relu_done"], 1)

                up(Place(j0, 0), 0, hb, UP_ORDER_AFTER_NORM)
                with dve.Fori(0, FFB // 2 - 1) as i:
                    at = Place(j0 + 4, 0, i, 24, 0)
                    up(at, 1, hb + 2 * i + 1)
                    down(at)
                    up(at, 0, hb + 2 * i + 2)
                    down(at)
                at = Place(j0 + 4 + 24 * (FFB // 2 - 1), 0)
                up(at, 1, hb + FFB - 1)
                down(at)
                accumulate_last(at)

            layer_norm(0)
            mlp(0)
            layer_norm(1)

            dve.wait_ge(s["attc_in"], 16 * N_ATTC)
            nc.vector.memset(qkn[:], 0.0)
            tt(lamv[:, 0:2], lamv[:, 0:2], lamv[:, 2:4], ALU.mult)
            drain()
            nc.vector.tensor_reduce(lam[:, 0:2], lamv[:, 0:2], AX.X, ALU.add)
            ts(subg[:], subg[:], 1.0 - LAM_INIT, None, ALU.mult)
            drain().then_inc(s["lam_sum"], 1)
            dve.wait_ge(s["lam_exp"], 1)
            tt(lam[:, 2:3], lam[:, 1:2], lam[:, 0:1], ALU.subtract)
            drain()
            ts(lam[:, 2:3], lam[:, 2:3], LAM_INIT, None, ALU.subtract)
            drain()
            stt(pair[:, 10:11], pair[:, 9:10], lam[0:16, 2:3], pair[:, 8:9], ALU.mult, ALU.add)
            drain()

            cv = lambda ap: ap.rearrange("p (c w) -> p c w", c=NCH)

            def rope(n, j):
                e = 2 * n + j + 1
                dve.wait_ge(s["raw_full"], e)
                src = (raw, raw_k)[j]
                tt(rot[:], src[:], cos[:], ALU.mult)
                drain()
                dve.wait_ge(s["perm_full"], e)
                tt(cv(src[:]), aux[:, 2:5, 0:CW], cv(sin[:]), ALU.mult)
                drain()
                tt(rot[:], rot[:], src[:], ALU.add)
                drain().then_inc(s["rope_done"], 1)
                nc.vector.tensor_copy(smp[:, j], rot[:, SEQ:T])
                drain()

            def rope_low(n, j):
                e = 2 * n + j + 1
                dve.wait_ge(s["qk_hi"], 2 * e)
                for m_ in range(2):
                    own = half_of(m_)
                    if j == 0:
                        tt(q2[m_][half_of(1 - m_)], rot[own, 0:SEQ], f(q2[m_][own]), ALU.subtract)
                    else:
                        tt(k2l[m_][own], rot[own, 0:SEQ], f(k2h[m_][own]), ALU.subtract).then_inc(s["k_low"], 1)
                drain()

            def project_head(at, n, new, fin):
                p = n - 1
                if fin:
                    for m_ in range(2):
                        rows = slice(HD * m_, HD * m_ + HD)
                        tt(qkn[rows, m_], smp[rows, 0], smp[rows, 1], ALU.mult)
                    dve.wait_ge(s["qb_full"], p + 1)
                    dve.wait_ge(s["pk_in"], 16 * p + 16)
                    for g in range(PAGES):
                        tt(pp[:].rearrange("p (b g d) -> p g b d", b=NB, g=PAGES)[:, g],
                           past[:].rearrange("p (b g) d -> p g b d", g=PAGES)[:, g],
                           aux[:, 0:2].rearrange("p a (b d) -> p (a b) d", b=4), ALU.mult)
                    drain()
                    for g in range(PAGES):
                        for m_ in range(2):
                            v = pp[:].rearrange("p (b g m d) -> p g m b d", b=NB, g=PAGES, m=2)[:, g, m_]
                            nc.vector.tensor_reduce(ssc[:, g, m_], v, AX.X, ALU.add)
                    drain().then_inc(s["ssc_ready"], 1)
                if new:
                    rope(n, 0)
                if fin:
                    dve.wait_ge(s["srow_full"], p + 1)
                    nc.vector.tensor_copy(srow[:, 0:257], aux[0:16, 0, 0:257])
                    drain()
                    nc.vector.tensor_reduce(st[0:16, 6:7], srow[:, 0:257], AX.X, ALU.max)
                    drain()
                    ts(st[0:16, 4:5], st[0:16, 6:7], -SCALE, None, ALU.mult)
                    drain().then_inc(s["snm_ready"], 1)
                if new:
                    rope_low(n, 0)
                if fin:
                    dve.wait_ge(s["sexp_ready"], p + 1)
                    nc.vector.reciprocal(st[0:16, 5:6], st[0:16, 5:6])
                    drain()
                    ts(srow[:, 0:257], srow[:, 0:257], st[0:16, 5:6], pair[:, 10:11], ALU.mult, ALU.mult)
                    drain().then_inc(s["sp_ready"], 1)
                    dve.wait_ge(s["wsm_full"], p + 1)
                    nc.vector.tensor_copy(wsm.rearrange("p k b -> p (k b)"), aux[:, 1, 0:24])
                    drain().then_inc(s["wsm_ready"], 1)
                    tt(smp[:, 2], smp[:, 2], wsm[:, 2], ALU.mult)
                    drain()
                if new:
                    rope(n, 1)
                if fin:
                    dve.wait_ge(s["so_full"], p + 1)
                    tt(ob[:, SEQ:T], aux[:, 1, 32:40], smp[:, 2], ALU.add)
                    drain().then_inc(s["o_smp"], 1)
                if new:
                    rope_low(n, 1)
                if new:
                    at.job()
                    dve.wait_ge(s["raw_v"], n + 1)
                    nc.vector.tensor_copy(smp[:, 2], raw[:, SEQ:T])
                if fin:
                    invert(p, "orms_sqrt", "orms_inv")
                    dve.wait_ge(s["orms_scale"], p + 1)
                    for c in range(NCH):
                        cols = slice(c * CW, (c + 1) * CW)
                        stt(ob[:, cols], ob[:, cols], subg[:, 0:1], aux[:, 0:3].rearrange("p a b -> p (a b)")[:, cols],
                            ALU.mult, ALU.mult).then_inc(s["on_ready"], 1)
                if fin:
                    drain()
                    for c in range(NCH):
                        cols = slice(c * CW, (c + 1) * CW)
                        dve.wait_ge(s["a_hi"], 3 * p + c + 1)
                        tt(al[:, 0, cols], ob[:, cols], f(ah[:, 0, cols]), ALU.subtract).then_inc(s["a_lo"], 1)
                if new:
                    dve.wait_ge(s["vt_hi"], n + 1)
                    tt(vtl[:], aux[:, 3:5].rearrange("p a (b c) -> p (a b) c", b=4), f(vth[:]), ALU.subtract)
                    drain().then_inc(s["vt_ready"], 1)
                if fin:
                    if new:
                        accumulate(at)
                    else:
                        accumulate_last(at)

            def attend(n):
                def output(i):
                    dve.wait_ge(s["o_half"], 8 * n + i + 1)
                    v = ob[:, i * 128:(i + 1) * 128]
                    tt(v, aux[:, 4, 128:256], v, ALU.add).then_inc(s["o_ready"], 1)

                def low(i):
                    dve.wait_ge(s["wt_hi"], 8 * n + i + 1)
                    tt(wt[:, 0:i + 1, 1], jb[:, 0:2].rearrange("p a (b c) -> p (a b) c", b=4)[:, 0:i + 1],
                       f(wt[:, 0:i + 1, 0]), ALU.subtract)
                    drain().then_inc(s["wt_ready"], 1)

                for i in range(8):
                    width = (i + 1) * 128
                    for m_ in range(2):
                        e = 16 * n + 2 * i + m_
                        dve.wait_ge(s["s_full"], e + 1)
                        src = aux[:, 2 * m_:2 * m_ + 2].rearrange("p a b -> p (a b)")[:, 0:width]
                        nc.vector.tensor_reduce(st[:, 6 + m_:7 + m_], src, AX.X, ALU.max)
                        drain()
                        ts(st[:, m_:m_ + 1], st[:, 6 + m_:7 + m_], -SCALE, None, ALU.mult).then_inc(s["nmax_ready"], 1)
                    if i == 7:
                        output(5)
                        low(6)
                    dve.wait_ge(s["p_ready"], 16 * n + 2 * i + 2)
                    nc.vector.reciprocal(st[:, 2:4], st[:, 2:4])
                    drain()
                    ts(pp[:, 1024:1024 + width], pp[:, 1024:1024 + width], st[:, 3:4], lam[:, 2:3], ALU.mult, ALU.mult)
                    drain()
                    stt(pp[:, 0:width], pp[:, 0:width], st[:, 2:3], pp[:, 1024:1024 + width], ALU.mult, ALU.add)
                    drain().then_inc(s["w_ready"], 1)
                    if 2 <= i < 7:
                        output(i - 2)
                    if 1 <= i < 7:
                        low(i - 1)
                output(6)
                low(7)
                output(7)
                drain()

            project_head(Place(J_ATT + 2, 0), 0, True, False)
            attend(0)
            with dve.Fori(1, HEADS_B) as n:
                project_head(Place(J_ATT + ATT_HEAD_JOBS - ATT_JOBS, 0, n, ATT_JOBS, 0), n, True, True)
                attend(n)
            project_head(Place(J_MLP1 - 8, 0), HEADS_B, False, True)

            layer_norm(2)
            mlp(1)
            layer_norm(3)


_OUT_SHAPES = {
    "yT": (P, KD, T), "kT": (P, HEADS_B, T), "vT": (P, HEADS_B, T), "conv_new": (P, GROUPS, 4, 11),
    "conv_old": (NB, CONV_W - 2, CONV_DIM), "ssm_p": (P, GROUPS, 256), "ssm_s": (P, 2 * GROUPS, NB, P),
}


def _tiles(w):
    k, m = w.shape
    return w.reshape(k // P, P, m // P, P).transpose(2, 1, 0, 3)


def _stream(w_in, w_out, w_up, w_down, w_kv, w_q, w_o):
    units = np.zeros((UNITS, P, 8, P), np.float32)
    at = [0]

    def put(block):
        units[at[0]:at[0] + len(block)] = block
        at[0] += len(block)

    def rows(w, k0, kt):
        t = _tiles(w[k0 * P:(k0 + kt) * P])
        m = t.shape[0]
        put(t.reshape(m * kt // 8, 8 // kt, P, kt, P).transpose(0, 2, 1, 3, 4).reshape(-1, P, 8, P))

    dt = np.zeros((D, P), np.float32)
    dt[:, :HEADS_A] = w_in[:, D_INNER + CONV_DIM:]
    put(_tiles(dt))
    t_in = _tiles(w_in[:, :D_INNER + CONV_DIM])
    z, x, b, c = t_in[:16], t_in[16:32], t_in[32:40], t_in[40:48]
    for g in range(GROUPS):
        put(np.stack([x[2 * g], x[2 * g + 1], b[g], c[g]]))
        if g:
            rows(w_out, 2 * (g - 1), 2)
        put(z[2 * g:2 * g + 2])
    rows(w_out, 2 * (GROUPS - 1), 2)

    def mlp(layer):
        up = _tiles(w_up[layer])
        put(up[0:4])
        for b_ in range(1, FFB):
            put(up[4 * b_:4 * b_ + 4])
            rows(w_down[layer], 4 * (b_ - 1), 4)
        rows(w_down[layer], 4 * (FFB - 1), 4)

    mlp(0)
    q, kv = _tiles(w_q), _tiles(w_kv)
    put(np.stack([q[0], kv[0]]))
    for h in range(HEADS_B):
        put(kv[HEADS_B + h:HEADS_B + h + 1])
        if h:
            rows(w_o, h - 1, 1)
        if h < HEADS_B - 1:
            put(np.stack([q[h + 1], kv[h + 1]]))
    rows(w_o, HEADS_B - 1, 1)
    mlp(1)
    assert at[0] == UNITS
    return units


def _layout(v):
    f = lambda n: np.asarray(v[n], np.float32) if np.asarray(v[n]).dtype == np.float32 else np.asarray(v[n])
    d = {}
    d["wstream"] = _stream(f("w_in_a")[0], f("w_out_a")[0], f("w_up"), f("w_down"), f("w_kv"), f("w_q_b")[0], f("w_o_b")[0])
    x = np.concatenate([f("x_prompt")[0], f("x_sample")[:, 0]])
    d["xT"] = x.T.reshape(KD, P, T).transpose(1, 0, 2)

    def by_tile(w):
        t = w.reshape(*w.shape[:-1], CONV_DIM // P, P)
        order = [[2 * g, 2 * g + 1, 16 + g, 24 + g] for g in range(GROUPS)]
        t = t[..., np.array(order), :]
        return np.moveaxis(t, (-1, -3, -2), (0, 1, 2))

    par = np.zeros((P, GROUPS, 24), np.float32)
    par[:, :, 0:16] = by_tile(f("conv_w_a")[0]).reshape(P, GROUPS, 16)
    par[:, :, 16:20] = by_tile(f("conv_b_a")[0])
    par[:, :, 20:22] = np.repeat(f("d_skip_a")[0].reshape(GROUPS, 2, 2), 64, axis=2).transpose(2, 0, 1)
    par[:, :, 22:24] = f("norm_a")[0].reshape(GROUPS, 2, P).transpose(2, 0, 1)
    d["par"] = par
    d["sconv"] = by_tile(f("state_conv")[0]).transpose(0, 1, 2, 4, 3)
    d["conv_keep"] = f("state_conv")[0][:, 1:]
    d["state"] = f("state_ssm")[0].reshape(NB, 2 * GROUPS, P, P).transpose(2, 1, 0, 3)
    a32 = np.zeros((HEADS_A, 4), np.float32)
    a32[:, 0] = f("dt_bias_a")[0]
    a32[:, 1] = f("a_log_a")[0]
    d["a32"] = a32
    lnp = np.stack([f("ln_g").reshape(4, D), f("ln_b").reshape(4, D)], 1)
    d["lnp"] = lnp.reshape(4, 2, KD, P).transpose(3, 0, 1, 2)
    d["lamv"] = np.stack([f("lambda_q1_b")[0], f("lambda_q2_b")[0], f("lambda_k1_b")[0], f("lambda_k2_b")[0]])
    d["subg"] = f("subln_b")[0].reshape(P, 1)
    d["cache_k"] = f("cache_k").reshape(PHYS, P, D)
    d["cache_v"] = f("cache_v").reshape(PHYS, P, D)
    d["ptab"] = f("page_table").reshape(1, NB * PAGES).astype(np.int32)

    eye = np.eye(P, dtype=np.float32)
    d["ident"] = eye
    ones = np.full((P, P + 2), 1 / D, np.float32)
    ones[:, P], ones[:, P + 1] = 1 / 256, 1 / P
    d["ones"] = ones
    d["row127"] = np.zeros((P, P), np.float32)
    d["row127"][P - 1] = 1
    i = np.arange(P)
    d["capm"] = np.where(i[None, :] >= i[:, None], 0, -1e30).astype(np.float32)
    scanm = np.ones((HEADS_A, T), np.float32)
    scanm[:, 0:SEQ:CHUNK] = 0
    scanm[:, SEQ:] = 0
    d["scanm"] = scanm
    sel = np.zeros((8, 6, P), np.float32)
    for r in range(R):
        sel[[r, R + r], r] = 1
        sel[[r, R + r], 4 + r // 2, 64 * (r % 2):64 * (r % 2) + 64] = 1
    d["sel"] = sel.reshape(8, 768)
    half = HD // 2
    inv = (np.float32(10000.0) ** (-np.arange(half, dtype=np.float32) / half)).astype(np.float32)
    pos = np.concatenate([np.arange(SEQ), np.full(NB, PAST)]).astype(np.float32)
    ang = inv[:, None] * pos[None, :]
    d["cos"] = np.tile(np.cos(ang).astype(np.float32), (4, 1))
    d["sin"] = np.tile(np.sin(ang).astype(np.float32), (4, 1))
    perm = np.zeros((P, P), np.float32)
    for m_ in range(P):
        if m_ % HD < half:
            perm[m_ + half, m_] = -1
        else:
            perm[m_ - half, m_] = 1
    d["perm"] = perm
    mbf = np.zeros((P, 2, P), mybir.dt.np(BF16))
    mbf[:, 0] = eye
    mbf[:, 1] = np.where(i[None, :] <= i[:, None], 0, -1e30)
    d["mbf"] = mbf
    pair = np.zeros((16, 12), np.float32)
    for r in range(16):
        pair[r, r % 8] = 1
        pair[r, 8 + r // 8] = 1
    d["pair"] = pair
    return {k: np.ascontiguousarray(w) for k, w in d.items()}


def kernel(**inputs):
    import concourse.bacc as _bacc
    from concourse.bass_utils import run_bass_kernel_spmd as _run

    nc = _bacc.Bacc("TRN2", target_bir_lowering=False, num_devices=1)
    arrays = {f"in_{k}": w for k, w in _layout(inputs).items()}
    a = {k[3:]: nc.dram_tensor(k, w.shape, mybir.dt.from_np(w.dtype), kind="ExternalInput").ap() for k, w in arrays.items()}
    o = {k: nc.dram_tensor(f"out_{k}", shape, F32, kind="ExternalOutput").ap() for k, shape in _OUT_SHAPES.items()}
    program(nc, a, o)
    r = _run(nc, [arrays], core_ids=[0]).results[0]
    g = {k: np.asarray(r[f"out_{k}"]) for k in _OUT_SHAPES}

    def tokens(t):
        return t.transpose(2, 1, 0).reshape(T, D)

    yt, kt, vt = tokens(g["yT"]), tokens(g["kT"]), tokens(g["vT"])
    new = np.zeros((CONV_DIM // P, P, 11), np.float32)
    for gr in range(GROUPS):
        for j, tile in enumerate((2 * gr, 2 * gr + 1, 16 + gr, 24 + gr)):
            new[tile] = g["conv_new"][:, gr, j]
    new = new.reshape(CONV_DIM, 11)
    conv_p = new[:, 0:3].T.reshape(1, 1, 3, CONV_DIM)
    conv_s = np.concatenate([g["conv_old"], new[:, 3:].T[:, None]], 1)[None]
    ssm_p = g["ssm_p"].reshape(P, HEADS_A, HD).transpose(1, 2, 0)[None, None]
    ssm_s = g["ssm_s"].reshape(2, HD, 16, NB, P).transpose(3, 2, 0, 1, 4).reshape(1, NB, HEADS_A, HD, P)
    c = np.ascontiguousarray
    return (c(yt[:SEQ][None]), c(yt[SEQ:][:, None]), c(conv_p), c(ssm_p),
            c(kt[:SEQ].reshape(1, SEQ, HEADS_B, 2, HD)), c(vt[:SEQ].reshape(1, SEQ, HEADS_B, 2 * HD)),
            c(conv_s), c(ssm_s),
            c(kt[SEQ:].reshape(NB, 1, HEADS_B, 2, HD)), c(vt[SEQ:].reshape(NB, 1, HEADS_B, 2 * HD)))
```
